# Optimizing a Trainium2 kernel written in Bass

```python
import math
import jax, jax.numpy as jnp
from jax import lax
import numpy as np

D_MODEL = 1024
BATCH = 1
SEQ = 256
DEPTH = 1

HEAD_DIM = 64
SWA_HEADS = 8
SWA_KV_HEADS = 2
SWA_GROUP = SWA_HEADS // SWA_KV_HEADS
WINDOW = 128
DIFF_HEADS = 4
DIFF_VDIM = 2 * HEAD_DIM
BLOCK = 128
D_FF = 2816
CONV_WIDTH = 3
RMS_EPS = 1e-6
NEG_INF = -1e30

SWA_Q = SWA_HEADS * HEAD_DIM
SWA_KV = SWA_KV_HEADS * HEAD_DIM
DIFF_QK = DIFF_HEADS * 2 * HEAD_DIM
DIFF_V = DIFF_HEADS * DIFF_VDIM
IN_COLS = SWA_Q + 2 * SWA_KV + 2 * DIFF_QK + DIFF_V + 2 * D_MODEL


def _rmsnorm(x, g):
    xf = x.astype(jnp.float32)
    y = xf * lax.rsqrt(jnp.mean(xf * xf, axis=-1, keepdims=True) + RMS_EPS)
    return (y * g.astype(jnp.float32)).astype(x.dtype)

def _alibi_slopes(n):
    return jnp.array([2.0 ** (-8.0 * (i + 1) / n) for i in range(n)], dtype=jnp.float32)

def _sliding_window_attention(q, k, v, sinks, slopes):
    b, s, _, d = q.shape
    nb = s // BLOCK
    qb = q.reshape(b, nb, BLOCK, SWA_KV_HEADS, SWA_GROUP, d)

    def with_prev(t):
        tb = t.reshape(b, nb, BLOCK, SWA_KV_HEADS, d)
        prev = jnp.concatenate([jnp.zeros_like(tb[:, :1]), tb[:, :-1]], axis=1)
        return jnp.concatenate([prev, tb], axis=2)

    kb, vb = with_prev(k), with_prev(v)
    scores = jnp.einsum('bnqkgd,bnskd->bnkgqs', qb, kb).astype(jnp.float32) * (d ** -0.5)
    qi = jnp.arange(BLOCK)[:, None]
    kj = jnp.arange(2 * BLOCK)[None, :]
    delta = qi + BLOCK - kj
    key_pos = jnp.arange(nb)[:, None, None] * BLOCK - BLOCK + kj[None]
    valid = (delta >= 0) & (delta < WINDOW) & (key_pos >= 0)
    bias = -slopes[:, :, None, None] * delta.astype(jnp.float32)
    scores = jnp.where(valid[None, :, None, None], scores + bias, NEG_INF)
    sink = jnp.broadcast_to(sinks.astype(jnp.float32).reshape(SWA_KV_HEADS, SWA_GROUP, 1, 1),
                            scores.shape[:-1] + (1,))
    probs = jax.nn.softmax(jnp.concatenate([scores, sink], axis=-1), axis=-1)[..., :-1]
    out = jnp.einsum('bnkgqs,bnskd->bnqkgd', probs.astype(v.dtype), vb)
    return out.reshape(b, s, SWA_HEADS * d)

def _diff_attention(q, k, v, lam, lam_init, subln_g, slopes):
    b, s = q.shape[:2]
    nb = s // BLOCK
    qb = jnp.moveaxis(q.reshape(b, nb, BLOCK, DIFF_HEADS, 2, HEAD_DIM), 1, 0)
    key_pos = jnp.arange(s)
    scale = HEAD_DIM ** -0.5

    def block_fn(args):
        qblk, n = args
        scores = jnp.einsum('bqhmd,bshmd->bhmqs', qblk, k).astype(jnp.float32) * scale
        q_pos = n * BLOCK + jnp.arange(BLOCK)
        delta = q_pos[:, None] - key_pos[None, :]
        scores = scores - slopes[:, None, None, None] * delta.astype(jnp.float32)
        scores = jnp.where(delta >= 0, scores, NEG_INF)
        p = jax.nn.softmax(scores, axis=-1)
        a = p[:, :, 0] - lam * p[:, :, 1]
        return jnp.einsum('bhqs,bshe->bqhe', a.astype(v.dtype), v)

    out = lax.map(block_fn, (qb, jnp.arange(nb)))
    out = jnp.moveaxis(out, 0, 1).reshape(b, s, DIFF_HEADS, DIFF_VDIM)
    out = _rmsnorm(out, subln_g) * (1.0 - lam_init)
    return out.reshape(b, s, DIFF_V)

def _conv_ffn(h, w_up, conv_w, conv_b, w_down):
    u = h @ w_up
    a, g = jnp.split(u, 2, axis=-1)
    s = a.shape[1]
    ap = jnp.pad(a, ((0, 0), (CONV_WIDTH - 1, 0), (0, 0)))
    a = ap[:, 0:s] * conv_w[0] + ap[:, 1:s + 1] * conv_w[1] + ap[:, 2:s + 2] * conv_w[2] + conv_b
    return (jax.nn.gelu(a, approximate=False) * g) @ w_down

def first_inputs(seed: int = 0) -> dict:
    key = jax.random.key(seed)
    ks = jax.random.split(key, 20)
    nrm = lambda k, shape, s: jax.random.normal(k, shape, jnp.float32) * s
    D = D_MODEL
    return {
        "x": nrm(ks[0], (BATCH, SEQ, D), 1.0),
        "c": nrm(ks[1], (BATCH, D), 1.0),
        "w_ada": nrm(ks[2], (DEPTH, D, 6 * D), 0.5 * D ** -0.5),
        "b_ada": nrm(ks[3], (DEPTH, 6 * D), 0.02),
        "norm1_g": 1.0 + nrm(ks[4], (DEPTH, D), 0.02),
        "w_in": nrm(ks[5], (DEPTH, D, IN_COLS), D ** -0.5),
        "swa_sinks": nrm(ks[6], (DEPTH, SWA_HEADS), 1.0),
        "diff_lambda": nrm(ks[7], (DEPTH, 4, HEAD_DIM), 0.1),
        "diff_subln_g": 1.0 + nrm(ks[8], (DEPTH, DIFF_VDIM), 0.02),
        "w_branch_swa": nrm(ks[9], (DEPTH, SWA_Q, D), SWA_Q ** -0.5),
        "w_branch_diff": nrm(ks[10], (DEPTH, DIFF_V, D), DIFF_V ** -0.5),
        "w_out": nrm(ks[11], (DEPTH, D, D), D ** -0.5),
        "norm2_g": 1.0 + nrm(ks[12], (DEPTH, D), 0.02),
        "w_up": nrm(ks[13], (DEPTH, D, 2 * D_FF), D ** -0.5),
        "conv_w": nrm(ks[14], (DEPTH, CONV_WIDTH, D_FF), CONV_WIDTH ** -0.5),
        "conv_b": nrm(ks[15], (DEPTH, D_FF), 0.02),
        "w_down": nrm(ks[16], (DEPTH, D_FF, D), D_FF ** -0.5),
        "final_g": 1.0 + nrm(ks[17], (D,), 0.02),
    }

def first_block(x, c, w_ada, b_ada, norm1_g, w_in, swa_sinks, diff_lambda, diff_subln_g,
              w_branch_swa, w_branch_diff, w_out, norm2_g, w_up, conv_w, conv_b, w_down, final_g):
    b, s, _ = x.shape
    sizes = [SWA_Q, SWA_KV, SWA_KV, DIFF_QK, DIFF_QK, DIFF_V, D_MODEL, D_MODEL]
    points = [int(p) for p in np.cumsum(sizes)[:-1]]
    slopes_swa = _alibi_slopes(SWA_HEADS).reshape(SWA_KV_HEADS, SWA_GROUP)
    slopes_diff = _alibi_slopes(DIFF_HEADS)
    cs = jax.nn.silu(c)
    for l in range(DEPTH):
        mod = cs @ w_ada[l] + b_ada[l]
        shift1, scale1, gate1, shift2, scale2, gate2 = [m[:, None, :] for m in jnp.split(mod, 6, axis=-1)]

        h = _rmsnorm(x, norm1_g[l]) * (1.0 + scale1) + shift1
        proj = h @ w_in[l]
        qa, ka, va, qd, kd, vd, ga, gd = jnp.split(proj, points, axis=-1)
        out_a = _sliding_window_attention(
            qa.reshape(b, s, SWA_HEADS, HEAD_DIM),
            ka.reshape(b, s, SWA_KV_HEADS, HEAD_DIM),
            va.reshape(b, s, SWA_KV_HEADS, HEAD_DIM),
            swa_sinks[l], slopes_swa)
        lam_init = 0.8 - 0.6 * math.exp(-0.3 * l)
        lp = diff_lambda[l].astype(jnp.float32)
        lam = jnp.exp(jnp.sum(lp[0] * lp[1])) - jnp.exp(jnp.sum(lp[2] * lp[3])) + lam_init
        out_d = _diff_attention(
            qd.reshape(b, s, DIFF_HEADS, 2, HEAD_DIM),
            kd.reshape(b, s, DIFF_HEADS, 2, HEAD_DIM),
            vd.reshape(b, s, DIFF_HEADS, DIFF_VDIM),
            lam, lam_init, diff_subln_g[l], slopes_diff)
        merged = (jax.nn.sigmoid(ga) * (out_a @ w_branch_swa[l])
                  + jax.nn.sigmoid(gd) * (out_d @ w_branch_diff[l]))
        x = x + gate1 * (merged @ w_out[l])

        h2 = _rmsnorm(x, norm2_g[l]) * (1.0 + scale2) + shift2
        x = x + gate2 * _conv_ffn(h2, w_up[l], conv_w[l], conv_b[l], w_down[l])
    return _rmsnorm(x, final_g)


MEM_LEN = 256
CONV_CH = 512
CONV_GROUPS = 8
MOBA_HEADS = 8
MOBA_HEAD_DIM = 64
MOBA_WIDTH = MOBA_HEADS * MOBA_HEAD_DIM
MOBA_BLOCK = 256
MOBA_TOPK = 3
MOBA_QCHUNK = 16
MEM_HEADS = 4
MEM_HEAD_DIM = 128
MEM_WIDTH = MEM_HEADS * MEM_HEAD_DIM
N_BRANCH = 3
IN_SPLITS = [CONV_CH, CONV_CH, CONV_CH, MOBA_WIDTH, MOBA_WIDTH, MOBA_WIDTH, MEM_WIDTH,
             D_MODEL, D_MODEL, D_MODEL]
IN_COLS_2 = sum(IN_SPLITS)
FFN_CONV_WIDTH = 3
EPS = 1e-6


def rmsnorm(x, g):
    xf = x.astype(jnp.float32)
    y = xf * lax.rsqrt(jnp.mean(xf * xf, axis=-1, keepdims=True) + EPS)
    return y.astype(x.dtype) * g

def causal_dwconv3(u, w, b):
    s = u.shape[1]
    up = jnp.pad(u, ((0, 0), (2, 0), (0, 0)))
    return up[:, :s] * w[0] + up[:, 1:s + 1] * w[1] + up[:, 2:] * w[2] + b

def moba_attention(q, k, v):
    bsz, s, h, dh = q.shape
    L = MOBA_BLOCK
    nb = -(-s // L)
    sp = nb * L
    pad = ((0, 0), (0, sp - s), (0, 0), (0, 0))
    q, k, v = jnp.pad(q, pad), jnp.pad(k, pad), jnp.pad(v, pad)
    qh = q.transpose(0, 2, 1, 3)
    kb = k.reshape(bsz, nb, L, h, dh).transpose(0, 3, 1, 2, 4)
    vb = v.reshape(bsz, nb, L, h, dh).transpose(0, 3, 1, 2, 4)
    kbar = jnp.mean(kb, axis=3)
    n_sel = min(MOBA_TOPK, nb - 1)
    scale = dh ** -0.5
    gather = jax.vmap(jax.vmap(lambda blocks, idx: blocks[idx]))

    def one_chunk(ci):
        start = ci * MOBA_QCHUNK
        own = start // L
        qc = lax.dynamic_slice_in_dim(qh, start, MOBA_QCHUNK, axis=2)
        qpos = start + jnp.arange(MOBA_QCHUNK)
        kpos = own * L + jnp.arange(L)
        k_own = lax.dynamic_index_in_dim(kb, own, axis=2, keepdims=False)
        v_own = lax.dynamic_index_in_dim(vb, own, axis=2, keepdims=False)
        s_own = jnp.einsum('bhqd,bhkd->bhqk', qc, k_own).astype(jnp.float32) * scale
        s_own = jnp.where(kpos[None, :] <= qpos[:, None], s_own, -jnp.inf)
        if n_sel == 0:
            p = jax.nn.softmax(s_own, axis=-1).astype(v.dtype)
            return jnp.einsum('bhqk,bhkd->bhqd', p, v_own)
        gate = jnp.einsum('bhqd,bhnd->bhqn', qc, kbar)
        gate = jnp.where(jnp.arange(nb) < own, gate, -jnp.inf)
        _, idx = lax.top_k(gate, n_sel)
        valid = idx < own
        k_sel = gather(kb, idx)
        v_sel = gather(vb, idx)
        s_sel = jnp.einsum('bhqd,bhqnkd->bhqnk', qc, k_sel).astype(jnp.float32) * scale
        s_sel = jnp.where(valid[..., None], s_sel, -jnp.inf)
        s_sel = s_sel.reshape(bsz, h, MOBA_QCHUNK, n_sel * L)
        p = jax.nn.softmax(jnp.concatenate([s_sel, s_own], axis=-1), axis=-1).astype(v.dtype)
        p_sel = p[..., :n_sel * L].reshape(bsz, h, MOBA_QCHUNK, n_sel, L)
        p_own = p[..., n_sel * L:]
        return (jnp.einsum('bhqnk,bhqnkd->bhqd', p_sel, v_sel)
                + jnp.einsum('bhqk,bhkd->bhqd', p_own, v_own))

    out = lax.map(one_chunk, jnp.arange(sp // MOBA_QCHUNK))
    out = out.transpose(1, 0, 3, 2, 4).reshape(bsz, sp, h * dh)
    return out[:, :s]

def memory_cross_attention(q_m, mem_n, w_mem_kv, memq_gain, memk_gain):
    bsz, s, _ = q_m.shape
    m = mem_n.shape[1]
    q = rmsnorm(q_m.reshape(bsz, s, MEM_HEADS, MEM_HEAD_DIM), memq_gain)
    k_m, v_m = jnp.split(mem_n @ w_mem_kv, 2, axis=-1)
    k = rmsnorm(k_m.reshape(bsz, m, MEM_HEADS, MEM_HEAD_DIM), memk_gain)
    v = v_m.reshape(bsz, m, MEM_HEADS, MEM_HEAD_DIM)
    sc = jnp.einsum('bshd,bmhd->bhsm', q, k).astype(jnp.float32) * (MEM_HEAD_DIM ** -0.5)
    p = jax.nn.softmax(sc, axis=-1).astype(v.dtype)
    o = jnp.einsum('bhsm,bmhd->bshd', p, v)
    return o.reshape(bsz, s, MEM_WIDTH)

def second_inputs(seed: int = 0) -> dict:
    key = jax.random.key(seed)
    ks = jax.random.split(key, 24)
    nrm = lambda k, shape, scale: jax.random.normal(k, shape, jnp.float32) * scale
    D = D_MODEL
    return {
        "x": nrm(ks[0], (BATCH, SEQ, D), 1.0),
        "mem": nrm(ks[1], (BATCH, MEM_LEN, D), 1.0),
        "g_mix": 1.0 + nrm(ks[2], (D,), 0.02),
        "w_in": nrm(ks[3], (D, IN_COLS_2), D ** -0.5),
        "b_gate": nrm(ks[4], (N_BRANCH * D,), 0.02),
        "conv_w": nrm(ks[5], (CONV_WIDTH, CONV_CH), CONV_WIDTH ** -0.5),
        "conv_b": nrm(ks[6], (CONV_CH,), 0.02),
        "moba_q_gain": 1.0 + nrm(ks[7], (MOBA_HEAD_DIM,), 0.02),
        "moba_k_gain": 1.0 + nrm(ks[8], (MOBA_HEAD_DIM,), 0.02),
        "g_mem": 1.0 + nrm(ks[9], (D,), 0.02),
        "w_mem_kv": nrm(ks[10], (D, 2 * MEM_WIDTH), D ** -0.5),
        "memq_gain": 1.0 + nrm(ks[11], (MEM_HEAD_DIM,), 0.02),
        "memk_gain": 1.0 + nrm(ks[12], (MEM_HEAD_DIM,), 0.02),
        "w_br_conv": nrm(ks[13], (CONV_CH, D), CONV_CH ** -0.5),
        "w_br_moba": nrm(ks[14], (MOBA_WIDTH, D), MOBA_WIDTH ** -0.5),
        "w_br_mem": nrm(ks[15], (MEM_WIDTH, D), MEM_WIDTH ** -0.5),
        "w_o": nrm(ks[16], (D, D), D ** -0.5),
        "g_ffn": 1.0 + nrm(ks[17], (D,), 0.02),
        "w_up": nrm(ks[18], (D, 2 * D_FF), D ** -0.5),
        "ffn_conv_w": nrm(ks[19], (FFN_CONV_WIDTH, D_FF), FFN_CONV_WIDTH ** -0.5),
        "ffn_conv_b": nrm(ks[20], (D_FF,), 0.02),
        "w_down": nrm(ks[21], (D_FF, D), D_FF ** -0.5),
    }

def second_block(x, mem, g_mix, w_in, b_gate, conv_w, conv_b, moba_q_gain, moba_k_gain,
              g_mem, w_mem_kv, memq_gain, memk_gain, w_br_conv, w_br_moba, w_br_mem,
              w_o, g_ffn, w_up, ffn_conv_w, ffn_conv_b, w_down):
    bsz, s, D = x.shape
    mem_n = rmsnorm(mem, g_mem)
    for _ in range(DEPTH):
        h = rmsnorm(x, g_mix)
        proj = h @ w_in
        cuts = list(np.cumsum(IN_SPLITS)[:-1])
        (c_b, c_c, c_x, q, k, v, q_m, g1, g2, g3) = jnp.split(proj, cuts, axis=-1)
        bg1, bg2, bg3 = jnp.split(b_gate, N_BRANCH)

        y_conv = c_b * causal_dwconv3(c_c * c_x, conv_w, conv_b)

        qh = rmsnorm(q.reshape(bsz, s, MOBA_HEADS, MOBA_HEAD_DIM), moba_q_gain)
        kh = rmsnorm(k.reshape(bsz, s, MOBA_HEADS, MOBA_HEAD_DIM), moba_k_gain)
        vh = v.reshape(bsz, s, MOBA_HEADS, MOBA_HEAD_DIM)
        y_moba = moba_attention(qh, kh, vh)

        y_mem = memory_cross_attention(q_m, mem_n, w_mem_kv, memq_gain, memk_gain)

        merged = (jax.nn.sigmoid(g1 + bg1) * (y_conv @ w_br_conv)
                  + jax.nn.sigmoid(g2 + bg2) * (y_moba @ w_br_moba)
                  + jax.nn.sigmoid(g3 + bg3) * (y_mem @ w_br_mem))
        x = x + merged @ w_o

        h2 = rmsnorm(x, g_ffn)
        a, b = jnp.split(h2 @ w_up, 2, axis=-1)
        a = causal_dwconv3(a, ffn_conv_w, ffn_conv_b)
        x = x + (jax.nn.silu(a) * b) @ w_down
    return x


def setup_inputs(seed=0):
    out = dict(first_inputs(seed))
    for name, value in second_inputs(seed + 1).items():
        if name != "x":
            out[name + "_2"] = value
    return out


def reference(
    x, c, w_ada, b_ada, norm1_g, w_in, swa_sinks, diff_lambda, diff_subln_g, w_branch_swa,
    w_branch_diff, w_out, norm2_g, w_up, conv_w, conv_b, w_down, final_g, mem_2, g_mix_2,
    w_in_2, b_gate_2, conv_w_2, conv_b_2, moba_q_gain_2, moba_k_gain_2, g_mem_2, w_mem_kv_2,
    memq_gain_2, memk_gain_2, w_br_conv_2, w_br_moba_2, w_br_mem_2, w_o_2, g_ffn_2, w_up_2,
    ffn_conv_w_2, ffn_conv_b_2, w_down_2,
):
    x = first_block(
        x, c, w_ada, b_ada, norm1_g, w_in, swa_sinks, diff_lambda, diff_subln_g, w_branch_swa,
        w_branch_diff, w_out, norm2_g, w_up, conv_w, conv_b, w_down, final_g,
    )
    return second_block(
        x, mem_2, g_mix_2, w_in_2, b_gate_2, conv_w_2, conv_b_2, moba_q_gain_2, moba_k_gain_2,
        g_mem_2, w_mem_kv_2, memq_gain_2, memk_gain_2, w_br_conv_2, w_br_moba_2, w_br_mem_2,
        w_o_2, g_ffn_2, w_up_2, ffn_conv_w_2, ffn_conv_b_2, w_down_2,
    )


_drawn_inputs = setup_inputs


def setup_inputs(seed=0):
    import zlib

    import numpy as np

    out = dict(_drawn_inputs(seed))
    spreads = {}
    factors = {'norm1_g': 8.0,
     'swa_sinks': 10.855,
     'diff_lambda': 2.778,
     'diff_subln_g': 8.0,
     'norm2_g': 6.901,
     'conv_b': 8.0,
     'g_mix_2': 3.044,
     'b_gate_2': 8.0,
     'conv_b_2': 24.376,
     'moba_q_gain_2': 32.643,
     'moba_k_gain_2': 31.266,
     'g_mem_2': 8.0,
     'memq_gain_2': 8.0,
     'memk_gain_2': 8.0,
     'g_ffn_2': 15.069,
     'ffn_conv_b_2': 21.249}
    for name, (base, spread) in spreads.items():
        noise = np.random.default_rng([zlib.crc32(name.encode()), seed]).standard_normal(out[name].shape)
        drawn = base * np.exp(spread * noise) if base else spread * noise
        out[name] = __import__('jax').numpy.asarray(drawn.astype(out[name].dtype))
    for name, factor in factors.items():
        out[name] = (out[name] * factor).astype(out[name].dtype)
    return out
```

```python
from contextlib import ExitStack

import numpy as np

import concourse.bass as bass
from concourse import mybir

ALU = mybir.AluOpType
ACT = mybir.ActivationFunctionType
F32 = mybir.dt.float32
F32R = mybir.dt.float32r
I32 = mybir.dt.int32
AX_X = mybir.AxisListType.X

P = 128
D = 1024
KT = D // P
S = 256
NT = S // P
UNIT = 2048
RAW, SPLIT = 6, 3
F = 2816
FJ = F // 256
HD = 64
EPS = 1e-6
BIG = 3e32
LAM_INIT = 0.8 - 0.6

VA = {}
VA_ROWS = [("b_ada", 48), ("norm1_g", 8), ("norm2_g", 8), ("final_g", 8), ("g_mix_2", 8), ("g_mem_2", 8),
           ("g_ffn_2", 8), ("c", 8), ("diff_subln_g", 1), ("memq_gain_2", 1), ("memk_gain_2", 1)]
VB_ROWS = [("b_gate_2", 24), ("conv_w_2", 12), ("conv_b_2", 4), ("conv_w", 66), ("conv_b", 22)]
VC_ROWS = [("ffn_conv_w_2", 66), ("ffn_conv_b_2", 22)]


def columns(rows):
    at, out = 0, {}
    for name, n in rows:
        out[name] = (at, n)
        at += n
    return out, at


VA, NA = columns(VA_ROWS)
MOBA_Q_COL, MOBA_K_COL = NA, NA + 1
NA += 2
VB, NB = columns(VB_ROWS)
VC, NC_ = columns(VC_ROWS)


def build_plan():
    plan = []
    w = 0

    def weights(n):
        nonlocal w
        for _ in range(n):
            plan.append(("w", w))
            w += 1

    weights(4)
    plan.extend(("ada", a) for a in range(8))
    for s in range(17):
        weights(1)
        if s >= 1:
            plan.append(("ada", 7 + s))
    weights(4 + 4 + 3 * FJ)
    weights(26 + 6 + 4 + 3 * FJ)
    raw_of = {e: r for r, e in enumerate(plan)}
    return plan, raw_of


PLAN, RAW_OF = build_plan()

FFN_HEAD = [("a", 0), ("g", 0), ("a", 1), ("g", 1), ("d", 0), ("a", 2), ("g", 2)]
FFN_BODY = [("d", 1), ("a", 3), ("g", 3), ("d", 2), ("a", 4), ("g", 4)]
FFN_LOOPS = (FJ - 3) // 2
FFN_TAIL = [("d", FJ - 2), ("d", FJ - 1)]
MEMKV, WIN1, BR1, WO1, FFN1 = 0, 4, 21, 25, 29
WIN2, BR2, WO2, FFN2 = 62, 88, 94, 98
NW = 131
assert len(PLAN) == NW + 24 and FFN2 + 3 * FJ == NW

IN1 = ["qa", "qa", "kava", "qd", "qd", "kd", "kd", "vd", "vd"] + ["ga"] * 4 + ["gd"] * 4
IN2 = [(k, c0 + 256 * i) for k, c0, n in (("q", 1536, 2), ("k", 2048, 2), ("v", 2560, 2), ("qm", 3072, 2),
                                           ("cc", 512, 2), ("cx", 1024, 2), ("cb", 0, 2), ("g", 3584, 12))
       for i in range(n)]

ITEMS1 = {4: ("swa", 0), 5: ("swa", 1), 6: ("swa", 2), 7: ("swa", 3),
          8: ("diff", 0), 9: ("diff", 1), 10: ("diff", 2), 11: ("diff", 3)}
ITEMS2 = {10: ("moba", 0), 11: ("moba", 1), 12: ("moba", 2), 13: ("moba", 3), 14: ("mem", 0), 15: ("mem", 1)}
ITEM_NO = {("swa", i): i for i in range(4)}
ITEM_NO.update({("diff", i): 4 + i for i in range(4)})
ITEM_NO.update({("moba", i): 8 + i for i in range(4)})
ITEM_NO.update({("mem", i): 12 + i for i in range(2)})
Y_TILE = {"swa": 0, "moba": 4}

SCORE_BANK, PT_BANKS, PV_BANK, NORM_BANK, MOD_COL = 4, (3, 6), 7, 3, 384


def unit_banks(w):
    for first, n in ((BR1, 4), (BR2, 6)):
        if first <= w < first + n:
            b = 2 * ((w - first) % 4)
            return (b, b + 1)
    return (w % 3,)


def build_evacuations():
    counts, done, last_in, before = {"act": 0, "dve": 0, "x1": 0, "x5": 0}, {}, {}, {}
    for w in [*range(FFN1), *range(WIN2, FFN2)]:
        if w == WIN2:
            last_in = {}
        on_dve = (BR1 <= w < FFN1 or BR2 <= w < FFN2
                  or WIN2 <= w < BR2 and IN2[w - WIN2][0] in ("cx", "cb"))
        e = "x1" if WO1 <= w < FFN1 else "x5" if WO2 <= w < FFN2 else "dve" if on_dve else "act"
        counts[e] += 1
        done[w] = (e, counts[e])
        before[w] = {last_in[b] for b in unit_banks(w) if b in last_in}
        for b in unit_banks(w):
            last_in[b] = w
    return done, before


EVACUATED, BANK_BEFORE = build_evacuations()


def item_spans(kind):
    return {"mem": [(1, 257), (257, 513)], "swa": [(0, 129), (129, 386)]}.get(kind, [(1, 129), (129, 385)])


def two_map_items(n):
    return n + 1 if n < 4 else n - 3


MOD_SLOTS = {5: 2, 9: 3, 13: 4, 16: 5}
MOD_PV = {2: 0, 3: 4, 4: 8, 5: 8}

MADE_IDENT, MADE_EPS, MADE_MATRICES, MADE_DIST, MADE_ALL = 2, 3, 9, 11, 18
N_SMALL = len(VA_ROWS) + len(VB_ROWS) + len(VC_ROWS) + 6


def two_blocks(nc, t, out):
    ctx = ExitStack()
    with ctx:
        base = [(nc.sbuf_base + 63) // 64 * 64]

        def place(name, shape, dt, at=None):
            n = int(np.prod(shape[1:])) * 4
            where = base[0] if at is None else at
            if at is None:
                base[0] += (n + 63) // 64 * 64
            return nc.alloc_sbuf_tensor_at(name, shape, dt, offset=where), where

        raw, _ = place("raw", [P, RAW, UNIT], F32)
        whi, _ = place("whi", [P, SPLIT, UNIT], F32R)
        wlo, _ = place("wlo", [P, SPLIT, UNIT], F32R)
        x, _ = place("x", [P, KT, S], F32)
        hhi, _ = place("hhi", [P, KT, S], F32R)
        hlo, _ = place("hlo", [P, KT, S], F32R)
        proj, _ = place("proj", [P, 14, S], F32)
        vtok, _ = place("vtok", [P, NT, 640], F32)
        kmem, _ = place("kmem", [P, 4, S], F32)
        vmem, _ = place("vmem", [P, NT, 512], F32)
        yhi, y_at = place("yhi", [P, 12, S], F32R)
        ylo, ylo_at = place("ylo", [P, 12, S], F32R)
        probs, probs_at = place("probs", [P, 2, 514], F32)
        pt, pt_at = place("pt", [P, 2, 512], F32)
        rows, _ = place("rows", [P, 3, P], F32, at=probs_at)
        dist_i, _ = place("dist_i", [P, 384], I32, at=pt_at)
        lam_in, _ = place("lam_in", [P, 4, HD], F32, at=pt_at + 2048)
        dist_swa, _ = place("dist_swa", [P, 384], F32)
        dist_diff, _ = place("dist_diff", [P, 384], F32)
        causal, _ = place("causal", [P, 384], F32)
        vec, _ = place("vec", [P, 3, P], F32)
        ident, _ = place("ident", [P, P], F32)
        mean_d, _ = place("mean_d", [P, P], F32)
        mean_128, _ = place("mean_128", [P, P], F32)
        mean_64, _ = place("mean_64", [P, P], F32)
        small, _ = place("small", [P, 256], F32)
        std, _ = place("std", [P, 512], F32)
        rstd, _ = place("rstd", [P, 512], F32)
        _, scratch_at = place("scratch", [P, 24, S], F32)
        ada = [place(f"ada{i}", [P, D], F32, at=a + 8 * S * 4)[0] for i, a in enumerate((y_at, ylo_at))]
        gate, _ = place("gate", [P, 24, S], F32, at=scratch_at)
        tok, _ = place("tok", [P, 2, NT, D], F32, at=scratch_at)
        tmp, _ = place("tmp", [P, KT, S], F32, at=scratch_at + 16 * S * 4)
        conv_c, _ = place("conv_c", [P, 4, S], F32, at=scratch_at + 12 * S * 4)
        conv_t, _ = place("conv_t", [P, 4, S], F32, at=scratch_at + 8 * S * 4)
        conv_u, _ = place("conv_u", [P, 4, S + 2], F32, at=scratch_at + 19 * S * 4)
        sq_lo, _ = place("sq_lo", [P, KT, S], F32, at=scratch_at)
        sq_mid, _ = place("sq_mid", [P, KT, S], F32, at=scratch_at + 8 * S * 4)
        qk_std, _ = place("qk_std", [P, 4, 512], F32, at=scratch_at)
        fa, _ = place("fa", [P, 2, 2, S + 2], F32, at=scratch_at)
        fc, _ = place("fc", [P, 2, 2 * S], F32, at=scratch_at + 5 * 1024)
        fg, _ = place("fg", [P, 2, 2 * S], F32, at=scratch_at + 9 * 1024)
        fp, _ = place("fp", [P, 2, 2 * S], F32, at=scratch_at + 13 * 1024)
        cw, _ = place("cw", [P, 2, 4, 2], F32)
        fhi, _ = place("fhi", [P, 2, 2 * S], F32R, at=y_at)
        flo, _ = place("flo", [P, 2, 2 * S], F32R, at=y_at + 4096)
        ps = ctx.enter_context(nc.psum_tensor("ps", [P, 8, 512], F32))

        def f32(ap):
            return ap.bitcast(F32)

        mg = proj
        QA, KA, QD, KD = 0, (4, 13), 5, 9
        Q2, K2, QM = 0, 4, 8
        mod = small[:, 0:48]
        gs1, gs2 = small[:, 48:56], small[:, 56:64]
        half_bg = small[:, 64:88]
        cs = small[:, 88:96]
        csig = small[:, 96:104]
        sinks = small[:, 104:112]
        nmax, rsum, rinv = small[:, 112:116], small[:, 116:120], small[:, 120:124]
        neglam = small[:, 124:125]
        lam_d, lam_e, lam_s = small[:, 126:128], small[:, 128:130], small[:, 130:131]
        gdiff, gmq, gmemq = small[:, 131:132], small[:, 132:133], small[:, 133:134]
        eps = small[:, 134:135]
        one = small[:, 135:136]
        rlam = small[:, 136:138]

        def va(name, i=0):
            c = VA[name][0] + i
            return vec[:, 0, c:c + 1]

        def vb(name, i=0):
            c = VB[name][0] + i
            return vec[:, 1, c:c + 1]

        sems = {}

        def sem(name):
            if name not in sems:
                sems[name] = ctx.enter_context(nc.semaphore(name))
            return sems[name]

        landed = [sem(f"raw_landed{i}") for i in range(RAW)]
        raw_done = sem("raw_done")
        hi_ready = sem("hi_ready")
        gemm_done = sem("gemm_done")
        emptied = {"act": sem("emptied_by_act"), "dve": sem("emptied_by_dve"),
                   "x1": sem("x1_ready"), "x5": sem("x5_ready")}

        def kview(w):
            return w.rearrange("(t p) n -> p t n", p=P)

        w_ada, w_in1, w_in2, w_kv = kview(t["w_ada"][0]), kview(t["w_in"][0]), kview(t["w_in_2"]), kview(t["w_mem_kv_2"])
        br1 = [kview(t["w_branch_swa"][0]), kview(t["w_branch_diff"][0])]
        br2 = [kview(t["w_br_conv_2"]), kview(t["w_br_moba_2"]), kview(t["w_br_mem_2"])]
        w_o1, w_o2 = kview(t["w_out"][0]), kview(t["w_o_2"])
        w_up = [kview(t["w_up"][0]), kview(t["w_up_2"])]
        w_down = [kview(t["w_down"][0]), kview(t["w_down_2"])]

        def unit_source(w):
            if w < WIN1:
                return w_kv[:, :, 256 * w:256 * w + 256]
            if w < BR1:
                c = 256 * (w - WIN1)
                return w_in1[:, :, c:c + 256]
            if w < WO1:
                b = w - BR1
                return br1[b % 2][:, :, 512 * (b // 2):512 * (b // 2) + 512]
            if w < FFN1:
                c = 256 * (w - WO1)
                return w_o1[:, :, c:c + 256]
            if w < BR2:
                c = IN2[w - WIN2][1]
                return w_in2[:, :, c:c + 256]
            if w < WO2:
                b = w - BR2
                return br2[b % 3][:, :, 512 * (b // 3):512 * (b // 3) + 512]
            c = 256 * (w - WO2)
            return w_o2[:, :, c:c + 256]

        def ada_source(a):
            m, k = a // 4, a % 4
            return w_ada[:, 2 * k:2 * k + 2, D * m:D * m + D]

        def ffn_source(f, kind, j):
            if kind == "d":
                return w_down[f][:, bass.ds(j * 2, 2), :]
            return w_up[f][:, :, bass.ds(j * 256 + (F if kind == "g" else 0), 256)]

        def as_unit(slot, like):
            return raw[:, slot, :].rearrange("p (a b) -> p a b", b=like.shape[2])

        block = ctx.enter_context(nc.Block())

        FF = [FFN1, FFN2]

        @block.sync
        def _(sp):
            for i, name in enumerate(("mem_2", "x")):
                sp.dma_start(tok[:, 1 - i], t[name][0].rearrange("(t p) d -> p t d", p=P)).then_inc(sem(f"tok_landed_{name}"), 16)

            def load(r, src, it=0):
                if r >= RAW:
                    sp.wait_ge(raw_done, it * 6 + (r - RAW + 1))
                sp.dma_start(as_unit(r % RAW, src), src).then_inc(landed[r % RAW], 16)

            def load_ffn(f):
                r0 = RAW_OF[("w", FF[f])]
                for c, (kind, j) in enumerate(FFN_HEAD):
                    load(r0 + c, ffn_source(f, kind, j))
                with sp.Fori(0, FFN_LOOPS) as it:
                    for c, (kind, j) in enumerate(FFN_BODY):
                        load(r0 + len(FFN_HEAD) + c, ffn_source(f, kind, it * 2 + j), it)
                for c, (kind, j) in enumerate(FFN_TAIL):
                    load(r0 + 3 * FJ - len(FFN_TAIL) + c, ffn_source(f, kind, j))

            for r, (kind, n) in enumerate(PLAN):
                if kind == "ada":
                    load(r, ada_source(n))
                elif n in FF:
                    load_ffn(FF.index(n))
                elif FFN1 <= n < WIN2 or n >= FFN2:
                    continue
                else:
                    load(r, unit_source(n))
            for tt in range(NT):
                sp.wait_ge(sem("out_act"), tt + 1)
                sp.wait_ge(sem("out_dve"), tt + 1)
                sp.dma_start(out[0, P * tt:P * tt + P, :], tok[:, 0, tt, :]).then_inc(sem("stored"), 16)
            sp.wait_ge(sem("stored"), 16 * NT)

        @block.gpsimd
        def _(pool):
            n = 0

            def step(ins):
                nonlocal n
                n += 1
                ins.then_inc(sem("const_made"), 1)
                pool.wait_ge(sem("const_made"), n)

            step(nc.gpsimd.memset(ident[:, :], 0.0))
            step(nc.gpsimd.affine_select(out=ident[:, :], in_=ident[:, :], compare_op=ALU.not_equal, fill=1.0,
                                         base=0, pattern=[[-1, P]], channel_multiplier=1))
            step(nc.gpsimd.memset(eps, EPS))
            step(nc.gpsimd.memset(one, 1.0))
            step(nc.gpsimd.memset(mean_d[:, :], 1.0 / D))
            step(nc.gpsimd.memset(mean_128[:, :], 1.0 / 128))
            step(nc.gpsimd.memset(mean_64[:, :], 0.0))
            step(nc.gpsimd.memset(mean_64[0:64, 0:64], 1.0 / 64))
            step(nc.gpsimd.memset(mean_64[64:128, 64:128], 1.0 / 64))
            step(nc.gpsimd.iota(dist_i[:, 0:128], pattern=[[-1, 128]], base=0, channel_multiplier=1))
            step(nc.gpsimd.iota(dist_i[:, 128:384], pattern=[[-1, 256]], base=128, channel_multiplier=1))
            step(nc.gpsimd.memset(causal[:, :], 0.0))
            pool.wait_ge(sem("dist_float"), 1)
            for tile, fill in ((dist_diff, BIG), (causal, -BIG)):
                for c0, cn, b in ((0, 128, 0), (128, 256, 128)):
                    step(nc.gpsimd.affine_select(out=tile[:, c0:c0 + cn], in_=tile[:, c0:c0 + cn], compare_op=ALU.is_ge,
                                                 fill=fill, base=b, pattern=[[-1, cn]], channel_multiplier=1))
            step(nc.gpsimd.tensor_copy(dist_swa[:, 0:128], dist_diff[:, 0:128]))
            step(nc.gpsimd.affine_select(out=dist_swa[:, 128:384], in_=dist_diff[:, 128:384], compare_op=ALU.is_ge,
                                         fill=BIG, base=127 - 128, pattern=[[1, 256]], channel_multiplier=-1))
            assert n == MADE_ALL

        @block.scalar
        def _(act):
            def small_load(dst, src):
                act.dma_start(dst, src).then_inc(sem("small_landed"), 16)

            def as_rows(ap):
                if len(ap.shape) == 2:
                    ap = ap.rearrange("a b -> (a b)")
                elif len(ap.shape) == 3:
                    ap = ap.rearrange("a b c -> (a b c)")
                return ap.rearrange("(r c) -> r c", c=P)

            for k, table in enumerate((VA, VB, VC)):
                for name, (r, n) in table.items():
                    small_load(rows[r:r + n, k, :], as_rows(t[name]))
            for r, name in ((MOBA_Q_COL, "moba_q_gain_2"), (MOBA_K_COL, "moba_k_gain_2")):
                for half in range(2):
                    small_load(rows[r:r + 1, 0, HD * half:HD * half + HD], t[name].rearrange("(a n) -> a n", a=1))
            small_load(sinks, t["swa_sinks"].to_broadcast([P, 8]))
            small_load(lam_in[:, :, :].rearrange("p a b -> p (a b)"),
                       t["diff_lambda"].rearrange("o a b -> o (a b)").to_broadcast([P, 4 * HD]))

            def copy(dst, src, func=ACT.Copy, **kw):
                return nc.scalar.activation(dst, src, func, **kw)

            def round_unit(w, it=0):
                if w >= NW:
                    return
                r = RAW_OF[("w", w)]
                act.wait_ge(landed[r % RAW], it * 16 + 16 * (r // RAW + 1))
                if w >= SPLIT:
                    act.wait_ge(gemm_done, it * 6 + (w - SPLIT + 1))
                copy(whi[:, w % SPLIT, :], raw[:, r % RAW, :]).then_inc(hi_ready, 1)

            def square_all(src, dst, ready=None, first=0):
                for i in range(4):
                    if ready is not None:
                        act.wait_ge(ready, first + i + 1)
                    copy(dst[:, 2 * i:2 * i + 2, :], src[:, 2 * i:2 * i + 2, :], ACT.Square).then_inc(sem("sq_ready"), 1)

            def root(n):
                act.wait_ge(sem("mean_done"), n + 1)
                copy(std[:, 0:S], ps[:, NORM_BANK, 0:S], ACT.Sqrt, bias=eps).then_inc(sem("std_ready"), 1)

            def round_h(k, shift=None):
                for c in range(KT):
                    act.wait_ge(sem("scaled_ready"), KT * k + c + 1)
                    if shift is None:
                        ins = copy(hhi[:, c, :], tmp[:, c, :])
                    else:
                        ins = copy(hhi[:, c, :], tmp[:, c, :], ACT.Identity, bias=shift[:, c:c + 1])
                    ins.then_inc(sem("hhi_ready"), 1)

            def empty(w, dst, src, func=ACT.Copy, **kw):
                act.wait_ge(gemm_done, w + 1)
                copy(dst, src, func, **kw).then_inc(emptied["act"], 1)

            def pair(bank):
                return bank.rearrange("p (a b) -> p a b", a=2)

            act.wait_ge(sem("turned"), 1)
            copy(vec[:, 0, 0:NA], ps[:, 7, 0:NA])
            copy(vec[:, 1, 0:NB], ps[:, 7, 128:128 + NB])
            copy(vec[:, 2, 0:NC_], ps[:, 7, 256:256 + NC_]).then_inc(sem("vec_ready"), 1)
            for i in range(4):
                act.wait_ge(sem("turned"), 2 + i)
                copy(proj[:, 2 * i:2 * i + 2, :], pair(ps[:, i, :])).then_inc(sem("mem_ready"), 1)
            square_all(proj, sq_mid, sem("mem_ready"))
            for i in range(4):
                act.wait_ge(sem("turned"), 6 + i)
                copy(x[:, 2 * i:2 * i + 2, :], pair(ps[:, 4 + i, :])).then_inc(sem("x_ready"), 1)
            act.wait_ge(sem("const_made"), MADE_EPS)
            root(0)
            act.wait_ge(sem("vec_ready"), 1)
            c0 = VA["c"][0]
            copy(csig, vec[:, 0, c0:c0 + 8], ACT.Sigmoid).then_inc(sem("csig_ready"), 1)
            act.wait_ge(sem("lam_dots"), 2)
            copy(lam_e, lam_d, ACT.Exp).then_inc(sem("lam_exp"), 1)
            round_unit(0)
            round_unit(1)
            round_h(0)
            square_all(x, sq_lo, sem("x_ready"))
            round_unit(2)
            round_unit(3)
            for w in range(4):
                bank = ps[:, unit_banks(w)[0], :]
                if w < 2:
                    act.wait_ge(gemm_done, w + 1)
                    copy(sq_mid[:, 2 * w:2 * w + 2, :], pair(bank), ACT.Square).then_inc(sem("memk_sq"), 1)
                    empty(w, kmem[:, 2 * w:2 * w + 2, :], pair(bank))
                else:
                    empty(w, vmem[:, :, 256 * (w - 2):256 * (w - 2) + 256], pair(bank))
            root(1)
            for i in range(2):
                act.wait_ge(sem("memk_mean"), i + 1)
                copy(qk_std[:, 2 + i, :], ps[:, 4 + i, :], ACT.Sqrt, bias=eps).then_inc(sem("memk_std"), 1)
            round_unit(4)
            round_unit(5)
            act.wait_ge(sem("mods_ready"), 1)
            round_h(1, shift=mod[:, 0:8])

            def exps(item):
                kind, i = item
                n = ITEM_NO[item]
                act.wait_ge(sem("max_ready"), n + 1)
                for m in range(2):
                    for q, (a, b) in enumerate(item_spans(kind)):
                        src = ps[:, SCORE_BANK + m, a - 1:b - 1] if kind == "mem" else probs[:, m, a:b]
                        c = 2 * m + q
                        ins = copy(probs[:, m, a:b], src, ACT.Exp, bias=nmax[:, c:c + 1], accum_out=rsum[:, c:c + 1])
                ins.then_inc(sem("exp_done"), 1)

            def empty_pt(item):
                act.wait_ge(sem("pt_done"), ITEM_NO[item] + 1)
                w = 512 if item[0] == "mem" else 384
                copy(pt[:, 0, 0:w], ps[:, PT_BANKS[0], 0:w]).then_inc(sem("pt0_ready"), 1)

            def empty_pv(item):
                kind, i = item
                act.wait_ge(sem("pv_done"), ITEM_NO[item] + 1)
                if kind == "diff":
                    copy(proj[:, KD + i, :], ps[:, PV_BANK, 0:S], ACT.Square)
                    ins = copy(proj[:, QD + i, :], ps[:, PV_BANK, 0:S])
                elif kind == "mem":
                    ins = copy(yhi[:, 8 + 2 * i:10 + 2 * i, :], pair(ps[:, PV_BANK, :]))
                else:
                    ins = copy(yhi[:, Y_TILE[kind] + i, :], ps[:, PV_BANK, 0:S])
                ins.then_inc(sem("yhi_ready"), 1)

            def attention(items, s):
                if s - 2 in items:
                    empty_pv(items[s - 2])
                if s - 1 in items:
                    empty_pt(items[s - 1])
                if s in items:
                    exps(items[s])

            for s in range(18):
                round_unit(WIN1 + s + 2)
                if s >= 1:
                    w, k = WIN1 + s - 1, s - 1
                    kind, bank = IN1[k], ps[:, unit_banks(w)[0], :]
                    if kind == "qa":
                        empty(w, proj[:, QA + 2 * k:QA + 2 * k + 2, :], pair(bank), scale=HD ** -0.5)
                    elif kind == "kava":
                        act.wait_ge(gemm_done, w + 1)
                        copy(proj[:, KA[0], :], bank[:, 0:S])
                        copy(proj[0:64, KA[1], :], bank[64:128, 0:S])
                        copy(proj[64:128, KA[1], :], bank[0:64, 0:S])
                        empty(w, vtok[:, :, 512:640], pair(bank[:, S:2 * S]))
                    elif kind == "qd":
                        c = QD + 2 * (k - 3)
                        empty(w, proj[:, c:c + 2, :], pair(bank), scale=HD ** -0.5)
                    elif kind == "kd":
                        c = KD + 2 * (k - 5)
                        empty(w, proj[:, c:c + 2, :], pair(bank))
                    elif kind == "vd":
                        c = 256 * (k - 7)
                        empty(w, vtok[:, :, c:c + 256], pair(bank))
                    else:
                        empty(w, gate[:, 2 * (k - 9):2 * (k - 9) + 2, :], pair(bank), ACT.Tanh, scale=0.5)
                attention(ITEMS1, s)
                if s == 14:
                    for i in range(2):
                        act.wait_ge(sem("diff_mean"), i + 1)
                        copy((std, rstd)[i][:, :], ps[:, 4 + i, :], ACT.Sqrt, bias=eps).then_inc(sem("diff_std"), 1)
                if s == 15:
                    for i in range(2):
                        act.wait_ge(sem("diff_out"), i + 1)
                        copy(yhi[:, 4 + 2 * i:6 + 2 * i, :], proj[:, QD + 2 * i:QD + 2 * i + 2, :])\
                            .then_inc(sem("ydhi_ready"), 1)

            def merge_and_project(b0, nbr, o0, k, start):
                for u in range(2 * nbr):
                    if u >= start:
                        round_unit(b0 + u + 2)
                    if u >= 1 and u % nbr == 0:
                        round_merged(k, 0)
                round_unit(o0 + 2)
                round_merged(k, 1)
                for u in range(1, 4):
                    round_unit(o0 + u + 2)

            def round_merged(k, half):
                for i in range(2):
                    act.wait_ge(sem("merged"), 4 * k + 2 * half + i + 1)
                    c = 4 * half + 2 * i
                    copy(hhi[:, c:c + 2, :], mg[:, c:c + 2, :], scale=0.5).then_inc(sem("mghi_ready"), 1)

            merge_and_project(BR1, 2, WO1, 0, 1)
            square_all(x, mg, sem("x1_ready"))
            root(2)
            act.wait_ge(sem("mods_ready"), 4)
            round_h(2, shift=mod[:, 24:32])

            def ffn(f):
                w0 = FF[f]
                func = (ACT.Gelu, ACT.Silu)[f]

                def pad_a(c, j, b, it=0):
                    act.wait_ge(gemm_done, it * 6 + (w0 + c + 1))
                    if j >= 2:
                        act.wait_ge(sem(f"conv_done{f}"), it * 2 + (j - 1))
                    else:
                        act.wait_ge(sem(f"pads_ready"), f + 1)
                    copy(fa[:, b, :, 2:S + 2], pair(ps[:, (0, 2)[b], :])).then_inc(sem(f"a_ready{f}"), 1)

                def activate(j, b, it=0):
                    act.wait_ge(sem(f"conv_done{f}"), it * 2 + (j + 1))
                    if j >= 2:
                        act.wait_ge(sem(f"glu_done{f}"), it * 2 + (j - 1))
                    copy(fg[:, b, :], fc[:, b, :], func).then_inc(sem(f"act_done{f}"), 1)

                def round_product(j, b, it=0):
                    act.wait_ge(sem(f"glu_done{f}"), it * 2 + (j + 1))
                    if j >= 2:
                        act.wait_ge(gemm_done, it * 6 + (w0 + 3 * j - 1))
                    copy(fhi[:, b, :], fp[:, b, :]).then_inc(sem(f"fhi_ready{f}"), 1)

                def slot(c, kind, j, it=0):
                    round_unit(w0 + c + 2, it)
                    if kind == "g":
                        pad_a(c - 1, j, j % 2, it)
                    if kind == "d" and j + 1 < FJ or kind == "a" and c == 2:
                        k = j + 1 if kind == "d" else 0
                        activate(k, k % 2, it)
                        round_product(k, k % 2, it)

                for c, (kind, j) in enumerate(FFN_HEAD):
                    slot(c, kind, j)
                with act.Fori(0, FFN_LOOPS) as it:
                    for c, (kind, j) in enumerate(FFN_BODY):
                        slot(len(FFN_HEAD) + c, kind, j, it)
                for c, (kind, j) in enumerate(FFN_TAIL):
                    slot(3 * FJ - len(FFN_TAIL) + c, kind, j)

            ffn(0)
            square_all(x, mg, sem("x2_ready"))
            root(3)
            square_all(x, mg, sem("x3_ready"))
            root(4)
            round_h(3)

            for s in range(27):
                round_unit(WIN2 + s + 2)
                if s >= 1:
                    w, k = WIN2 + s - 1, s - 1
                    kind, bank = IN2[k][0], ps[:, unit_banks(w)[0], :]
                    if kind in ("q", "k"):
                        act.wait_ge(gemm_done, w + 1)
                        copy(tmp[:, 2 * k:2 * k + 2, :], pair(bank), ACT.Square).then_inc(sem("qk_sq"), 1)
                        empty(w, proj[:, 2 * k:2 * k + 2, :], pair(bank))
                    elif kind == "v":
                        empty(w, vtok[:, :, 256 * (k - 4):256 * (k - 4) + 256], pair(bank))
                    elif kind == "qm":
                        c = 2 * (k - 6)
                        act.wait_ge(gemm_done, w + 1)
                        copy(conv_t[:, c:c + 2, :], pair(bank), ACT.Square).then_inc(sem("qm_sq"), 1)
                        empty(w, proj[:, QM + c:QM + c + 2, :], pair(bank))
                    elif kind == "cc":
                        c = 2 * (k - 8)
                        empty(w, conv_c[:, c:c + 2, :], pair(bank))
                    elif kind == "g":
                        act.wait_ge(gemm_done, w + 1)
                        g = 2 * (k - 14)
                        copy(gate[:, g, :], bank[:, 0:S], ACT.Tanh, scale=0.5, bias=half_bg[:, g:g + 1])
                        empty(w, gate[:, g + 1, :], bank[:, S:2 * S], ACT.Tanh, scale=0.5, bias=half_bg[:, g + 1:g + 2])
                attention(ITEMS2, s)
                if s == 5:
                    for i in range(4):
                        act.wait_ge(sem("qk_mean"), i + 1)
                        copy(qk_std[:, i, :], ps[:, 4 + i, :], ACT.Sqrt, bias=eps).then_inc(sem("qk_std"), 1)
                if s == 9:
                    for i in range(2):
                        act.wait_ge(sem("qm_mean"), i + 1)
                        copy((std, rstd)[i][:, :], ps[:, 4 + i, :], ACT.Sqrt, bias=eps).then_inc(sem("qm_std"), 1)
                if s in (14, 15):
                    i = s - 14
                    act.wait_ge(emptied["dve"], EVACUATED[WIN2 + 12 + i][1])
                    copy(yhi[:, 2 * i:2 * i + 2, :], conv_t[:, 2 * i:2 * i + 2, :]).then_inc(sem("ychi_ready"), 1)
            merge_and_project(BR2, 3, WO2, 1, 1)
            square_all(x, mg, sem("x5_ready"))
            root(5)
            round_h(4)
            ffn(1)
            for tt in range(NT):
                act.wait_ge(sem("out_turned"), 2 * tt + 1)
                copy(tok[:, 0, tt, 0:512], ps[:, 2 * tt, :]).then_inc(sem("out_act"), 1)

        @block.vector
        def _(dve):
            V = nc.vector
            link_n = 0

            def link(ins):
                nonlocal link_n
                link_n += 1
                ins.then_inc(sem("dve_step"), 1)
                dve.wait_ge(sem("dve_step"), link_n)

            def pair(bank):
                return bank.rearrange("p (a b) -> p a b", a=2)

            def fold_ada(a):
                r, m, k = RAW_OF[("ada", a)], a // 4, a % 4
                acc = ada[m % 2]
                if k == 0 and m >= 2:
                    dve.wait_ge(sem("mod_done"), m - 1)
                dve.wait_ge(landed[r % RAW], 16 * (r // RAW + 1))
                src = raw[:, r % RAW, :].rearrange("p (a b) -> p a b", a=2)
                if k:
                    dve.wait_ge(raw_done, RAW_OF[("ada", a - 1)] + 1)
                    link(V.scalar_tensor_tensor(out=acc[:, :], in0=src[:, 0, :], scalar=cs[:, 2 * k:2 * k + 1],
                                                in1=acc[:, :], op0=ALU.mult, op1=ALU.add))
                else:
                    link(V.tensor_scalar(acc[:, :], src[:, 0, :], cs[:, 0:1], None, ALU.mult))
                V.scalar_tensor_tensor(out=acc[:, :], in0=src[:, 1, :], scalar=cs[:, 2 * k + 1:2 * k + 2],
                                       in1=acc[:, :], op0=ALU.mult, op1=ALU.add).then_inc(raw_done, 1)

            def split_low(w, it=0):
                if w >= NW:
                    return
                r = RAW_OF[("w", w)]
                dve.wait_ge(hi_ready, it * 6 + (w + 1))
                if w >= SPLIT:
                    dve.wait_ge(gemm_done, it * 6 + (w - SPLIT + 1))
                V.tensor_tensor(wlo[:, w % SPLIT, :], raw[:, r % RAW, :], f32(whi[:, w % SPLIT, :]),
                                ALU.subtract).then_inc(raw_done, 1)
                r += 1
                while r < len(PLAN) and PLAN[r][0] == "ada":
                    fold_ada(PLAN[r][1])
                    r += 1

            def mods(m):
                dve.wait_ge(sem("mod_done"), m + 1)
                c = VA["b_ada"][0] + 8 * m
                V.tensor_tensor(mod[:, 8 * m:8 * m + 8], ps[:, 7, MOD_COL + 8 * m:MOD_COL + 8 * m + 8],
                                vec[:, 0, c:c + 8], ALU.add).then_inc(sem("mods_ready"), 1)
                dve.wait_ge(sem("mods_ready"), m + 1)

            def gains(dst, m, name):
                c = VA[name][0]
                link(V.scalar_tensor_tensor(out=dst, in0=mod[:, 8 * m:8 * m + 8], scalar=1.0, in1=vec[:, 0, c:c + 8],
                                            op0=ALU.add, op1=ALU.mult))

            def rsqrt_of(n):
                dve.wait_ge(sem("std_ready"), n + 1)
                link(V.reciprocal(rstd[:, 0:S], std[:, 0:S]))

            def norm_h(k, n, src, gcol, shift=None):
                rsqrt_of(n)
                for c in range(KT + 2):
                    if c < KT:
                        V.scalar_tensor_tensor(out=tmp[:, c, :], in0=src[:, c, :], scalar=gcol(c), in1=rstd[:, 0:S],
                                               op0=ALU.mult, op1=ALU.mult).then_inc(sem("scaled_ready"), 1)
                    if c >= 2:
                        e = c - 2
                        dve.wait_ge(sem("hhi_ready"), KT * k + e + 1)
                        if shift is None:
                            ins = V.tensor_tensor(hlo[:, e, :], tmp[:, e, :], f32(hhi[:, e, :]), ALU.subtract)
                        else:
                            ins = V.scalar_tensor_tensor(out=hlo[:, e, :], in0=tmp[:, e, :], scalar=shift[:, e:e + 1],
                                                         in1=f32(hhi[:, e, :]), op0=ALU.add, op1=ALU.subtract)
                        ins.then_inc(sem("hlo_ready"), 1)

            dve.wait_ge(sem("small_landed"), 16 * N_SMALL)
            for i in range(2):
                V.tensor_tensor_reduce(out=lam_in[:, 2 * i, :], in0=lam_in[:, 2 * i, :], in1=lam_in[:, 2 * i + 1, :],
                                       scale=1.0, scalar=0.0, op0=ALU.mult, op1=ALU.add,
                                       accum_out=lam_d[:, i:i + 1]).then_inc(sem("lam_dots"), 1)
            dve.wait_ge(sem("const_made"), MADE_DIST)
            V.tensor_copy(dist_diff[:, :], dist_i[:, :]).then_inc(sem("dist_float"), 1)
            dve.wait_ge(sem("csig_ready"), 1)
            dve.wait_ge(sem("vec_ready"), 1)
            c0 = VA["c"][0]
            V.tensor_tensor(cs, vec[:, 0, c0:c0 + 8], csig, ALU.mult)
            V.tensor_scalar(gdiff, va("diff_subln_g"), 1.0 - LAM_INIT, None, ALU.mult)
            V.tensor_scalar(gmq, vec[:, 0, MOBA_Q_COL:MOBA_Q_COL + 1], HD ** -0.5, None, ALU.mult)
            V.tensor_scalar(gmemq, va("memq_gain_2"), P ** -0.5, None, ALU.mult)
            V.tensor_scalar(half_bg, vec[:, 1, 0:24], 0.5, None, ALU.mult)
            dve.wait_ge(sem("lam_exp"), 1)
            link(V.tensor_tensor(lam_s, lam_e[:, 0:1], lam_e[:, 1:2], ALU.subtract))
            link(V.tensor_scalar(neglam, lam_s, LAM_INIT, -1.0, ALU.add, ALU.mult))

            norm_h(0, 0, proj, lambda c: va("g_mem_2", c))
            split_low(0)
            split_low(1)
            split_low(2)
            split_low(3)
            for i in range(2):
                dve.wait_ge(sem("memk_std"), i + 1)
                link(V.reciprocal(qk_std[:, 2 + i, :], qk_std[:, 2 + i, :]))
                dve.wait_ge(emptied["act"], i + 1)
                V.scalar_tensor_tensor(out=kmem[:, 2 * i:2 * i + 2, :], in0=kmem[:, 2 * i:2 * i + 2, :],
                                       scalar=va("memk_gain_2"), in1=pair(qk_std[:, 2 + i, :]),
                                       op0=ALU.mult, op1=ALU.mult).then_inc(sem("kmem_ready"), 1)
            mods(0)
            mods(1)
            gains(gs1, 1, "norm1_g")
            split_low(4)
            norm_h(1, 1, x, lambda c: gs1[:, c:c + 1], shift=mod[:, 0:8])
            split_low(5)

            def scores(item):
                kind, i = item
                n = ITEM_NO[item]
                if kind == "mem":
                    dve.wait_ge(sem("scores_done"), n + 1)
                else:
                    if n:
                        dve.wait_ge(sem("pt_done"), n)
                    if kind == "swa":
                        for m in range(2):
                            V.tensor_copy(probs[:, m, 0:386:385],
                                          sinks[:, 2 * i + m:2 * i + m + 1].to_broadcast([P, 2]))
                    dve.wait_ge(sem("scores_done"), n + 1)
                    if n == 0:
                        dve.wait_ge(sem("const_made"), MADE_ALL)
                    for m in range(2):
                        slope = {"swa": 2.0 ** -(2 * i + m + 1), "diff": 2.0 ** (-2 * (i + 1)), "moba": -1.0}[kind]
                        dist = {"swa": dist_swa, "diff": dist_diff, "moba": causal}[kind]
                        ins = V.scalar_tensor_tensor(out=probs[:, m, 1:385], in0=dist[:, :], scalar=-slope,
                                                     in1=ps[:, SCORE_BANK + m, 0:384], op0=ALU.mult, op1=ALU.add)
                    link(ins)
                for q, (a, b) in enumerate(item_spans(kind)):
                    src = ps[:, SCORE_BANK:SCORE_BANK + 2, a - 1:b - 1] if kind == "mem" else probs[:, :, a:b]
                    ins = V.tensor_reduce(nmax[:, q:4:2], src, AX_X, ALU.max, negate=True)
                ins.then_inc(sem("max_ready"), 1)

            def normalise(item):
                kind, i = item
                dve.wait_ge(sem("exp_done"), ITEM_NO[item] + 1)
                link(V.reciprocal(rinv, rsum))
                spans = [(1, 257), (257, 513)] if kind == "mem" else [(1, 129), (129, 385)]
                if kind == "diff":
                    link(V.tensor_scalar(rlam, rinv[:, 2:4], neglam, None, ALU.mult))
                    for q, (a, b) in enumerate(spans):
                        ins = V.tensor_scalar(probs[:, 1, a:b], probs[:, 1, a:b], rlam[:, q:q + 1], None, ALU.mult)
                    link(ins)
                    for q, (a, b) in enumerate(spans):
                        ins = V.scalar_tensor_tensor(out=probs[:, 0, a:b], in0=probs[:, 0, a:b], scalar=rinv[:, q:q + 1],
                                                     in1=probs[:, 1, a:b], op0=ALU.mult, op1=ALU.add)
                else:
                    for m in range(2):
                        for q, (a, b) in enumerate(spans):
                            c = 2 * m + q
                            ins = V.tensor_scalar(probs[:, m, a:b], probs[:, m, a:b], rinv[:, c:c + 1], None, ALU.mult)
                ins.then_inc(sem("probs_ready"), 1)

            def empty_pt(item):
                if item[0] == "diff":
                    return
                dve.wait_ge(sem("pt_done"), ITEM_NO[item] + 1)
                w = 512 if item[0] == "mem" else 384
                V.tensor_copy(pt[:, 1, 0:w], ps[:, PT_BANKS[1], 0:w]).then_inc(sem("pt1_ready"), 1)

            def low_pv(item):
                kind, i = item
                if kind == "diff":
                    return
                dve.wait_ge(sem("yhi_ready"), ITEM_NO[item] + 1)
                if kind == "mem":
                    c = slice(8 + 2 * i, 10 + 2 * i)
                    ins = V.tensor_tensor(ylo[:, c, :], pair(ps[:, PV_BANK, :]), f32(yhi[:, c, :]), ALU.subtract)
                else:
                    c = Y_TILE[kind] + i
                    ins = V.tensor_tensor(ylo[:, c, :], ps[:, PV_BANK, 0:S], f32(yhi[:, c, :]), ALU.subtract)
                ins.then_inc(sem("ylo_ready"), 1)

            def attention(items, s):
                if s - 1 in items:
                    empty_pt(items[s - 1])
                if s in items:
                    scores(items[s])
                    normalise(items[s])

            for s in range(18):
                split_low(WIN1 + s + 2)
                if s - 2 in ITEMS1:
                    low_pv(ITEMS1[s - 2])
                if s in MOD_SLOTS:
                    mods(MOD_SLOTS[s])
                attention(ITEMS1, s)
                if s == 14:
                    gains(gs2, 4, "norm2_g")
                    for i in range(2):
                        dve.wait_ge(sem("diff_std"), i + 1)
                        r = (std, rstd)[i]
                        link(V.reciprocal(r[:, :], r[:, :]))
                        c = slice(QD + 2 * i, QD + 2 * i + 2)
                        V.scalar_tensor_tensor(out=proj[:, c, :], in0=proj[:, c, :], scalar=gdiff, in1=pair(r[:, :]),
                                               op0=ALU.mult, op1=ALU.mult).then_inc(sem("diff_out"), 1)
                if s == 15:
                    for i in range(2):
                        dve.wait_ge(sem("ydhi_ready"), i + 1)
                        c = slice(4 + 2 * i, 6 + 2 * i)
                        V.tensor_tensor(ylo[:, c, :], proj[:, QD + 2 * i:QD + 2 * i + 2, :], f32(yhi[:, c, :]),
                                        ALU.subtract).then_inc(sem("ydlo_ready"), 1)

            def merge(w, b, nbr, k):
                r, half = b % nbr, b // nbr
                dve.wait_ge(gemm_done, w + 1)
                for i, bank in enumerate(unit_banks(w)):
                    c = 4 * half + 2 * i
                    g = gate[:, KT * r + c:KT * r + c + 2, :]
                    if r == 0:
                        ins = V.scalar_tensor_tensor(out=mg[:, c:c + 2, :], in0=g, scalar=1.0, in1=pair(ps[:, bank, :]),
                                                     op0=ALU.add, op1=ALU.mult)
                        if i == 1:
                            ins.then_inc(emptied["dve"], 1)
                    else:
                        term = pair(probs[:, i, 0:512])
                        ins = V.scalar_tensor_tensor(out=term, in0=g, scalar=1.0, in1=pair(ps[:, bank, :]),
                                                     op0=ALU.add, op1=ALU.mult)
                        if i == 1:
                            ins.then_inc(emptied["dve"], 1)
                            dve.wait_ge(emptied["dve"], EVACUATED[w][1])
                        else:
                            link(ins)
                        ins = V.tensor_tensor(mg[:, c:c + 2, :], mg[:, c:c + 2, :], term, ALU.add)
                        if r == nbr - 1:
                            ins.then_inc(sem("merged"), 1)
                            dve.wait_ge(sem("merged"), 4 * k + 2 * half + i + 1)
                        else:
                            link(ins)

            def low_merged(k, half):
                for i in range(2):
                    dve.wait_ge(sem("mghi_ready"), 4 * k + 2 * half + i + 1)
                    c = slice(4 * half + 2 * i, 4 * half + 2 * i + 2)
                    V.scalar_tensor_tensor(out=hlo[:, c, :], in0=mg[:, c, :], scalar=0.5, in1=f32(hhi[:, c, :]),
                                           op0=ALU.mult, op1=ALU.subtract).then_inc(sem("mglo_ready"), 1)

            def merge_all(b0, nbr, o0, k, start):
                for u in range(2 * nbr):
                    if u >= start:
                        split_low(b0 + u + 2)
                    if u >= 1:
                        merge(b0 + u - 1, u - 1, nbr, k)
                        if u % nbr == 0:
                            low_merged(k, 0)
                split_low(o0 + 2)
                merge(b0 + 2 * nbr - 1, 2 * nbr - 1, nbr, k)
                low_merged(k, 1)

            merge_all(BR1, 2, WO1, 0, 1)
            for u in range(4):
                w = WO1 + u
                if u:
                    split_low(w + 2)
                dve.wait_ge(gemm_done, w + 1)
                bank = ps[:, unit_banks(w)[0], :]
                for i in range(2):
                    c = 2 * u + i
                    ins = V.scalar_tensor_tensor(out=x[:, c, :], in0=bank[:, S * i:S * i + S],
                                                 scalar=mod[:, 16 + c:17 + c], in1=x[:, c, :], op0=ALU.mult, op1=ALU.add)
                ins.then_inc(sem("x1_ready"), 1)
            norm_h(2, 2, x, lambda c: gs2[:, c:c + 1], shift=mod[:, 24:32])

            def ffn(f):
                w0 = FF[f]
                table = (vec[:, 1, 40:128], vec[:, 2, 0:88])[f].rearrange("p (a b) -> p a b", b=22)
                conv_step = sem(f"conv_step{f}")
                V.memset(fa[:, :, :, 0:2].rearrange("p a b c -> p (a b) c"), 0.0).then_inc(sem("pads_ready"), 1)
                dve.wait_ge(sem("pads_ready"), f + 1)

                def convolve(j, b, it=0):
                    n = it * 10 + 5 * j
                    if j >= 2:
                        dve.wait_ge(sem(f"act_done{f}"), it * 2 + (j - 1))
                    V.tensor_copy(cw[:, b, :, :], table[:, :, bass.ds(it * 4 + 2 * j, 2)]).then_inc(conv_step, 1)
                    dve.wait_ge(sem(f"a_ready{f}"), it * 2 + (j + 1))
                    dve.wait_ge(conv_step, n + 1)
                    for tap in range(3):
                        for c in range(2):
                            dst = fc[:, b, S * c:S * c + S]
                            src = fa[:, b, c, tap:tap + S]
                            if tap == 0:
                                V.tensor_scalar(dst, src, cw[:, b, 0, c:c + 1], cw[:, b, 3, c:c + 1],
                                                ALU.mult, ALU.add).then_inc(conv_step, 1)
                                continue
                            dve.wait_ge(conv_step, n + 2 * tap + c)
                            ins = V.scalar_tensor_tensor(out=dst, in0=src, scalar=cw[:, b, tap, c:c + 1], in1=dst,
                                                         op0=ALU.mult, op1=ALU.add)
                            if tap == 1:
                                ins.then_inc(conv_step, 1)
                    ins.then_inc(sem(f"conv_done{f}"), 1)

                def gate_it(c, j, b, it=0):
                    dve.wait_ge(sem(f"act_done{f}"), it * 2 + (j + 1))
                    dve.wait_ge(gemm_done, it * 6 + (w0 + c + 1))
                    V.tensor_tensor(fp[:, b, :], fg[:, b, :], ps[:, (1, 3)[b], :], ALU.mult)\
                        .then_inc(sem(f"glu_done{f}"), 1)
                    dve.wait_ge(sem(f"fhi_ready{f}"), it * 2 + (j + 1))
                    V.tensor_tensor(flo[:, b, :], fp[:, b, :], f32(fhi[:, b, :]), ALU.subtract)\
                        .then_inc(sem(f"flo_ready{f}"), 1)

                def slot(c, kind, j, it=0):
                    split_low(w0 + c + 2, it)
                    if kind == "g":
                        convolve(j, j % 2, it)
                    if kind == "d" and j + 1 < FJ or kind == "a" and c == 2:
                        k = j + 1 if kind == "d" else 0
                        gate_it(3 * k if k else 1, k, k % 2, it)

                for c, (kind, j) in enumerate(FFN_HEAD):
                    slot(c, kind, j)
                with dve.Fori(0, FFN_LOOPS) as it:
                    for c, (kind, j) in enumerate(FFN_BODY):
                        slot(len(FFN_HEAD) + c, kind, j, it)
                for c, (kind, j) in enumerate(FFN_TAIL):
                    slot(3 * FJ - len(FFN_TAIL) + c, kind, j)
                dve.wait_ge(gemm_done, w0 + 3 * FJ)

            ffn(0)
            for u in range(4):
                for i in range(2):
                    c = 2 * u + i
                    ins = V.scalar_tensor_tensor(out=x[:, c, :], in0=ps[:, 4 + u, S * i:S * i + S],
                                                 scalar=mod[:, 40 + c:41 + c], in1=x[:, c, :], op0=ALU.mult, op1=ALU.add)
                ins.then_inc(sem("x2_ready"), 1)
            rsqrt_of(3)
            for c in range(KT):
                ins = V.scalar_tensor_tensor(out=x[:, c, :], in0=x[:, c, :], scalar=va("final_g", c), in1=rstd[:, 0:S],
                                             op0=ALU.mult, op1=ALU.mult)
                if c % 2:
                    ins.then_inc(sem("x3_ready"), 1)
            norm_h(3, 4, x, lambda c: va("g_mix_2", c))

            for s in range(27):
                split_low(WIN2 + s + 2)
                if s == 5:
                    for i in range(4):
                        dve.wait_ge(sem("qk_std"), i + 1)
                        link(V.reciprocal(qk_std[:, i, :], qk_std[:, i, :]))
                        c = slice(2 * i, 2 * i + 2)
                        g = gmq if i < 2 else vec[:, 0, MOBA_K_COL:MOBA_K_COL + 1]
                        V.scalar_tensor_tensor(out=proj[:, c, :], in0=proj[:, c, :], scalar=g, in1=pair(qk_std[:, i, :]),
                                               op0=ALU.mult, op1=ALU.mult).then_inc(sem("qk_ready"), 1)
                    link(V.memset(conv_u[:, :, 0:2], 0.0))
                if s == 9:
                    for i in range(2):
                        dve.wait_ge(sem("qm_std"), i + 1)
                        r = (std, rstd)[i]
                        link(V.reciprocal(r[:, :], r[:, :]))
                        c = slice(QM + 2 * i, QM + 2 * i + 2)
                        V.scalar_tensor_tensor(out=proj[:, c, :], in0=proj[:, c, :], scalar=gmemq, in1=pair(r[:, :]),
                                               op0=ALU.mult, op1=ALU.mult).then_inc(sem("qm_ready"), 1)
                w, k = WIN2 + s - 1, s - 1
                kind = IN2[k][0] if s else ""
                if kind in ("cx", "cb"):
                    dve.wait_ge(gemm_done, w + 1)
                    bank = pair(ps[:, unit_banks(w)[0], :])
                if kind == "cx":
                    c = slice(2 * (k - 10), 2 * (k - 10) + 2)
                    dve.wait_ge(emptied["act"], EVACUATED[WIN2 + 8 + (k - 10)][1])
                    V.tensor_tensor(conv_u[:, c, 2:S + 2], conv_c[:, c, :], bank, ALU.mult).then_inc(emptied["dve"], 1)
                if kind == "cb":
                    h = k - 12
                    dve.wait_ge(emptied["dve"], EVACUATED[w - 2][1])
                    for tap in range(3):
                        for i in range(2):
                            c = 2 * h + i
                            src, wt = conv_u[:, c, tap:tap + S], vb("conv_w_2", 4 * tap + c)
                            if tap == 0:
                                ins = V.tensor_scalar(conv_t[:, c, :], src, wt, vb("conv_b_2", c), ALU.mult, ALU.add)
                            else:
                                ins = V.scalar_tensor_tensor(out=conv_t[:, c, :], in0=src, scalar=wt, in1=conv_t[:, c, :],
                                                             op0=ALU.mult, op1=ALU.add)
                        link(ins)
                    c = slice(2 * h, 2 * h + 2)
                    V.tensor_tensor(conv_t[:, c, :], conv_t[:, c, :], bank, ALU.mult).then_inc(emptied["dve"], 1)
                if s - 2 in ITEMS2:
                    low_pv(ITEMS2[s - 2])
                attention(ITEMS2, s)
                if s in (14, 15):
                    i = s - 14
                    dve.wait_ge(sem("ychi_ready"), i + 1)
                    c = slice(2 * i, 2 * i + 2)
                    V.tensor_tensor(ylo[:, c, :], conv_t[:, c, :], f32(yhi[:, c, :]), ALU.subtract)\
                        .then_inc(sem("yclo_ready"), 1)
            merge_all(BR2, 3, WO2, 1, 1)
            for u in range(4):
                w = WO2 + u
                if u:
                    split_low(w + 2)
                dve.wait_ge(gemm_done, w + 1)
                V.tensor_tensor(x[:, 2 * u:2 * u + 2, :], x[:, 2 * u:2 * u + 2, :], pair(ps[:, unit_banks(w)[0], :]),
                                ALU.add).then_inc(sem("x5_ready"), 1)
            norm_h(4, 5, x, lambda c: va("g_ffn_2", c))
            ffn(1)
            for u in range(4):
                V.tensor_tensor(x[:, 2 * u:2 * u + 2, :], x[:, 2 * u:2 * u + 2, :], pair(ps[:, 4 + u, :]),
                                ALU.add).then_inc(sem("x6_ready"), 1)
            for tt in range(NT):
                dve.wait_ge(sem("out_turned"), 2 * tt + 2)
                V.tensor_copy(tok[:, 0, tt, 512:1024], ps[:, 2 * tt + 1, :]).then_inc(sem("out_dve"), 1)

        @block.tensor
        def _(pe):
            mm = nc.tensor.matmul

            def three(out_, whi_, wlo_, ahi, alo, start, stop, weights_move=False, **kw):
                terms = [(whi_, ahi), (whi_, alo), (wlo_, ahi)]
                for i, (w_, a_) in enumerate(terms):
                    l, r = (a_, w_) if weights_move else (w_, a_)
                    ins = mm(out_, l, r, start=start and i == 0, stop=stop and i == 2, **kw)
                return ins

            def begin(w):
                pe.wait_ge(raw_done, RAW_OF[("w", w)] + 1)
                for v in sorted(BANK_BEFORE.get(w, ())):
                    e, n = EVACUATED[v]
                    pe.wait_ge(emptied[e], n)

            def wt(ring, w, kt, c, n, width):
                return ring[:, w % SPLIT, kt * width + c:kt * width + c + n]

            def channels(w, i, width, ah, al, kts, ready=None, last=False, bank=None, it=0):
                b = unit_banks(w)[i // 2] if bank is None else bank
                for kt in range(kts):
                    if ready is not None:
                        pe.wait_ge(ready[0], ready[1] + kt + 1)
                    ins = three(ps[:, b, S * (i % 2):S * (i % 2) + S], wt(whi, w, kt, P * i, P, width),
                                wt(wlo, w, kt, P * i, P, width), ah[:, kt, :], al[:, kt, :], kt == 0, kt == kts - 1)
                if last:
                    ins.then_inc(gemm_done, 1)

            def positions(w, tt, c, n, out_, last=False):
                for kt in range(KT):
                    ins = three(out_, wt(whi, w, kt, c, n, 256), wt(wlo, w, kt, c, n, 256),
                                hhi[:, kt, P * tt:P * tt + P], hlo[:, kt, P * tt:P * tt + P], kt == 0, kt == KT - 1,
                                weights_move=True)
                if last:
                    ins.then_inc(gemm_done, 1)

            def mean(matrix, src, bank, width, n_in, done, waits=None):
                for i in range(n_in):
                    if waits is not None:
                        pe.wait_ge(waits[0], waits[1] + i // 2 + 1)
                    ins = mm(ps[:, bank, 0:width], matrix[:, :], src(i), start=i == 0, stop=i == n_in - 1)
                ins.then_inc(done, 1)

            def norm_mean(n, src):
                mean(mean_d, lambda i: src[:, i, :], NORM_BANK, S, KT, sem("mean_done"), (sem("sq_ready"), 4 * n))

            def mod_sums(m):
                pe.wait_ge(raw_done, RAW_OF[("ada", 4 * m + 3)] + 1)
                if m:
                    pe.wait_ge(sem("mods_ready"), m)
                if m >= 2 and MOD_PV[m]:
                    pe.wait_ge(sem("yhi_ready"), MOD_PV[m])
                    pe.wait_ge(sem("ylo_ready"), min(4, MOD_PV[m]))
                for c in range(KT):
                    ins = mm(ps[:, 7, MOD_COL + 8 * m + c:MOD_COL + 8 * m + c + 1], ada[m % 2][:, P * c:P * c + P],
                             one, start=True, stop=True)
                ins.then_inc(sem("mod_done"), 1)

            pe.wait_ge(sem("const_made"), MADE_IDENT)
            pe.wait_ge(sem("small_landed"), 16 * N_SMALL)
            for k, n in enumerate((NA, NB, NC_)):
                ins = nc.tensor.transpose(ps[:, 7, 128 * k:128 * k + n], rows[0:n, k, :], ident[0:n, 0:n])
            ins.then_inc(sem("turned"), 1)
            for j, name in ((1, "mem_2"), (0, "x")):
                pe.wait_ge(sem(f"tok_landed_{name}"), 16)
                for i in range(4):
                    b = i if j else 4 + i
                    if b == 7:
                        pe.wait_ge(sem("vec_ready"), 1)
                    for c in (2 * i, 2 * i + 1):
                        for tt in range(NT):
                            at = S * (c - 2 * i) + P * tt
                            ins = nc.tensor.transpose(ps[:, b, at:at + P], tok[:, j, tt, P * c:P * c + P], ident[:, :])
                    ins.then_inc(sem("turned"), 1)
            pe.wait_ge(sem("const_made"), MADE_MATRICES)
            pe.wait_ge(sem("mem_ready"), 4)
            norm_mean(0, sq_mid)
            for w in range(4):
                begin(w)
                if w < 2:
                    for i in range(2):
                        channels(w, i, 256, hhi, hlo, KT, (sem("hlo_ready"), 0) if w == 0 else None, last=i == 1)
                else:
                    for tt in range(2):
                        positions(w, tt, 0, 256, ps[:, unit_banks(w)[0], 256 * tt:256 * tt + 256], last=tt == 1)
            pe.wait_ge(sem("std_ready"), 1)
            norm_mean(1, sq_lo)
            pe.wait_ge(sem("x_ready"), 4)
            for i in range(2):
                pe.wait_ge(sem("memk_sq"), i + 1)
                mm(ps[:, 4 + i, :], mean_128[:, :], sq_mid[:, 2 * i:2 * i + 2, :].rearrange("p a b -> p (a b)"),
                   start=True, stop=True).then_inc(sem("memk_mean"), 1)
            mod_sums(0)
            mod_sums(1)

            def score_maps(item):
                kind, i = item
                n = ITEM_NO[item]
                if n:
                    pe.wait_ge(sem("exp_done"), n)
                if kind == "diff" and i == 0:
                    pe.wait_ge(emptied["act"], EVACUATED[WIN1 + 6][1])
                if kind == "swa" and i == 0:
                    pe.wait_ge(emptied["act"], EVACUATED[WIN1 + 2][1])
                if kind == "moba" and i == 0:
                    pe.wait_ge(sem("qk_ready"), 4)
                    pe.wait_ge(sem("qm_std"), 2)
                if kind == "mem" and i == 0:
                    pe.wait_ge(sem("qm_ready"), 2)
                    pe.wait_ge(sem("kmem_ready"), 2)
                for m in range(2):
                    part = slice(64 * m, 64 * m + 64)
                    if kind == "swa":
                        q, k = proj[part, QA + i, :], proj[part, KA[0 if i // 2 == m else 1], :]
                    elif kind == "diff":
                        q, k = proj[part, QD + i, :], proj[part, KD + i, :]
                    elif kind == "moba":
                        q, k = proj[part, Q2 + i, :], proj[part, K2 + i, :]
                    else:
                        q, k = proj[:, QM + 2 * i + m, :], kmem[:, 2 * i + m, :]
                    first = 256 if kind == "mem" else 128
                    b = SCORE_BANK + m
                    mm(ps[:, b, 0:first], q[:, 0:P], k[:, 0:first], start=True, stop=True)
                    ins = mm(ps[:, b, first:first + 256], q[:, P:2 * P], k[:, 0:256], start=True, stop=True)
                ins.then_inc(sem("scores_done"), 1)

            def turn_probs(item):
                kind, i = item
                n = ITEM_NO[item]
                pe.wait_ge(sem("probs_ready"), n + 1)
                if n:
                    pe.wait_ge(sem("pt0_ready"), n)
                    pe.wait_ge(sem("pt1_ready"), two_map_items(n - 1) if n - 1 < 4 or n - 1 >= 8 else 4)
                for m in range(1 if kind == "diff" else 2):
                    b = PT_BANKS[m]
                    if kind == "mem":
                        blocks = [(1, 0), (257, 128), (129, 256), (385, 384)]
                    else:
                        blocks = [(1, 0), (129, 128), (257, 256)]
                    for src, dst in blocks:
                        ins = nc.tensor.transpose(ps[:, b, dst:dst + P], probs[:, m, src:src + P], ident[:, :])
                ins.then_inc(sem("pt_done"), 1)

            def values(item):
                kind, i = item
                n = ITEM_NO[item]
                pe.wait_ge(sem("pt0_ready"), n + 1)
                if kind != "diff":
                    pe.wait_ge(sem("pt1_ready"), two_map_items(n))
                if n:
                    pe.wait_ge(sem("yhi_ready"), n)
                    pe.wait_ge(sem("ylo_ready"), two_map_items(n - 1) if n - 1 < 4 or n - 1 >= 8 else 4)
                if kind == "diff" and i == 0:
                    pe.wait_ge(emptied["act"], EVACUATED[WIN1 + 8][1])
                if kind == "moba" and i == 0:
                    pe.wait_ge(emptied["act"], EVACUATED[WIN2 + 5][1])
                if kind in ("swa", "diff"):
                    pe.wait_ge(sem("mods_ready"), mods_before[0])
                for m in range(1 if kind == "diff" else 2):
                    if kind == "swa":
                        o, v = ps[64 * m:64 * m + 64, PV_BANK, 0:S], vtok[:, :, 512 + 64 * (i // 2):576 + 64 * (i // 2)]
                    elif kind == "diff":
                        o, v = ps[:, PV_BANK, 0:S], vtok[:, :, P * i:P * i + P]
                    elif kind == "moba":
                        h = 2 * i + m
                        o, v = ps[64 * m:64 * m + 64, PV_BANK, 0:S], vtok[:, :, 64 * h:64 * h + 64]
                    else:
                        h = 2 * i + m
                        o, v = ps[:, PV_BANK, S * m:S * m + S], vmem[:, :, P * h:P * h + P]
                    mm(o, v[:, 0, :], pt[:, m, 0:256], start=True, stop=False)
                    if kind == "mem":
                        ins = mm(o, v[:, 1, :], pt[:, m, 256:512], start=False, stop=True)
                    else:
                        ins = mm(o[:, P:2 * P], v[:, 1, :], pt[:, m, 256:384], start=False, stop=True)
                ins.then_inc(sem("pv_done"), 1)

            def slot(w, items, s, halves):
                begin(w)
                halves(0)
                if s - 1 in items:
                    turn_probs(items[s - 1])
                if s in items:
                    score_maps(items[s])
                halves(1)
                if s - 1 in items:
                    values(items[s - 1])

            mods_before = [2]
            for s in range(17):
                w = WIN1 + s
                kind = IN1[s]
                ready = (sem("hlo_ready"), KT) if s == 0 else None
                if s in MOD_SLOTS:
                    mod_sums(MOD_SLOTS[s])
                    mods_before[0] = MOD_SLOTS[s] + 1
                b = unit_banks(w)[0]

                def halves(i):
                    if kind == "vd":
                        positions(w, i, 0, 256, ps[:, b, 256 * i:256 * i + 256], last=i == 1)
                    elif kind == "kava" and i == 0:
                        channels(w, 0, 256, hhi, hlo, KT)
                    elif kind == "kava":
                        for tt in range(2):
                            positions(w, tt, P, P, ps[:, b, S + P * tt:S + P * tt + P], last=tt == 1)
                    else:
                        channels(w, i, 256, hhi, hlo, KT, ready, last=i == 1)

                slot(w, ITEMS1, s, halves)
                if s == 13:
                    pe.wait_ge(sem("yhi_ready"), 8)
                    for i in range(2):
                        mm(ps[:, 4 + i, :], mean_128[:, :],
                           proj[:, KD + 2 * i:KD + 2 * i + 2, :].rearrange("p a b -> p (a b)"),
                           start=True, stop=True).then_inc(sem("diff_mean"), 1)

            def branch(w, tile0, waits):
                begin(w)
                for s_, n in waits:
                    pe.wait_ge(s_, n)
                for i in range(4):
                    channels(w, i, 512, yhi[:, tile0:tile0 + 4, :], ylo[:, tile0:tile0 + 4, :], 4, last=i == 3)

            def project_merged(o0, k):
                for u in range(4):
                    begin(o0 + u)
                    for i in range(2):
                        for kt in range(KT):
                            if u == 0 and i == 0 and kt % 2 == 0:
                                pe.wait_ge(sem("mglo_ready"), 4 * k + kt // 2 + 1)
                            ins = three(ps[:, unit_banks(o0 + u)[0], S * i:S * i + S], wt(whi, o0 + u, kt, P * i, P, 256),
                                        wt(wlo, o0 + u, kt, P * i, P, 256), hhi[:, kt, :], hlo[:, kt, :],
                                        kt == 0, kt == KT - 1)
                    ins.then_inc(gemm_done, 1)

            pe.wait_ge(sem("mods_ready"), 6)
            for u in range(4):
                branch(BR1 + u, 4 * (u % 2), [(sem("ylo_ready"), 4)] if u == 0 else [(sem("ydlo_ready"), 2)])
            project_merged(WO1, 0)
            norm_mean(2, mg)

            def ffn(f):
                w0 = FF[f]

                def up(c, kind, j, it=0):
                    w = w0 + c
                    pe.wait_ge(raw_done, it * 6 + (RAW_OF[("w", w)] + 1))
                    if j >= 2:
                        pe.wait_ge(sem(f"a_ready{f}" if kind == "a" else f"glu_done{f}"), it * 2 + (j - 1))
                    bank = 2 * (j % 2) + (kind == "g")
                    for i in range(2):
                        channels(w, i, 256, hhi, hlo, KT, (sem("hlo_ready"), KT * (2, 4)[f]) if c == 0 and i == 0 else None,
                                 last=i == 1, bank=bank)

                def down(c, j, it=0):
                    w = w0 + c
                    first = j == 0 and isinstance(it, int)
                    pe.wait_ge(raw_done, it * 6 + (RAW_OF[("w", w)] + 1))
                    pe.wait_ge(sem(f"flo_ready{f}"), it * 2 + (j + 1))
                    for i in range(KT):
                        for kt in range(2):
                            ins = three(ps[:, 4 + i // 2, S * (i % 2):S * (i % 2) + S], wt(whi, w, kt, P * i, P, D),
                                        wt(wlo, w, kt, P * i, P, D), fhi[:, j % 2, S * kt:S * kt + S],
                                        flo[:, j % 2, S * kt:S * kt + S], first and i % 2 == 0 and kt == 0,
                                        j == FJ - 1 and kt == 1, skip_group_check=True)
                    ins.then_inc(gemm_done, 1)

                def slot_(c, kind, j, it=0):
                    if kind == "d":
                        down(c, j, it)
                    else:
                        up(c, kind, j, it)

                for c, (kind, j) in enumerate(FFN_HEAD):
                    slot_(c, kind, j)
                with pe.Fori(0, FFN_LOOPS) as it:
                    for c, (kind, j) in enumerate(FFN_BODY):
                        slot_(len(FFN_HEAD) + c, kind, j, it)
                for c, (kind, j) in enumerate(FFN_TAIL):
                    slot_(3 * FJ - len(FFN_TAIL) + c, kind, j)

            ffn(0)
            norm_mean(3, mg)
            pe.wait_ge(sem("std_ready"), 4)
            norm_mean(4, mg)

            for s in range(26):
                w = WIN2 + s
                kind = IN2[s][0]
                ready = (sem("hlo_ready"), KT * 3) if s == 0 else None
                b = unit_banks(w)[0]

                def halves(i):
                    if kind == "v":
                        positions(w, i, 0, 256, ps[:, b, 256 * i:256 * i + 256], last=i == 1)
                    else:
                        channels(w, i, 256, hhi, hlo, KT, ready, last=i == 1)

                slot(w, ITEMS2, s, halves)
                if s == 4:
                    for i in range(4):
                        pe.wait_ge(sem("qk_sq"), i + 1)
                        mm(ps[:, 4 + i, :], mean_64[:, :], tmp[:, 2 * i:2 * i + 2, :].rearrange("p a b -> p (a b)"),
                           start=True, stop=True).then_inc(sem("qk_mean"), 1)
                if s == 8:
                    pe.wait_ge(sem("qk_std"), 4)
                    for i in range(2):
                        pe.wait_ge(sem("qm_sq"), i + 1)
                        mm(ps[:, 4 + i, :], mean_128[:, :], conv_t[:, 2 * i:2 * i + 2, :].rearrange("p a b -> p (a b)"),
                           start=True, stop=True).then_inc(sem("qm_mean"), 1)
            for u in range(6):
                r = u % 3
                branch(BR2 + u, 4 * r, [[(sem("yclo_ready"), 2)], [(sem("ylo_ready"), 8)], [(sem("ylo_ready"), 10)]][r])
            project_merged(WO2, 1)
            norm_mean(5, mg)
            ffn(1)
            pe.wait_ge(sem("x6_ready"), 4)
            for tt in range(NT):
                for half in range(2):
                    for c in range(4):
                        ins = nc.tensor.transpose(ps[:, 2 * tt + half, P * c:P * c + P],
                                                  x[:, 4 * half + c, P * tt:P * tt + P], ident[:, :])
                    ins.then_inc(sem("out_turned"), 1)


_INS = ["x", "c", "w_ada", "b_ada", "norm1_g", "w_in", "swa_sinks", "diff_lambda", "diff_subln_g", "w_branch_swa",
        "w_branch_diff", "w_out", "norm2_g", "w_up", "conv_w", "conv_b", "w_down", "final_g", "mem_2", "g_mix_2",
        "w_in_2", "b_gate_2", "conv_w_2", "conv_b_2", "moba_q_gain_2", "moba_k_gain_2", "g_mem_2", "w_mem_kv_2",
        "memq_gain_2", "memk_gain_2", "w_br_conv_2", "w_br_moba_2", "w_br_mem_2", "w_o_2", "g_ffn_2", "w_up_2",
        "ffn_conv_w_2", "ffn_conv_b_2", "w_down_2"]


def kernel(**inputs):
    import concourse.bacc as bacc
    from concourse.bass_utils import run_bass_kernel_spmd

    nc = bacc.Bacc("TRN2", target_bir_lowering=False, num_devices=1, dynamic_dma_scratch_size=2048)
    arrays, tensors = {}, {}
    for name in _INS:
        a = np.ascontiguousarray(inputs[name])
        arrays[f"in_{name}"] = a
        tensors[name] = nc.dram_tensor(f"in_{name}", a.shape, mybir.dt.from_np(a.dtype), kind="ExternalInput").ap()
    out = nc.dram_tensor("out", (1, S, D), F32, kind="ExternalOutput").ap()
    two_blocks(nc, tensors, out)
    r = run_bass_kernel_spmd(nc, [arrays], core_ids=[0])
    return r.results[0]["out"]
```

```python
from contextlib import ExitStack

import numpy as np

import concourse.bass as bass
from concourse import mybir

ALU = mybir.AluOpType
ACT = mybir.ActivationFunctionType
F32 = mybir.dt.float32
F32R = mybir.dt.float32r
I32 = mybir.dt.int32
AX_X = mybir.AxisListType.X

P = 128
D = 1024
KT = D // P
S = 256
NT = S // P
UNIT = 2048
RAW, SPLIT = 4, 4
AHEAD = SPLIT - 1
F = 2816
FJ = F // 256
HD = 64
EPS = 1e-6
BIG = 3e32
LAM_INIT = 0.8 - 0.6

VECTORS = [("b_ada", 48), ("norm1_g", 8), ("norm2_g", 8), ("final_g", 8), ("g_mix_2", 8), ("g_mem_2", 8),
           ("g_ffn_2", 8), ("c", 8), ("diff_subln_g", 1), ("memq_gain_2", 1), ("memk_gain_2", 1),
           ("moba_q_gain_2", 1), ("moba_k_gain_2", 1), ("b_gate_2", 24), ("conv_w_2", 12), ("conv_b_2", 4),
           ("conv_w", 66), ("conv_b", 22), ("ffn_conv_w_2", 66), ("ffn_conv_b_2", 22)]
COLUMN, NV = {}, 0
for _name, _n in VECTORS:
    COLUMN[_name] = NV
    NV += _n


def build_plan():
    plan = []
    w = 0

    def weights(n):
        nonlocal w
        for _ in range(n):
            plan.append(("w", w))
            w += 1

    after = {-1: (0, 1), 0: (2, 3), 1: (4,), 2: (5,), 3: (6, 7)}
    after.update({5 + i: (8 + i,) for i in range(5)})
    after.update({19 + i: (13 + i,) for i in range(7)})
    after.update({29 + i: (20 + i,) for i in range(4)})
    for i in range(-1, NW):
        if i >= 0:
            weights(1)
        plan.extend(("ada", a) for a in after.get(i, ()))
    raw_of = {e: r for r, e in enumerate(plan)}
    return plan, raw_of


MEMKV, WIN1, BR1, WO1, FFN1 = 0, 4, 21, 25, 29
WIN2, BR2, WO2, FFN2 = 62, 88, 94, 98
NW = 131
PLAN, RAW_OF = build_plan()

FFN_HEAD = [("a", 0), ("g", 0), ("a", 1), ("g", 1), ("d", 0), ("a", 2)]
STEPS = 4
FFN_BODY = [(kind, j + back) for j in range(2, 2 + STEPS) for kind, back in (("g", 0), ("d", -1), ("a", 1))]
FFN_LOOPS = (FJ - 3) // STEPS
BODY = len(FFN_BODY)
FFN_TAIL = [("g", FJ - 1), ("d", FJ - 2), ("d", FJ - 1)]
assert len(PLAN) == NW + 24 and FFN2 + 3 * FJ == NW

IN1 = ["qa", "qa", "kava", "qd", "qd", "kd", "kd", "vd", "vd"] + ["ga"] * 4 + ["gd"] * 4
IN2 = [(k, c0 + 256 * i) for k, c0, n in (("q", 1536, 2), ("k", 2048, 2), ("v", 2560, 2), ("qm", 3072, 2),
                                           ("cc", 512, 2), ("cx", 1024, 2), ("cb", 0, 2), ("g", 3584, 12))
       for i in range(n)]

ITEMS1 = {4: ("swa", 0), 5: ("swa", 1), 6: ("swa", 2), 7: ("swa", 3),
          8: ("diff", 0), 9: ("diff", 1), 10: ("diff", 2), 11: ("diff", 3)}
ITEMS2 = {11: ("moba", 0), 13: ("moba", 1), 15: ("moba", 2), 17: ("moba", 3), 19: ("mem", 0), 21: ("mem", 1)}
ITEM_NO = {("swa", i): i for i in range(4)}
ITEM_NO.update({("diff", i): 4 + i for i in range(4)})
ITEM_NO.update({("moba", i): 8 + i for i in range(4)})
ITEM_NO.update({("mem", i): 12 + i for i in range(2)})
Y_TILE = {"swa": 0, "moba": 4}

SCORE_BANK, PT_BANKS, PV_BANK, MOD_COL = 4, (3, 6), 7, 384
NORMS = {"mem": (KT, 0, 3, 3), "one": (KT, 0, 6, 6), "two": (KT, 0, 3, 3), "final": (KT, 0, 3, 3), "mix": (KT, 0, 1, 1),
         "ffn2": (KT, 0, 3, 3), "memk": (4, 1, 4, 4), "diff": (4, 1, 4, 4), "qk": (8, 2, 4, 4), "qm": (4, 1, 6, 6)}
STAT, N_STAT = {}, 0
for _name, (_tiles, _heads, _, _) in NORMS.items():
    STAT[_name] = (N_STAT, NT * (_tiles * _heads or 1))
    N_STAT += STAT[_name][1]
BCAST = 256


def unit_banks(w):
    for first, n in ((BR1, 4), (BR2, 6)):
        if first <= w < first + n:
            b = 2 * ((w - first) % 4)
            return (b, b + 1)
    return (w % 3,)


def build_evacuations():
    counts, done, last_in, before = {"act": 0, "dve": 0, "x1": 0, "x5": 0}, {}, {}, {}
    for w in [*range(FFN1), *range(WIN2, FFN2)]:
        if w == WIN2:
            last_in = {}
        on_dve = (BR1 <= w < FFN1 or BR2 <= w < FFN2
                  or WIN2 <= w < BR2 and IN2[w - WIN2][0] in ("cx", "cb"))
        e = "x1" if WO1 <= w < FFN1 else "x5" if WO2 <= w < FFN2 else "dve" if on_dve else "act"
        counts[e] += 1
        done[w] = (e, counts[e])
        before[w] = {last_in[b] for b in unit_banks(w) if b in last_in}
        for b in unit_banks(w):
            last_in[b] = w
    return done, before


EVACUATED, BANK_BEFORE = build_evacuations()


def item_spans(kind):
    return {"mem": [(1, 257), (257, 513)], "swa": [(0, 129), (129, 386)]}.get(kind, [(1, 129), (129, 385)])


def two_map_items(n):
    return n + 1 if n < 4 else n - 3


MOD_SLOTS = {4: 2, 16: 3}
MOD_PV = {2: 0, 3: 8}

MADE_IDENT, MADE_EPS, MADE_MATRICES, MADE_DIST, MADE_ALL = 2, 3, 9, 11, 18


def two_blocks(nc, t, out):
    ctx = ExitStack()
    with ctx:
        base = [(nc.sbuf_base + 63) // 64 * 64]

        def place(name, shape, dt, at=None):
            n = int(np.prod(shape[1:])) * 4
            where = base[0] if at is None else at
            if at is None:
                base[0] += (n + 63) // 64 * 64
            return nc.alloc_sbuf_tensor_at(name, shape, dt, offset=where), where

        raw, _ = place("raw", [P, RAW, UNIT], F32)
        whi, _ = place("whi", [P, SPLIT, UNIT], F32R)
        wlo, _ = place("wlo", [P, SPLIT, UNIT], F32R)
        x, _ = place("x", [P, KT, S], F32)
        hhi, _ = place("hhi", [P, KT, S], F32R)
        hlo, _ = place("hlo", [P, KT, S], F32R)
        proj, _ = place("proj", [P, 14, S], F32)
        vtok, _ = place("vtok", [P, NT, 640], F32)
        kmem, _ = place("kmem", [P, 4, S], F32)
        vmem, _ = place("vmem", [P, NT, 512], F32)
        yhi, y_at = place("yhi", [P, 12, S], F32R)
        ylo, ylo_at = place("ylo", [P, 12, S], F32R)
        probs, probs_at = place("probs", [P, 2, 514], F32)
        pt, pt_at = place("pt", [P, 2, 512], F32)
        dist_i, _ = place("dist_i", [P, 384], I32, at=pt_at)
        lam_in, _ = place("lam_in", [P, 4, HD], F32, at=pt_at + 2048)
        dist_swa, _ = place("dist_swa", [P, 384], F32)
        dist_diff, _ = place("dist_diff", [P, 384], F32)
        causal, _ = place("causal", [P, 384], F32)
        vec, _ = place("vec", [P, NV], F32)
        ident, _ = place("ident", [P, P], F32)
        mean_d, _ = place("mean_d", [P, P], F32)
        mean_128, _ = place("mean_128", [P, P], F32)
        mean_64, _ = place("mean_64", [P, P], F32)
        small, _ = place("small", [P, 256], F32)
        std, _ = place("std", [P, N_STAT], F32)
        rstd, _ = place("rstd", [P, N_STAT], F32)
        _, scratch_at = place("scratch", [P, 24, S], F32)
        ada = [place(f"ada{i}", [P, D], F32, at=a + 8 * S * 4)[0] for i, a in enumerate((y_at, ylo_at))]
        gate, _ = place("gate", [P, 24, S], F32, at=scratch_at)
        tmp, _ = place("tmp", [P, KT, S], F32, at=scratch_at + 16 * S * 4)
        conv_c, _ = place("conv_c", [P, 4, S], F32, at=scratch_at + 12 * S * 4)
        conv_t, _ = place("conv_t", [P, 4, S], F32, at=scratch_at + 8 * S * 4)
        conv_u, _ = place("conv_u", [P, 4, S + 2], F32, at=scratch_at + 19 * S * 4)
        sq_lo, _ = place("sq_lo", [P, KT, S], F32, at=scratch_at)
        sq_mid, _ = place("sq_mid", [P, KT, S], F32, at=scratch_at + 8 * S * 4)
        fa, _ = place("fa", [P, 2, 2, S + 2], F32, at=scratch_at)
        fc, _ = place("fc", [P, 2, 2 * S], F32, at=scratch_at + 5 * 1024)
        fg, _ = place("fg", [P, 2, 2 * S], F32, at=scratch_at + 9 * 1024)
        fp, _ = place("fp", [P, 2, 2 * S], F32, at=scratch_at + 13 * 1024)
        cw, _ = place("cw", [P, 2, 4, 2], F32)
        fhi, _ = place("fhi", [P, 2, 2 * S], F32R, at=y_at)
        flo, _ = place("flo", [P, 2, 2 * S], F32R, at=y_at + 4096)
        ps = ctx.enter_context(nc.psum_tensor("ps", [P, 8, 512], F32))

        def f32(ap):
            return ap.bitcast(F32)

        mg = proj
        QA, KA, QD, KD = 0, (4, 13), 5, 9
        Q2, K2, QM = 0, 4, 8
        mod = small[:, 0:48]
        gs1, gs2 = small[:, 48:56], small[:, 56:64]
        half_bg = small[:, 64:88]
        cs = small[:, 88:96]
        csig = small[:, 96:104]
        sinks = small[:, 104:112]
        nmax, rsum, rinv = small[:, 112:116], small[:, 116:120], small[:, 120:124]
        neglam = small[:, 124:125]
        lam_d, lam_e, lam_s = small[:, 126:128], small[:, 128:130], small[:, 130:131]
        gdiff, gmq, gmemq = small[:, 131:132], small[:, 132:133], small[:, 133:134]
        eps = small[:, 134:135]
        one, eps_root = small[:, 135:136], small[:, 140:141]
        rlam = small[:, 136:138]

        def col(name, i=0, n=1):
            c = COLUMN[name] + i
            return vec[:, c:c + n]

        sems = {}

        def sem(name):
            if name not in sems:
                sems[name] = ctx.enter_context(nc.semaphore(name))
            return sems[name]

        landed = [sem(f"raw_landed{i}") for i in range(RAW)]
        raw_done = sem("raw_done")
        hi_ready = sem("hi_ready")
        gemm_done = sem("gemm_done")
        emptied = {"act": sem("emptied_by_act"), "dve": sem("emptied_by_dve"),
                   "x1": sem("x1_ready"), "x5": sem("x5_ready")}

        def unit_source(w):
            for name, first in (("w_o_2", WO2), ("branches_2", BR2), ("w_in_2", WIN2), ("w_out", WO1),
                                ("branches", BR1), ("w_in", WIN1), ("w_mem_kv_2", MEMKV)):
                if w >= first:
                    return t[name][w - first]

        def ffn_source(f, kind, j):
            array = t[("w_down", "w_down_2")[f] if kind == "d" else ("w_up", "w_up_2")[f]]
            return array.rearrange("u p n -> p u n")[:, bass.ds(j + (FJ if kind == "g" else 0), 1), :]

        block = ctx.enter_context(nc.Block())

        FF = [FFN1, FFN2]

        @block.sync
        def _(sp):
            def load(r, src, it=0):
                if r >= RAW:
                    sp.wait_ge(raw_done, it * BODY + (r - RAW + 1))
                dst = raw[:, r % RAW:r % RAW + 1, :] if len(src.shape) == 3 else raw[:, r % RAW, :]
                sp.dma_start(dst, src).then_inc(landed[r % RAW], 16)

            for r, (kind, n) in enumerate(PLAN):
                f = 1 if n >= FFN2 else 0
                c = n - FF[f]
                if kind == "ada":
                    load(r, t["w_ada"][n])
                elif not 0 <= c < 3 * FJ:
                    load(r, unit_source(n))
                elif c < len(FFN_HEAD):
                    load(r, ffn_source(f, *FFN_HEAD[c]))
                elif c == len(FFN_HEAD):
                    with sp.Fori(0, FFN_LOOPS) as it:
                        for b, (kind_, j) in enumerate(FFN_BODY):
                            load(r + b, ffn_source(f, kind_, it * STEPS + j), it)
                elif c >= 3 * FJ - len(FFN_TAIL):
                    load(r, ffn_source(f, *FFN_TAIL[c - 3 * FJ]))
            for u in range(4):
                sp.wait_ge(sem("x6_ready"), u + 1)
                sp.dma_start(out[u], x[:, 2 * u:2 * u + 2, :].rearrange("p a b -> p (a b)")).then_inc(sem("stored"), 16)
            sp.wait_ge(sem("stored"), 16 * 4)

        @block.gpsimd
        def _(pool):
            n = 0

            def step(ins):
                nonlocal n
                n += 1
                ins.then_inc(sem("const_made"), 1)
                pool.wait_ge(sem("const_made"), n)

            step(nc.gpsimd.memset(ident[:, :], 0.0))
            step(nc.gpsimd.affine_select(out=ident[:, :], in_=ident[:, :], compare_op=ALU.not_equal, fill=1.0,
                                         base=0, pattern=[[-1, P]], channel_multiplier=1))
            step(nc.gpsimd.memset(eps, EPS))
            step(nc.gpsimd.memset(one, 1.0))
            step(nc.gpsimd.memset(mean_d[:, :], 1.0 / D))
            step(nc.gpsimd.memset(mean_128[:, :], 1.0 / 128))
            step(nc.gpsimd.memset(mean_64[:, :], 0.0))
            step(nc.gpsimd.memset(mean_64[0:64, 0:64], 1.0 / 64))
            step(nc.gpsimd.memset(mean_64[64:128, 64:128], 1.0 / 64))
            step(nc.gpsimd.iota(dist_i[:, 0:128], pattern=[[-1, 128]], base=0, channel_multiplier=1))
            step(nc.gpsimd.iota(dist_i[:, 128:384], pattern=[[-1, 256]], base=128, channel_multiplier=1))
            step(nc.gpsimd.memset(causal[:, :], 0.0))
            pool.wait_ge(sem("dist_float"), 1)
            for tile, fill in ((dist_diff, BIG), (causal, -BIG)):
                for c0, cn, b in ((0, 128, 0), (128, 256, 128)):
                    step(nc.gpsimd.affine_select(out=tile[:, c0:c0 + cn], in_=tile[:, c0:c0 + cn], compare_op=ALU.is_ge,
                                                 fill=fill, base=b, pattern=[[-1, cn]], channel_multiplier=1))
            step(nc.gpsimd.tensor_copy(dist_swa[:, 0:128], dist_diff[:, 0:128]))
            step(nc.gpsimd.affine_select(out=dist_swa[:, 128:384], in_=dist_diff[:, 128:384], compare_op=ALU.is_ge,
                                         fill=BIG, base=127 - 128, pattern=[[1, 256]], channel_multiplier=-1))
            assert n == MADE_ALL

        @block.scalar
        def _(act):
            act.dma_start(vec[:, :], t["vectors"]).then_inc(sem("vec_landed"), 16)
            act.dma_start(proj[:, 0:KT, :].rearrange("p a b -> p (a b)"), t["mem_2"]).then_inc(sem("mem_landed"), 16)
            act.dma_start(lam_in[:, :, :].rearrange("p a b -> p (a b)"),
                          t["diff_lambda"].rearrange("o a b -> o (a b)").to_broadcast([P, 4 * HD]))\
                .then_inc(sem("lam_landed"), 16)
            act.dma_start(sinks, t["swa_sinks"].to_broadcast([P, 8])).then_inc(sem("sinks_landed"), 16)
            act.dma_start(x[:, :, :].rearrange("p a b -> p (a b)"), t["x"]).then_inc(sem("x_landed"), 16)

            def copy(dst, src, func=ACT.Copy, **kw):
                return nc.scalar.activation(dst, src, func, **kw)

            def round_unit(w, it=0):
                if w >= NW:
                    return
                r = RAW_OF[("w", w)]
                act.wait_ge(landed[r % RAW], it * (16 * BODY // RAW) + 16 * (r // RAW + 1))
                if w >= SPLIT:
                    act.wait_ge(gemm_done, it * BODY + (w - SPLIT + 1))
                copy(whi[:, w % SPLIT, :], raw[:, r % RAW, :]).then_inc(hi_ready, 1)

            def square_all(src, dst, ready=None, first=0):
                for i in range(4):
                    if ready is not None:
                        act.wait_ge(ready, first + i + 1)
                    copy(dst[:, 2 * i:2 * i + 2, :], src[:, 2 * i:2 * i + 2, :], ACT.Square).then_inc(sem("sq_ready"), 1)

            def root(name, preload=False):
                if preload:
                    copy(eps_root, eps, ACT.Sqrt)
                (c, n), bank = STAT[name], NORMS[name][2]
                act.wait_ge(sem(f"{name}_mean"), 1)
                copy(std[:, c:c + n], ps[:, bank, 0:n], ACT.Sqrt, bias=eps).then_inc(sem(f"{name}_std"), 1)

            def round_h(k, shift=None):
                for c in range(KT):
                    act.wait_ge(sem("scaled_ready"), KT * k + c + 1)
                    if shift is None:
                        ins = copy(hhi[:, c, :], tmp[:, c, :])
                    else:
                        ins = copy(hhi[:, c, :], tmp[:, c, :], ACT.Identity, bias=shift[:, c:c + 1])
                    ins.then_inc(sem("hhi_ready"), 1)

            def empty(w, dst, src, func=ACT.Copy, **kw):
                act.wait_ge(gemm_done, w + 1)
                copy(dst, src, func, **kw).then_inc(emptied["act"], 1)

            def pair(bank):
                return bank.rearrange("p (a b) -> p a b", a=2)

            act.wait_ge(sem("vec_landed"), 16)
            copy(csig, col("c", n=8), ACT.Sigmoid).then_inc(sem("csig_ready"), 1)
            act.wait_ge(sem("lam_dots"), 2)
            copy(lam_e, lam_d, ACT.Exp).then_inc(sem("lam_exp"), 1)
            act.wait_ge(sem("mem_landed"), 16)
            square_all(proj, sq_mid)
            act.wait_ge(sem("const_made"), MADE_EPS)
            root("mem", preload=True)
            round_unit(0)
            round_h(0)
            act.wait_ge(sem("x_landed"), 16)
            square_all(x, sq_lo)
            round_unit(1)
            root("one")
            round_unit(2)
            for w in range(4):
                bank = ps[:, unit_banks(w)[0], :]
                if w == 0:
                    round_unit(3)
                if w == 3:
                    root("memk")
                    round_unit(4)
                if w < 2:
                    act.wait_ge(gemm_done, w + 1)
                    copy(sq_mid[:, 2 * w:2 * w + 2, :], pair(bank), ACT.Square).then_inc(sem("memk_sq"), 1)
                    empty(w, kmem[:, 2 * w:2 * w + 2, :], pair(bank))
                else:
                    empty(w, vmem[:, :, 256 * (w - 2):256 * (w - 2) + 256], pair(bank))
            round_h(1)
            round_unit(5)
            round_unit(6)

            def exps(item):
                kind, i = item
                n = ITEM_NO[item]
                act.wait_ge(sem("max_ready"), n + 1)
                for m in range(2):
                    for q, (a, b) in enumerate(item_spans(kind)):
                        src = ps[:, SCORE_BANK + m, a - 1:b - 1] if kind == "mem" else probs[:, m, a:b]
                        c = 2 * m + q
                        ins = copy(probs[:, m, a:b], src, ACT.Exp, bias=nmax[:, c:c + 1], accum_out=rsum[:, c:c + 1])
                ins.then_inc(sem("exp_done"), 1)

            def empty_pt(item):
                act.wait_ge(sem("pt_done"), ITEM_NO[item] + 1)
                w = 512 if item[0] == "mem" else 384
                copy(pt[:, 0, 0:w], ps[:, PT_BANKS[0], 0:w]).then_inc(sem("pt0_ready"), 1)

            def empty_pv(item):
                kind, i = item
                act.wait_ge(sem("pv_done"), ITEM_NO[item] + 1)
                if kind == "diff":
                    copy(proj[:, KD + i, :], ps[:, PV_BANK, 0:S], ACT.Square)
                    ins = copy(proj[:, QD + i, :], ps[:, PV_BANK, 0:S])
                elif kind == "mem":
                    ins = copy(yhi[:, 8 + 2 * i:10 + 2 * i, :], pair(ps[:, PV_BANK, :]))
                else:
                    ins = copy(yhi[:, Y_TILE[kind] + i, :], ps[:, PV_BANK, 0:S])
                ins.then_inc(sem("yhi_ready"), 1)

            def attention(items, s):
                if s - 2 in items:
                    empty_pv(items[s - 2])
                if s - 1 in items:
                    empty_pt(items[s - 1])
                if s in items:
                    exps(items[s])

            for s in range(18):
                round_unit(WIN1 + s + AHEAD)
                if s >= 1:
                    w, k = WIN1 + s - 1, s - 1
                    kind, bank = IN1[k], ps[:, unit_banks(w)[0], :]
                    if kind == "qa":
                        empty(w, proj[:, QA + 2 * k:QA + 2 * k + 2, :], pair(bank), scale=HD ** -0.5)
                    elif kind == "kava":
                        act.wait_ge(gemm_done, w + 1)
                        copy(proj[:, KA[0], :], bank[:, 0:S])
                        copy(proj[0:64, KA[1], :], bank[64:128, 0:S])
                        copy(proj[64:128, KA[1], :], bank[0:64, 0:S])
                        empty(w, vtok[:, :, 512:640], pair(bank[:, S:2 * S]))
                    elif kind == "qd":
                        c = QD + 2 * (k - 3)
                        empty(w, proj[:, c:c + 2, :], pair(bank), scale=HD ** -0.5)
                    elif kind == "kd":
                        c = KD + 2 * (k - 5)
                        empty(w, proj[:, c:c + 2, :], pair(bank))
                    elif kind == "vd":
                        c = 256 * (k - 7)
                        empty(w, vtok[:, :, c:c + 256], pair(bank))
                    else:
                        empty(w, gate[:, 2 * (k - 9):2 * (k - 9) + 2, :], pair(bank), ACT.Tanh, scale=0.5)
                attention(ITEMS1, s)
                if s == 14:
                    root("diff")
                if s == 15:
                    for i in range(2):
                        act.wait_ge(sem("diff_out"), i + 1)
                        copy(yhi[:, 4 + 2 * i:6 + 2 * i, :], proj[:, QD + 2 * i:QD + 2 * i + 2, :])\
                            .then_inc(sem("ydhi_ready"), 1)

            def merge_and_project(b0, nbr, o0, k, start):
                for u in range(2 * nbr):
                    if u >= start:
                        round_unit(b0 + u + AHEAD)
                    if u >= 1 and u % nbr == 0:
                        round_merged(k, 0)
                round_unit(o0 + AHEAD)
                round_merged(k, 1)
                for u in range(1, 4):
                    round_unit(o0 + u + AHEAD)

            def round_merged(k, half):
                for i in range(2):
                    act.wait_ge(sem("merged"), 4 * k + 2 * half + i + 1)
                    c = 4 * half + 2 * i
                    copy(hhi[:, c:c + 2, :], mg[:, c:c + 2, :], scale=0.5).then_inc(sem("mghi_ready"), 1)

            merge_and_project(BR1, 2, WO1, 0, 1)
            square_all(x, mg, sem("x1_ready"))
            root("two", preload=True)
            act.wait_ge(sem("mods_ready"), 4)
            round_h(2, shift=mod[:, 24:32])

            def ffn(f):
                w0 = FF[f]
                func = (ACT.Gelu, ACT.Silu)[f]

                def pad_a(c, j, b, it=0):
                    act.wait_ge(gemm_done, it * BODY + (w0 + c + 1))
                    if j >= 2:
                        act.wait_ge(sem(f"conv_done{f}"), it * STEPS + (j - 1))
                    else:
                        act.wait_ge(sem(f"pads_ready"), f + 1)
                    copy(fa[:, b, :, 2:S + 2], pair(ps[:, (0, 2)[b], :])).then_inc(sem(f"a_ready{f}"), 1)

                def activate(j, b, it=0):
                    act.wait_ge(sem(f"conv_done{f}"), it * STEPS + (j + 1))
                    if j >= 2:
                        act.wait_ge(sem(f"glu_done{f}"), it * STEPS + (j - 1))
                    copy(fg[:, b, :], fc[:, b, :], func).then_inc(sem(f"act_done{f}"), 1)

                def round_product(j, b, it=0):
                    act.wait_ge(sem(f"glu_done{f}"), it * STEPS + (j + 1))
                    if j >= 2:
                        act.wait_ge(gemm_done, it * BODY + (w0 + 3 * j - 1))
                    copy(fhi[:, b, :], fp[:, b, :]).then_inc(sem(f"fhi_ready{f}"), 1)

                def slot(c, kind, j, it=0):
                    round_unit(w0 + c + AHEAD, it)
                    if kind == "g":
                        pad_a(c - 1, j, j % 2, it)
                    if kind == "d" and j + 1 < FJ or kind == "a" and c == 2:
                        k = j + 1 if kind == "d" else 0
                        activate(k, k % 2, it)
                        round_product(k, k % 2, it)

                for c, (kind, j) in enumerate(FFN_HEAD):
                    slot(c, kind, j)
                with act.Fori(0, FFN_LOOPS) as it:
                    for c, (kind, j) in enumerate(FFN_BODY):
                        slot(len(FFN_HEAD) + c, kind, j, it)
                for c, (kind, j) in enumerate(FFN_TAIL):
                    slot(3 * FJ - len(FFN_TAIL) + c, kind, j)

            ffn(0)
            square_all(x, mg, sem("x2_ready"))
            root("final", preload=True)
            square_all(x, mg, sem("x3_ready"))
            root("mix")
            round_h(3)

            for s in range(27):
                round_unit(WIN2 + s + AHEAD)
                if s >= 1:
                    w, k = WIN2 + s - 1, s - 1
                    kind, bank = IN2[k][0], ps[:, unit_banks(w)[0], :]
                    if kind in ("q", "k"):
                        act.wait_ge(gemm_done, w + 1)
                        copy(tmp[:, 2 * k:2 * k + 2, :], pair(bank), ACT.Square).then_inc(sem("qk_sq"), 1)
                        empty(w, proj[:, 2 * k:2 * k + 2, :], pair(bank))
                    elif kind == "v":
                        empty(w, vtok[:, :, 256 * (k - 4):256 * (k - 4) + 256], pair(bank))
                    elif kind == "qm":
                        c = 2 * (k - 6)
                        act.wait_ge(gemm_done, w + 1)
                        copy(conv_t[:, c:c + 2, :], pair(bank), ACT.Square).then_inc(sem("qm_sq"), 1)
                        empty(w, proj[:, QM + c:QM + c + 2, :], pair(bank))
                    elif kind == "cc":
                        c = 2 * (k - 8)
                        empty(w, conv_c[:, c:c + 2, :], pair(bank))
                    elif kind == "g":
                        act.wait_ge(gemm_done, w + 1)
                        g = 2 * (k - 14)
                        copy(gate[:, g, :], bank[:, 0:S], ACT.Tanh, scale=0.5, bias=half_bg[:, g:g + 1])
                        empty(w, gate[:, g + 1, :], bank[:, S:2 * S], ACT.Tanh, scale=0.5, bias=half_bg[:, g + 1:g + 2])
                attention(ITEMS2, s)
                if s == 5:
                    root("qk")
                if s == 9:
                    root("qm")
                if s in (14, 15):
                    i = s - 14
                    act.wait_ge(emptied["dve"], EVACUATED[WIN2 + 12 + i][1])
                    copy(yhi[:, 2 * i:2 * i + 2, :], conv_t[:, 2 * i:2 * i + 2, :]).then_inc(sem("ychi_ready"), 1)
            merge_and_project(BR2, 3, WO2, 1, 1)
            square_all(x, mg, sem("x5_ready"))
            root("ffn2", preload=True)
            round_h(4)
            ffn(1)

        @block.vector
        def _(dve):
            V = nc.vector
            link_n = 0

            def link(ins):
                nonlocal link_n
                link_n += 1
                ins.then_inc(sem("dve_step"), 1)
                dve.wait_ge(sem("dve_step"), link_n)

            def pair(bank):
                return bank.rearrange("p (a b) -> p a b", a=2)

            def fold_ada(a):
                r, m, k = RAW_OF[("ada", a)], a // 4, a % 4
                acc = ada[m % 2]
                if k == 0 and m >= 2:
                    dve.wait_ge(sem("mod_done"), m - 1)
                dve.wait_ge(landed[r % RAW], 16 * (r // RAW + 1))
                src = raw[:, r % RAW, :].rearrange("p (a b) -> p a b", a=2)
                if k:
                    dve.wait_ge(raw_done, RAW_OF[("ada", a - 1)] + 1)
                    link(V.scalar_tensor_tensor(out=acc[:, :], in0=src[:, 0, :], scalar=cs[:, 2 * k:2 * k + 1],
                                                in1=acc[:, :], op0=ALU.mult, op1=ALU.add))
                else:
                    link(V.tensor_scalar(acc[:, :], src[:, 0, :], cs[:, 0:1], None, ALU.mult))
                V.scalar_tensor_tensor(out=acc[:, :], in0=src[:, 1, :], scalar=cs[:, 2 * k + 1:2 * k + 2],
                                       in1=acc[:, :], op0=ALU.mult, op1=ALU.add).then_inc(raw_done, 1)

            def split_low(w, it=0):
                if w >= NW:
                    return
                r = RAW_OF[("w", w)]
                dve.wait_ge(hi_ready, it * BODY + (w + 1))
                if w >= SPLIT:
                    dve.wait_ge(gemm_done, it * BODY + (w - SPLIT + 1))
                V.tensor_tensor(wlo[:, w % SPLIT, :], raw[:, r % RAW, :], f32(whi[:, w % SPLIT, :]),
                                ALU.subtract).then_inc(raw_done, 1)
                r += 1
                while r < len(PLAN) and PLAN[r][0] == "ada":
                    fold_ada(PLAN[r][1])
                    r += 1

            def mods(m):
                dve.wait_ge(sem("mod_done"), m + 1)
                V.tensor_tensor(mod[:, 8 * m:8 * m + 8], ps[:, 7, MOD_COL + 8 * m:MOD_COL + 8 * m + 8],
                                col("b_ada", 8 * m, 8), ALU.add).then_inc(sem("mods_ready"), 1)
                dve.wait_ge(sem("mods_ready"), m + 1)

            def gains(dst, m, name):
                link(V.scalar_tensor_tensor(out=dst, in0=mod[:, 8 * m:8 * m + 8], scalar=1.0, in1=col(name, n=8),
                                            op0=ALU.add, op1=ALU.mult))

            def invert(name):
                c, n = STAT[name]
                dve.wait_ge(sem(f"{name}_std"), 1)
                V.reciprocal(rstd[:, c:c + n], std[:, c:c + n]).then_inc(sem(f"{name}_rstd"), 1)

            def spread(name, i=0):
                dve.wait_ge(sem(f"{name}_spread"), 1)
                _, heads, _, bank = NORMS[name]
                return pair(ps[:, bank + i, :]) if heads else ps[:, bank, BCAST:BCAST + S]

            def norm_h(k, scaled, shift=None):
                for c in range(KT + 2):
                    if c < KT:
                        scaled(c).then_inc(sem("scaled_ready"), 1)
                    if c >= 2:
                        e = c - 2
                        dve.wait_ge(sem("hhi_ready"), KT * k + e + 1)
                        if shift is None:
                            ins = V.tensor_tensor(hlo[:, e, :], tmp[:, e, :], f32(hhi[:, e, :]), ALU.subtract)
                        else:
                            ins = V.scalar_tensor_tensor(out=hlo[:, e, :], in0=tmp[:, e, :], scalar=shift[:, e:e + 1],
                                                         in1=f32(hhi[:, e, :]), op0=ALU.add, op1=ALU.subtract)
                        ins.then_inc(sem("hlo_ready"), 1)

            def norm_wide(k, name, src, gcol, shift=None):
                invert(name)
                r = spread(name)
                norm_h(k, lambda c: V.scalar_tensor_tensor(out=tmp[:, c, :], in0=src[:, c, :], scalar=gcol(c), in1=r,
                                                           op0=ALU.mult, op1=ALU.mult), shift)

            dve.wait_ge(sem("lam_landed"), 16)
            for i in range(2):
                V.tensor_tensor_reduce(out=lam_in[:, 2 * i, :], in0=lam_in[:, 2 * i, :], in1=lam_in[:, 2 * i + 1, :],
                                       scale=1.0, scalar=0.0, op0=ALU.mult, op1=ALU.add,
                                       accum_out=lam_d[:, i:i + 1]).then_inc(sem("lam_dots"), 1)
            dve.wait_ge(sem("vec_landed"), 16)
            dve.wait_ge(sem("csig_ready"), 1)
            V.tensor_scalar(gdiff, col("diff_subln_g"), 1.0 - LAM_INIT, None, ALU.mult)
            V.tensor_scalar(gmq, col("moba_q_gain_2"), HD ** -0.5, None, ALU.mult)
            V.tensor_scalar(gmemq, col("memq_gain_2"), P ** -0.5, None, ALU.mult)
            V.tensor_scalar(half_bg, col("b_gate_2", n=24), 0.5, None, ALU.mult)
            link(V.tensor_tensor(cs, col("c", n=8), csig, ALU.mult))
            fold_ada(0)
            dve.wait_ge(sem("const_made"), MADE_DIST)
            V.tensor_copy(dist_diff[:, :], dist_i[:, :]).then_inc(sem("dist_float"), 1)
            dve.wait_ge(sem("lam_exp"), 1)
            link(V.tensor_tensor(lam_s, lam_e[:, 0:1], lam_e[:, 1:2], ALU.subtract))
            link(V.tensor_scalar(neglam, lam_s, LAM_INIT, -1.0, ALU.add, ALU.mult))

            norm_wide(0, "mem", proj, lambda c: col("g_mem_2", c))
            fold_ada(1)
            split_low(0)
            split_low(1)
            invert("one")
            split_low(2)
            r = spread("one")
            for c in range(KT):
                ins = V.tensor_tensor(tmp[:, c, :], x[:, c, :], r, ALU.mult)
            link(ins)
            mods(0)
            split_low(3)
            invert("memk")
            split_low(4)
            mods(1)
            gains(gs1, 1, "norm1_g")
            norm_h(1, lambda c: V.tensor_scalar(tmp[:, c, :], tmp[:, c, :], gs1[:, c:c + 1], mod[:, c:c + 1],
                                                ALU.mult, ALU.add))
            split_low(5)
            for i in range(2):
                r = spread("memk", i)
                dve.wait_ge(emptied["act"], i + 1)
                V.scalar_tensor_tensor(out=kmem[:, 2 * i:2 * i + 2, :], in0=kmem[:, 2 * i:2 * i + 2, :],
                                       scalar=col("memk_gain_2"), in1=r,
                                       op0=ALU.mult, op1=ALU.mult).then_inc(sem("kmem_ready"), 1)
            split_low(6)

            def scores(item):
                kind, i = item
                n = ITEM_NO[item]
                if kind == "mem":
                    dve.wait_ge(sem("scores_done"), n + 1)
                else:
                    if n:
                        dve.wait_ge(sem("pt_done"), n)
                    if n == 0:
                        dve.wait_ge(sem("sinks_landed"), 16)
                    if kind == "swa":
                        for m in range(2):
                            V.tensor_copy(probs[:, m, 0:386:385],
                                          sinks[:, 2 * i + m:2 * i + m + 1].to_broadcast([P, 2]))
                    dve.wait_ge(sem("scores_done"), n + 1)
                    if n == 0:
                        dve.wait_ge(sem("const_made"), MADE_ALL)
                    for m in range(2):
                        slope = {"swa": 2.0 ** -(2 * i + m + 1), "diff": 2.0 ** (-2 * (i + 1)), "moba": -1.0}[kind]
                        dist = {"swa": dist_swa, "diff": dist_diff, "moba": causal}[kind]
                        ins = V.scalar_tensor_tensor(out=probs[:, m, 1:385], in0=dist[:, :], scalar=-slope,
                                                     in1=ps[:, SCORE_BANK + m, 0:384], op0=ALU.mult, op1=ALU.add)
                    link(ins)
                for q, (a, b) in enumerate(item_spans(kind)):
                    src = ps[:, SCORE_BANK:SCORE_BANK + 2, a - 1:b - 1] if kind == "mem" else probs[:, :, a:b]
                    ins = V.tensor_reduce(nmax[:, q:4:2], src, AX_X, ALU.max, negate=True)
                ins.then_inc(sem("max_ready"), 1)

            def normalise(item):
                kind, i = item
                dve.wait_ge(sem("exp_done"), ITEM_NO[item] + 1)
                link(V.reciprocal(rinv, rsum))
                spans = [(1, 257), (257, 513)] if kind == "mem" else [(1, 129), (129, 385)]
                if kind == "diff":
                    link(V.tensor_scalar(rlam, rinv[:, 2:4], neglam, None, ALU.mult))
                    for q, (a, b) in enumerate(spans):
                        ins = V.tensor_scalar(probs[:, 1, a:b], probs[:, 1, a:b], rlam[:, q:q + 1], None, ALU.mult)
                    link(ins)
                    for q, (a, b) in enumerate(spans):
                        ins = V.scalar_tensor_tensor(out=probs[:, 0, a:b], in0=probs[:, 0, a:b], scalar=rinv[:, q:q + 1],
                                                     in1=probs[:, 1, a:b], op0=ALU.mult, op1=ALU.add)
                else:
                    for m in range(2):
                        for q, (a, b) in enumerate(spans):
                            c = 2 * m + q
                            ins = V.tensor_scalar(probs[:, m, a:b], probs[:, m, a:b], rinv[:, c:c + 1], None, ALU.mult)
                ins.then_inc(sem("probs_ready"), 1)

            def empty_pt(item):
                if item[0] == "diff":
                    return
                dve.wait_ge(sem("pt_done"), ITEM_NO[item] + 1)
                w = 512 if item[0] == "mem" else 384
                V.tensor_copy(pt[:, 1, 0:w], ps[:, PT_BANKS[1], 0:w]).then_inc(sem("pt1_ready"), 1)

            def low_pv(item):
                kind, i = item
                if kind == "diff":
                    return
                dve.wait_ge(sem("yhi_ready"), ITEM_NO[item] + 1)
                if kind == "mem":
                    c = slice(8 + 2 * i, 10 + 2 * i)
                    ins = V.tensor_tensor(ylo[:, c, :], pair(ps[:, PV_BANK, :]), f32(yhi[:, c, :]), ALU.subtract)
                else:
                    c = Y_TILE[kind] + i
                    ins = V.tensor_tensor(ylo[:, c, :], ps[:, PV_BANK, 0:S], f32(yhi[:, c, :]), ALU.subtract)
                ins.then_inc(sem("ylo_ready"), 1)

            def attention(items, s):
                if s - 1 in items:
                    empty_pt(items[s - 1])
                if s in items:
                    scores(items[s])
                    normalise(items[s])

            for s in range(18):
                split_low(WIN1 + s + AHEAD)
                if s - 2 in ITEMS1:
                    low_pv(ITEMS1[s - 2])
                if s in MOD_SLOTS:
                    mods(MOD_SLOTS[s])
                attention(ITEMS1, s)
                if s == 14:
                    invert("diff")
                if s == 15:
                    for i in range(2):
                        r = spread("diff", i)
                        c = slice(QD + 2 * i, QD + 2 * i + 2)
                        V.scalar_tensor_tensor(out=proj[:, c, :], in0=proj[:, c, :], scalar=gdiff, in1=r,
                                               op0=ALU.mult, op1=ALU.mult).then_inc(sem("diff_out"), 1)
                if s == 16:
                    for i in range(2):
                        dve.wait_ge(sem("ydhi_ready"), i + 1)
                        c = slice(4 + 2 * i, 6 + 2 * i)
                        V.tensor_tensor(ylo[:, c, :], proj[:, QD + 2 * i:QD + 2 * i + 2, :], f32(yhi[:, c, :]),
                                        ALU.subtract).then_inc(sem("ydlo_ready"), 1)

            def merge(w, b, nbr, k):
                r, half = b % nbr, b // nbr
                dve.wait_ge(gemm_done, w + 1)
                for i, bank in enumerate(unit_banks(w)):
                    c = 4 * half + 2 * i
                    g = gate[:, KT * r + c:KT * r + c + 2, :]
                    if r == 0:
                        ins = V.scalar_tensor_tensor(out=mg[:, c:c + 2, :], in0=g, scalar=1.0, in1=pair(ps[:, bank, :]),
                                                     op0=ALU.add, op1=ALU.mult)
                        if i == 1:
                            ins.then_inc(emptied["dve"], 1)
                    else:
                        term = pair(probs[:, i, 0:512])
                        ins = V.scalar_tensor_tensor(out=term, in0=g, scalar=1.0, in1=pair(ps[:, bank, :]),
                                                     op0=ALU.add, op1=ALU.mult)
                        if i == 1:
                            ins.then_inc(emptied["dve"], 1)
                            dve.wait_ge(emptied["dve"], EVACUATED[w][1])
                        else:
                            link(ins)
                        ins = V.tensor_tensor(mg[:, c:c + 2, :], mg[:, c:c + 2, :], term, ALU.add)
                        if r == nbr - 1:
                            ins.then_inc(sem("merged"), 1)
                            dve.wait_ge(sem("merged"), 4 * k + 2 * half + i + 1)
                        else:
                            link(ins)

            def low_merged(k, half):
                for i in range(2):
                    dve.wait_ge(sem("mghi_ready"), 4 * k + 2 * half + i + 1)
                    c = slice(4 * half + 2 * i, 4 * half + 2 * i + 2)
                    V.scalar_tensor_tensor(out=hlo[:, c, :], in0=mg[:, c, :], scalar=0.5, in1=f32(hhi[:, c, :]),
                                           op0=ALU.mult, op1=ALU.subtract).then_inc(sem("mglo_ready"), 1)

            def merge_all(b0, nbr, o0, k, start):
                for u in range(2 * nbr):
                    if u >= start:
                        split_low(b0 + u + AHEAD)
                    if u >= 1:
                        merge(b0 + u - 1, u - 1, nbr, k)
                        if u % nbr == 0:
                            low_merged(k, 0)
                split_low(o0 + AHEAD)
                merge(b0 + 2 * nbr - 1, 2 * nbr - 1, nbr, k)
                low_merged(k, 1)

            merge_all(BR1, 2, WO1, 0, 1)
            for u in range(4):
                w = WO1 + u
                if u:
                    split_low(w + AHEAD)
                dve.wait_ge(gemm_done, w + 1)
                bank = ps[:, unit_banks(w)[0], :]
                for i in range(2):
                    c = 2 * u + i
                    ins = V.scalar_tensor_tensor(out=x[:, c, :], in0=bank[:, S * i:S * i + S],
                                                 scalar=mod[:, 16 + c:17 + c], in1=x[:, c, :], op0=ALU.mult, op1=ALU.add)
                ins.then_inc(sem("x1_ready"), 1)
                if u == 0:
                    mods(4)
                    gains(gs2, 4, "norm2_g")
            norm_wide(2, "two", x, lambda c: gs2[:, c:c + 1], shift=mod[:, 24:32])

            def ffn(f):
                w0 = FF[f]
                table = col(("conv_w", "ffn_conv_w_2")[f], n=88).rearrange("p (a b) -> p a b", b=22)
                conv_step = sem(f"conv_step{f}")
                V.memset(fa[:, :, :, 0:2].rearrange("p a b c -> p (a b) c"), 0.0).then_inc(sem("pads_ready"), 1)
                dve.wait_ge(sem("pads_ready"), f + 1)

                def convolve(j, b, it=0):
                    n = 5 * (it * STEPS + j)
                    if j >= 2:
                        dve.wait_ge(sem(f"act_done{f}"), it * STEPS + (j - 1))
                    V.tensor_copy(cw[:, b, :, :], table[:, :, bass.ds(it * 2 * STEPS + 2 * j, 2)]).then_inc(conv_step, 1)
                    dve.wait_ge(sem(f"a_ready{f}"), it * STEPS + (j + 1))
                    dve.wait_ge(conv_step, n + 1)
                    for tap in range(3):
                        for c in range(2):
                            dst = fc[:, b, S * c:S * c + S]
                            src = fa[:, b, c, tap:tap + S]
                            if tap == 0:
                                V.tensor_scalar(dst, src, cw[:, b, 0, c:c + 1], cw[:, b, 3, c:c + 1],
                                                ALU.mult, ALU.add).then_inc(conv_step, 1)
                                continue
                            dve.wait_ge(conv_step, n + 2 * tap + c)
                            ins = V.scalar_tensor_tensor(out=dst, in0=src, scalar=cw[:, b, tap, c:c + 1], in1=dst,
                                                         op0=ALU.mult, op1=ALU.add)
                            if tap == 1:
                                ins.then_inc(conv_step, 1)
                    ins.then_inc(sem(f"conv_done{f}"), 1)

                def gate_it(c, j, b, it=0):
                    dve.wait_ge(sem(f"act_done{f}"), it * STEPS + (j + 1))
                    dve.wait_ge(gemm_done, it * BODY + (w0 + c + 1))
                    V.tensor_tensor(fp[:, b, :], fg[:, b, :], ps[:, (1, 3)[b], :], ALU.mult)\
                        .then_inc(sem(f"glu_done{f}"), 1)
                    dve.wait_ge(sem(f"fhi_ready{f}"), it * STEPS + (j + 1))
                    V.tensor_tensor(flo[:, b, :], fp[:, b, :], f32(fhi[:, b, :]), ALU.subtract)\
                        .then_inc(sem(f"flo_ready{f}"), 1)

                def slot(c, kind, j, it=0):
                    if f == 0 and c == 3:
                        mods(5)
                    split_low(w0 + c + AHEAD, it)
                    if kind == "g":
                        convolve(j, j % 2, it)
                    if kind == "d" and j + 1 < FJ or kind == "a" and c == 2:
                        k = j + 1 if kind == "d" else 0
                        gate_it(3 * k if k else 1, k, k % 2, it)

                for c, (kind, j) in enumerate(FFN_HEAD):
                    slot(c, kind, j)
                with dve.Fori(0, FFN_LOOPS) as it:
                    for c, (kind, j) in enumerate(FFN_BODY):
                        slot(len(FFN_HEAD) + c, kind, j, it)
                for c, (kind, j) in enumerate(FFN_TAIL):
                    slot(3 * FJ - len(FFN_TAIL) + c, kind, j)
                dve.wait_ge(gemm_done, w0 + 3 * FJ)

            ffn(0)
            for u in range(4):
                for i in range(2):
                    c = 2 * u + i
                    ins = V.scalar_tensor_tensor(out=x[:, c, :], in0=ps[:, 4 + u, S * i:S * i + S],
                                                 scalar=mod[:, 40 + c:41 + c], in1=x[:, c, :], op0=ALU.mult, op1=ALU.add)
                ins.then_inc(sem("x2_ready"), 1)
            invert("final")
            r = spread("final")
            for c in range(KT):
                ins = V.scalar_tensor_tensor(out=x[:, c, :], in0=x[:, c, :], scalar=col("final_g", c), in1=r,
                                             op0=ALU.mult, op1=ALU.mult)
                if c % 2:
                    ins.then_inc(sem("x3_ready"), 1)
            norm_wide(3, "mix", x, lambda c: col("g_mix_2", c))

            for s in range(27):
                split_low(WIN2 + s + AHEAD)
                if s == 5:
                    invert("qk")
                if s == 6:
                    for i in range(4):
                        r = spread("qk", i)
                        c = slice(2 * i, 2 * i + 2)
                        V.scalar_tensor_tensor(out=proj[:, c, :], in0=proj[:, c, :],
                                               scalar=gmq if i < 2 else col("moba_k_gain_2"), in1=r,
                                               op0=ALU.mult, op1=ALU.mult).then_inc(sem("qk_ready"), 1)
                    link(V.memset(conv_u[:, :, 0:2], 0.0))
                if s == 9:
                    invert("qm")
                if s == 10:
                    for i in range(2):
                        r = spread("qm", i)
                        c = slice(QM + 2 * i, QM + 2 * i + 2)
                        V.scalar_tensor_tensor(out=proj[:, c, :], in0=proj[:, c, :], scalar=gmemq, in1=r,
                                               op0=ALU.mult, op1=ALU.mult).then_inc(sem("qm_ready"), 1)
                w, k = WIN2 + s - 1, s - 1
                kind = IN2[k][0] if s else ""
                if kind in ("cx", "cb"):
                    dve.wait_ge(gemm_done, w + 1)
                    bank = pair(ps[:, unit_banks(w)[0], :])
                if kind == "cx":
                    c = slice(2 * (k - 10), 2 * (k - 10) + 2)
                    dve.wait_ge(emptied["act"], EVACUATED[WIN2 + 8 + (k - 10)][1])
                    V.tensor_tensor(conv_u[:, c, 2:S + 2], conv_c[:, c, :], bank, ALU.mult).then_inc(emptied["dve"], 1)
                if kind == "cb":
                    h = k - 12
                    dve.wait_ge(emptied["dve"], EVACUATED[w - 2][1])
                    for tap in range(3):
                        for i in range(2):
                            c = 2 * h + i
                            src, wt = conv_u[:, c, tap:tap + S], col("conv_w_2", 4 * tap + c)
                            if tap == 0:
                                ins = V.tensor_scalar(conv_t[:, c, :], src, wt, col("conv_b_2", c), ALU.mult, ALU.add)
                            else:
                                ins = V.scalar_tensor_tensor(out=conv_t[:, c, :], in0=src, scalar=wt, in1=conv_t[:, c, :],
                                                             op0=ALU.mult, op1=ALU.add)
                        link(ins)
                    c = slice(2 * h, 2 * h + 2)
                    V.tensor_tensor(conv_t[:, c, :], conv_t[:, c, :], bank, ALU.mult).then_inc(emptied["dve"], 1)
                if s - 2 in ITEMS2:
                    low_pv(ITEMS2[s - 2])
                attention(ITEMS2, s)
                if s in (14, 15):
                    i = s - 14
                    dve.wait_ge(sem("ychi_ready"), i + 1)
                    c = slice(2 * i, 2 * i + 2)
                    V.tensor_tensor(ylo[:, c, :], conv_t[:, c, :], f32(yhi[:, c, :]), ALU.subtract)\
                        .then_inc(sem("yclo_ready"), 1)
            merge_all(BR2, 3, WO2, 1, 1)
            for u in range(4):
                w = WO2 + u
                if u:
                    split_low(w + AHEAD)
                dve.wait_ge(gemm_done, w + 1)
                V.tensor_tensor(x[:, 2 * u:2 * u + 2, :], x[:, 2 * u:2 * u + 2, :], pair(ps[:, unit_banks(w)[0], :]),
                                ALU.add).then_inc(sem("x5_ready"), 1)
            norm_wide(4, "ffn2", x, lambda c: col("g_ffn_2", c))
            ffn(1)
            for u in range(4):
                V.tensor_tensor(x[:, 2 * u:2 * u + 2, :], x[:, 2 * u:2 * u + 2, :], pair(ps[:, 4 + u, :]),
                                ALU.add).then_inc(sem("x6_ready"), 1)

        @block.tensor
        def _(pe):
            mm = nc.tensor.matmul

            def three(out_, whi_, wlo_, ahi, alo, start, stop, weights_move=False, **kw):
                terms = [(whi_, ahi), (whi_, alo), (wlo_, ahi)]
                for i, (w_, a_) in enumerate(terms):
                    l, r = (a_, w_) if weights_move else (w_, a_)
                    ins = mm(out_, l, r, start=start and i == 0, stop=stop and i == 2, **kw)
                return ins

            def begin(w):
                pe.wait_ge(raw_done, RAW_OF[("w", w)] + 1)
                for v in sorted(BANK_BEFORE.get(w, ())):
                    e, n = EVACUATED[v]
                    pe.wait_ge(emptied[e], n)

            def wt(ring, w, kt, c, n, width):
                return ring[:, w % SPLIT, kt * width + c:kt * width + c + n]

            def channels(w, i, width, ah, al, kts, ready=None, last=False, bank=None, it=0):
                b = unit_banks(w)[i // 2] if bank is None else bank
                for kt in range(kts):
                    if ready is not None:
                        pe.wait_ge(ready[0], ready[1] + kt + 1)
                    ins = three(ps[:, b, S * (i % 2):S * (i % 2) + S], wt(whi, w, kt, P * i, P, width),
                                wt(wlo, w, kt, P * i, P, width), ah[:, kt, :], al[:, kt, :], kt == 0, kt == kts - 1)
                if last:
                    ins.then_inc(gemm_done, 1)

            def positions(w, tt, c, n, out_, last=False):
                for kt in range(KT):
                    ins = three(out_, wt(whi, w, kt, c, n, 256), wt(wlo, w, kt, c, n, 256),
                                hhi[:, kt, P * tt:P * tt + P], hlo[:, kt, P * tt:P * tt + P], kt == 0, kt == KT - 1,
                                weights_move=True)
                if last:
                    ins.then_inc(gemm_done, 1)

            def both_channels(w, ready, bank=None):
                b = unit_banks(w)[0] if bank is None else bank
                for kt in range(KT):
                    pe.wait_ge(ready[0], ready[1] + (kt // ready[2]) + 1)
                    for i in range(2):
                        for n, (w_, a_) in enumerate(((whi, hhi), (whi, hlo), (wlo, hhi))):
                            ins = mm(ps[:, b, S * i:S * i + S], wt(w_, w, kt, P * i, P, 256), a_[:, kt, :],
                                     start=kt == 0 and i == 0 and n == 0, stop=kt == KT - 1 and n == 2,
                                     skip_group_check=True)
                ins.then_inc(gemm_done, 1)

            def statistics(name, src, ready):
                tiles, heads, bank, _ = NORMS[name]
                mean = mean_64[:, 0:P:64] if heads == 2 else (mean_128 if heads else mean_d)[:, 0:1]
                for c in range(tiles):
                    if c % 2 == 0:
                        pe.wait_ge(ready[0], ready[1] + c // 2 + 1)
                    for tt in range(NT):
                        if heads:
                            at = (c * NT + tt) * heads
                            ins = mm(ps[:, bank, at:at + heads], src[:, c, P * tt:P * tt + P], mean, start=True, stop=True)
                        else:
                            ins = mm(ps[:, bank, tt:tt + 1], src[:, c, P * tt:P * tt + P], mean,
                                     start=c == 0 and tt == 0, stop=c == KT - 1, skip_group_check=True)
                ins.then_inc(sem(f"{name}_mean"), 1)

            def broadcast(name):
                tiles, heads, _, bank = NORMS[name]
                at = STAT[name][0]
                pe.wait_ge(sem(f"{name}_rstd"), 1)
                for c in range(tiles if heads else 1):
                    for tt in range(NT):
                        b, to = (bank + c // 2, S * (c % 2)) if heads else (bank, BCAST)
                        rows = P // (heads or 1)
                        for h in range(heads or 1):
                            k = at + (c * NT + tt) * (heads or 1) + h
                            ins = mm(ps[rows * h:rows * h + rows, b, to + P * tt:to + P * tt + P],
                                     rstd[:, k:k + 1].to_broadcast([P, rows]), ident[:, :], start=True, stop=True)
                ins.then_inc(sem(f"{name}_spread"), 1)

            def norm_wide(name, n, src):
                statistics(name, src, (sem("sq_ready"), 4 * n))
                broadcast(name)

            def mod_sums(m):
                pe.wait_ge(raw_done, RAW_OF[("ada", 4 * m + 3)] + 1)
                if m:
                    pe.wait_ge(sem("mods_ready"), m)
                if MOD_PV.get(m):
                    pe.wait_ge(sem("yhi_ready"), MOD_PV[m])
                    pe.wait_ge(sem("ylo_ready"), min(4, MOD_PV[m]))
                for c in range(KT):
                    ins = mm(ps[:, 7, MOD_COL + 8 * m + c:MOD_COL + 8 * m + c + 1], ada[m % 2][:, P * c:P * c + P],
                             one, start=True, stop=True)
                ins.then_inc(sem("mod_done"), 1)

            pe.wait_ge(sem("const_made"), MADE_MATRICES)
            norm_wide("mem", 0, sq_mid)
            for w in range(4):
                begin(w)
                if w == 0:
                    both_channels(w, (sem("hlo_ready"), 0, 1))
                    statistics("one", sq_lo, (sem("sq_ready"), 4))
                elif w == 1:
                    for i in range(2):
                        channels(w, i, 256, hhi, hlo, KT, last=i == 1)
                    broadcast("one")
                else:
                    for tt in range(2):
                        positions(w, tt, 0, 256, ps[:, unit_banks(w)[0], 256 * tt:256 * tt + 256], last=tt == 1)
                if w == 2:
                    mod_sums(0)
                    statistics("memk", sq_mid, (sem("memk_sq"), 0))
            broadcast("memk")
            mod_sums(1)

            def score_maps(item):
                kind, i = item
                n = ITEM_NO[item]
                if n:
                    pe.wait_ge(sem("exp_done"), n)
                if kind == "diff" and i == 0:
                    pe.wait_ge(emptied["act"], EVACUATED[WIN1 + 6][1])
                if kind == "swa" and i == 0:
                    pe.wait_ge(emptied["act"], EVACUATED[WIN1 + 2][1])
                if kind == "moba" and i == 0:
                    pe.wait_ge(sem("qk_ready"), 4)
                if kind == "mem" and i == 0:
                    pe.wait_ge(sem("qm_ready"), 2)
                    pe.wait_ge(sem("kmem_ready"), 2)
                for m in range(2):
                    part = slice(64 * m, 64 * m + 64)
                    if kind == "swa":
                        q, k = proj[part, QA + i, :], proj[part, KA[0 if i // 2 == m else 1], :]
                    elif kind == "diff":
                        q, k = proj[part, QD + i, :], proj[part, KD + i, :]
                    elif kind == "moba":
                        q, k = proj[part, Q2 + i, :], proj[part, K2 + i, :]
                    else:
                        q, k = proj[:, QM + 2 * i + m, :], kmem[:, 2 * i + m, :]
                    first = 256 if kind == "mem" else 128
                    b = SCORE_BANK + m
                    mm(ps[:, b, 0:first], q[:, 0:P], k[:, 0:first], start=True, stop=True)
                    ins = mm(ps[:, b, first:first + 256], q[:, P:2 * P], k[:, 0:256], start=True, stop=True)
                ins.then_inc(sem("scores_done"), 1)

            def turn_probs(item):
                kind, i = item
                n = ITEM_NO[item]
                pe.wait_ge(sem("probs_ready"), n + 1)
                if n:
                    pe.wait_ge(sem("pt0_ready"), n)
                    pe.wait_ge(sem("pt1_ready"), two_map_items(n - 1) if n - 1 < 4 or n - 1 >= 8 else 4)
                for m in range(1 if kind == "diff" else 2):
                    b = PT_BANKS[m]
                    if kind == "mem":
                        blocks = [(1, 0), (257, 128), (129, 256), (385, 384)]
                    else:
                        blocks = [(1, 0), (129, 128), (257, 256)]
                    for src, dst in blocks:
                        ins = nc.tensor.transpose(ps[:, b, dst:dst + P], probs[:, m, src:src + P], ident[:, :])
                ins.then_inc(sem("pt_done"), 1)

            def values(item):
                kind, i = item
                n = ITEM_NO[item]
                pe.wait_ge(sem("pt0_ready"), n + 1)
                if kind != "diff":
                    pe.wait_ge(sem("pt1_ready"), two_map_items(n))
                if n:
                    pe.wait_ge(sem("yhi_ready"), n)
                    pe.wait_ge(sem("ylo_ready"), two_map_items(n - 1) if n - 1 < 4 or n - 1 >= 8 else 4)
                if kind == "diff" and i == 0:
                    pe.wait_ge(emptied["act"], EVACUATED[WIN1 + 8][1])
                if kind == "moba" and i == 0:
                    pe.wait_ge(emptied["act"], EVACUATED[WIN2 + 5][1])
                if kind in ("swa", "diff"):
                    pe.wait_ge(sem("mods_ready"), mods_before[0])
                for m in range(1 if kind == "diff" else 2):
                    if kind == "swa":
                        o, v = ps[64 * m:64 * m + 64, PV_BANK, 0:S], vtok[:, :, 512 + 64 * (i // 2):576 + 64 * (i // 2)]
                    elif kind == "diff":
                        o, v = ps[:, PV_BANK, 0:S], vtok[:, :, P * i:P * i + P]
                    elif kind == "moba":
                        h = 2 * i + m
                        o, v = ps[64 * m:64 * m + 64, PV_BANK, 0:S], vtok[:, :, 64 * h:64 * h + 64]
                    else:
                        h = 2 * i + m
                        o, v = ps[:, PV_BANK, S * m:S * m + S], vmem[:, :, P * h:P * h + P]
                    mm(o, v[:, 0, :], pt[:, m, 0:256], start=True, stop=False)
                    if kind == "mem":
                        ins = mm(o, v[:, 1, :], pt[:, m, 256:512], start=False, stop=True)
                    else:
                        ins = mm(o[:, P:2 * P], v[:, 1, :], pt[:, m, 256:384], start=False, stop=True)
                ins.then_inc(sem("pv_done"), 1)

            def slot(w, items, s, halves):
                begin(w)
                halves(0)
                if s - 1 in items:
                    turn_probs(items[s - 1])
                if s in items:
                    score_maps(items[s])
                halves(1)
                if s - 1 in items:
                    values(items[s - 1])

            mods_before = [2]
            for s in range(17):
                w = WIN1 + s
                kind = IN1[s]
                if s in MOD_SLOTS:
                    mod_sums(MOD_SLOTS[s])
                    mods_before[0] = MOD_SLOTS[s] + 1
                b = unit_banks(w)[0]

                def halves(i):
                    if kind == "vd":
                        positions(w, i, 0, 256, ps[:, b, 256 * i:256 * i + 256], last=i == 1)
                    elif kind == "kava" and i == 0:
                        channels(w, 0, 256, hhi, hlo, KT)
                    elif kind == "kava":
                        for tt in range(2):
                            positions(w, tt, P, P, ps[:, b, S + P * tt:S + P * tt + P], last=tt == 1)
                    else:
                        channels(w, i, 256, hhi, hlo, KT, last=i == 1)

                if s == 0:
                    begin(w)
                    both_channels(w, (sem("hlo_ready"), KT, 1))
                    continue
                slot(w, ITEMS1, s, halves)
                if s == 13:
                    statistics("diff", proj[:, KD:KD + 4, :], (sem("yhi_ready"), 6))
                if s == 14:
                    broadcast("diff")

            def branch(w, tile0, waits):
                begin(w)
                for s_, n in waits:
                    pe.wait_ge(s_, n)
                for i in range(4):
                    channels(w, i, 512, yhi[:, tile0:tile0 + 4, :], ylo[:, tile0:tile0 + 4, :], 4, last=i == 3)

            def project_merged(o0, k):
                for u in range(4):
                    begin(o0 + u)
                    if u == 0:
                        both_channels(o0, (sem("mglo_ready"), 4 * k, 2))
                        if k == 0:
                            mod_sums(4)
                        continue
                    for i in range(2):
                        channels(o0 + u, i, 256, hhi, hlo, KT, last=i == 1)

            pe.wait_ge(sem("mods_ready"), 4)
            for u in range(4):
                branch(BR1 + u, 4 * (u % 2), [(sem("ylo_ready"), 4)] if u == 0 else [(sem("ydlo_ready"), 2)])
            project_merged(WO1, 0)
            norm_wide("two", 2, mg)

            def ffn(f):
                w0 = FF[f]

                def up(c, kind, j, it=0):
                    w = w0 + c
                    pe.wait_ge(raw_done, it * BODY + (RAW_OF[("w", w)] + 1))
                    if j >= 2:
                        pe.wait_ge(sem(f"a_ready{f}" if kind == "a" else f"glu_done{f}"), it * STEPS + (j - 1))
                    bank = 2 * (j % 2) + (kind == "g")
                    if c == 0:
                        both_channels(w, (sem("hlo_ready"), KT * (2, 4)[f], 1), bank)
                        return
                    if c == 3 and f == 0:
                        mod_sums(5)
                    for i in range(2):
                        channels(w, i, 256, hhi, hlo, KT, last=i == 1, bank=bank)

                def down(c, j, it=0):
                    w = w0 + c
                    first = j == 0 and isinstance(it, int)
                    pe.wait_ge(raw_done, it * BODY + (RAW_OF[("w", w)] + 1))
                    pe.wait_ge(sem(f"flo_ready{f}"), it * STEPS + (j + 1))
                    if f == 0 and c == 4:
                        pe.wait_ge(sem("mods_ready"), 6)
                    for i in range(KT):
                        for kt in range(2):
                            ins = three(ps[:, 4 + i // 2, S * (i % 2):S * (i % 2) + S], wt(whi, w, kt, P * i, P, D),
                                        wt(wlo, w, kt, P * i, P, D), fhi[:, j % 2, S * kt:S * kt + S],
                                        flo[:, j % 2, S * kt:S * kt + S], first and i % 2 == 0 and kt == 0,
                                        j == FJ - 1 and kt == 1, skip_group_check=True)
                    ins.then_inc(gemm_done, 1)

                def slot_(c, kind, j, it=0):
                    if kind == "d":
                        down(c, j, it)
                    else:
                        up(c, kind, j, it)

                for c, (kind, j) in enumerate(FFN_HEAD):
                    slot_(c, kind, j)
                with pe.Fori(0, FFN_LOOPS) as it:
                    for c, (kind, j) in enumerate(FFN_BODY):
                        slot_(len(FFN_HEAD) + c, kind, j, it)
                for c, (kind, j) in enumerate(FFN_TAIL):
                    slot_(3 * FJ - len(FFN_TAIL) + c, kind, j)

            ffn(0)
            norm_wide("final", 3, mg)
            norm_wide("mix", 4, mg)

            for s in range(26):
                w = WIN2 + s
                kind = IN2[s][0]
                b = unit_banks(w)[0]

                def halves(i):
                    if kind == "v":
                        positions(w, i, 0, 256, ps[:, b, 256 * i:256 * i + 256], last=i == 1)
                    else:
                        channels(w, i, 256, hhi, hlo, KT, last=i == 1)

                if s == 0:
                    begin(w)
                    both_channels(w, (sem("hlo_ready"), KT * 3, 1))
                    continue
                slot(w, ITEMS2, s, halves)
                if s == 4:
                    statistics("qk", tmp, (sem("qk_sq"), 0))
                if s == 5:
                    broadcast("qk")
                if s == 8:
                    pe.wait_ge(sem("qk_ready"), 4)
                    statistics("qm", conv_t, (sem("qm_sq"), 0))
                if s == 9:
                    broadcast("qm")
            for u in range(6):
                r = u % 3
                branch(BR2 + u, 4 * r, [[(sem("yclo_ready"), 2)], [(sem("ylo_ready"), 8)], [(sem("ylo_ready"), 10)]][r])
            project_merged(WO2, 1)
            norm_wide("ffn2", 5, mg)
            ffn(1)


_VECTORS = [name for name, _ in VECTORS]


def kernel(**inputs):
    import concourse.bacc as bacc
    from concourse.bass_utils import run_bass_kernel_spmd

    a = {name: np.asarray(v) for name, v in inputs.items()}

    def column_units(w, order=None):
        n = w.shape[1] // 256
        u = w.reshape(KT, P, n, 256).transpose(2, 1, 0, 3).reshape(n, P, UNIT)
        return u if order is None else u[order]

    def branch_units(ws):
        return np.stack([w.reshape(4, P, 2, 512).transpose(2, 1, 0, 3).reshape(2, P, UNIT) for w in ws], axis=1)\
            .reshape(2 * len(ws), P, UNIT)

    def row_units(w):
        return w.reshape(FJ, 2, P, D).transpose(0, 2, 1, 3).reshape(FJ, P, UNIT)

    def channel_major(v):
        return v[0].T.reshape(KT, P, S).transpose(1, 0, 2).reshape(P, KT * S)

    doubled = {n: np.concatenate([a[n], a[n]]) for n in ("moba_q_gain_2", "moba_k_gain_2")}
    arrays = {
        "w_mem_kv_2": column_units(a["w_mem_kv_2"]),
        "w_ada": a["w_ada"][0].reshape(4, 2, P, 6, D).transpose(3, 0, 2, 1, 4).reshape(24, P, UNIT),
        "w_in": column_units(a["w_in"][0]),
        "branches": branch_units([a["w_branch_swa"][0], a["w_branch_diff"][0]]),
        "w_out": column_units(a["w_out"][0]),
        "w_up": column_units(a["w_up"][0]),
        "w_down": row_units(a["w_down"][0]),
        "w_in_2": column_units(a["w_in_2"], [c // 256 for _, c in IN2]),
        "branches_2": branch_units([a["w_br_conv_2"], a["w_br_moba_2"], a["w_br_mem_2"]]),
        "w_o_2": column_units(a["w_o_2"]),
        "w_up_2": column_units(a["w_up_2"]),
        "w_down_2": row_units(a["w_down_2"]),
        "vectors": np.concatenate([doubled.get(n, a[n]).reshape(-1, P) for n in _VECTORS]).T,
        "x": channel_major(a["x"]),
        "mem_2": channel_major(a["mem_2"]),
        "swa_sinks": a["swa_sinks"],
        "diff_lambda": a["diff_lambda"],
    }
    nc = bacc.Bacc("TRN2", target_bir_lowering=False, num_devices=1, dynamic_dma_scratch_size=2048)
    feeds, tensors = {}, {}
    for name, v in arrays.items():
        feeds[f"in_{name}"] = np.ascontiguousarray(v)
        tensors[name] = nc.dram_tensor(f"in_{name}", v.shape, mybir.dt.from_np(v.dtype), kind="ExternalInput").ap()
    out = nc.dram_tensor("out", (4, P, 2 * S), F32, kind="ExternalOutput").ap()
    two_blocks(nc, tensors, out)
    r = run_bass_kernel_spmd(nc, [feeds], core_ids=[0])
    return r.results[0]["out"].reshape(4, P, 2, S).transpose(3, 0, 2, 1).reshape(1, S, D)
```

```python
from contextlib import ExitStack

import numpy as np

import concourse.bass as bass
from concourse import mybir

ALU = mybir.AluOpType
ACT = mybir.ActivationFunctionType
F32 = mybir.dt.float32
F32R = mybir.dt.float32r
I32 = mybir.dt.int32
AX_X = mybir.AxisListType.X

P = 128
D = 1024
KT = D // P
S = 256
NT = S // P
UNIT = 2048
RAW, SPLIT = 4, 4
AHEAD = SPLIT - 1
F = 2816
FJ = F // 256
HD = 64
EPS = 1e-6
BIG = 3e32
LAM_INIT = 0.8 - 0.6

VECTORS = [("b_ada", 48), ("norm1_g", 8), ("norm2_g", 8), ("final_g", 8), ("g_mix_2", 8), ("g_mem_2", 8),
           ("g_ffn_2", 8), ("c", 8), ("diff_subln_g", 1), ("memq_gain_2", 1), ("memk_gain_2", 1),
           ("moba_q_gain_2", 1), ("moba_k_gain_2", 1), ("b_gate_2", 24), ("conv_w_2", 12), ("conv_b_2", 4),
           ("conv_w", 66), ("conv_b", 22), ("ffn_conv_w_2", 66), ("ffn_conv_b_2", 22)]
COLUMN, NV = {}, 0
for _name, _n in VECTORS:
    COLUMN[_name] = NV
    NV += _n


def build_plan():
    after = {-1: range(8)}
    for a, w in enumerate((3, 4, 5, 6, 7, 9, 11, 13, 14, 15, 16, 17, WO1 + 3, FFN1, FFN1 + 2, FFN1 + 3), 8):
        after[w] = (a,)
    plan = []
    for w in range(-1, NW):
        if w >= 0:
            plan.append(("w", w))
        plan.extend(("ada", a) for a in after.get(w, ()))
    raw_of = {e: r for r, e in enumerate(plan)}
    return plan, raw_of


WIN1, BR1, WO1, FFN1, MEMKV = 0, 17, 21, 25, 58
WIN2, BR2, WO2, FFN2 = 62, 88, 94, 98
NW = 131
PLAN, RAW_OF = build_plan()

FFN_HEAD = [("a", 0), ("g", 0), ("a", 1), ("g", 1), ("d", 0), ("a", 2)]
STEPS = 4
FFN_BODY = [(kind, j + back) for j in range(2, 2 + STEPS) for kind, back in (("g", 0), ("d", -1), ("a", 1))]
FFN_LOOPS = (FJ - 3) // STEPS
BODY = len(FFN_BODY)
FFN_TAIL = [("g", FJ - 1), ("d", FJ - 2), ("d", FJ - 1)]
assert len(PLAN) == NW + 24 and FFN2 + 3 * FJ == NW

IN1 = ["qa", "qa", "kava", "qd", "qd", "kd", "kd", "vd", "vd"] + ["ga"] * 4 + ["gd"] * 4
IN2 = [(k, c0 + 256 * i) for k, c0, n in (("q", 1536, 2), ("k", 2048, 2), ("v", 2560, 2), ("qm", 3072, 2),
                                           ("cc", 512, 2), ("cx", 1024, 2), ("cb", 0, 2), ("g", 3584, 12))
       for i in range(n)]

ITEMS1 = {4: ("swa", 0), 5: ("swa", 1), 6: ("swa", 2), 7: ("swa", 3),
          8: ("diff", 0), 9: ("diff", 1), 10: ("diff", 2), 11: ("diff", 3)}
ITEMS2 = {11: ("moba", 0), 13: ("moba", 1), 15: ("moba", 2), 17: ("moba", 3), 19: ("mem", 0), 21: ("mem", 1)}
ITEM_NO = {("swa", i): i for i in range(4)}
ITEM_NO.update({("diff", i): 4 + i for i in range(4)})
ITEM_NO.update({("moba", i): 8 + i for i in range(4)})
ITEM_NO.update({("mem", i): 12 + i for i in range(2)})
Y_TILE = {"swa": 0, "moba": 4}

SCORE_BANK, PT_BANKS, PV_BANK = 4, (3, 6), 7
MOD_AT = {m: (7, 384 + 8 * m) for m in range(6)}
MOD_AT[2] = MOD_AT[5] = (3, 0)
NORMS = {"mem": (KT, 0, 3, 3), "one": (KT, 0, 6, 6), "two": (KT, 0, 3, 3), "final": (KT, 0, 3, 3), "mix": (KT, 0, 6, 6),
         "ffn2": (KT, 0, 3, 3), "memk": (4, 1, 4, 4), "diff": (4, 1, 4, 4), "qk": (8, 2, 4, 4), "qm": (4, 1, 6, None)}
STAT, N_STAT = {}, 0
for _name, (_tiles, _heads, _, _) in NORMS.items():
    STAT[_name] = (N_STAT, NT * (_tiles * _heads or 1))
    N_STAT += STAT[_name][1]
SUMMED = ("mem", "two", "final", "mix", "ffn2")
BCAST = 256


def unit_banks(w):
    for first, n in ((BR1, 4), (BR2, 6)):
        if first <= w < first + n:
            b = 2 * ((w - first + 1) % 4)
            return (b, b + 1)
    for first, b in ((WO1, 4), (WO2, 6)):
        if first <= w < first + 4:
            return ((b + w - first) % 8,)
    return (w % 3,)


def build_evacuations():
    counts, done, last_in, before = {"act": 0, "dve": 0, "x1": 0, "x5": 0}, {}, {}, {}
    for w in [*range(FFN1), *range(MEMKV, FFN2)]:
        if w == MEMKV:
            last_in = {}
        on_dve = (BR1 <= w < FFN1 or BR2 <= w < FFN2
                  or WIN2 <= w < BR2 and IN2[w - WIN2][0] in ("cx", "cb"))
        e = "x1" if WO1 <= w < FFN1 else "x5" if WO2 <= w < FFN2 else "dve" if on_dve else "act"
        counts[e] += 1
        done[w] = (e, counts[e])
        before[w] = {last_in[b] for b in unit_banks(w) if b in last_in}
        for b in unit_banks(w):
            last_in[b] = w
    return done, before


EVACUATED, BANK_BEFORE = build_evacuations()


def item_spans(kind):
    return {"mem": [(1, 257), (257, 513)], "swa": [(0, 129), (129, 386)]}.get(kind, [(1, 129), (129, 385)])


def two_map_items(n):
    return n + 1 if n < 4 else n - 3


MOD_SLOTS = {5: 2, 14: 3}
MOD_PV = {3: 8}

MADE_EPS, MADE_MATRICES, MADE_DIST, MADE_ALL = 3, 9, 11, 18


def two_blocks(nc, t, out):
    ctx = ExitStack()
    with ctx:
        base = [(nc.sbuf_base + 63) // 64 * 64]

        def place(name, shape, dt, at=None):
            n = int(np.prod(shape[1:])) * 4
            where = base[0] if at is None else at
            if at is None:
                base[0] += (n + 63) // 64 * 64
            return nc.alloc_sbuf_tensor_at(name, shape, dt, offset=where), where

        raw, _ = place("raw", [P, RAW, UNIT], F32)
        whi, _ = place("whi", [P, SPLIT, UNIT], F32R)
        wlo, _ = place("wlo", [P, SPLIT, UNIT], F32R)
        x, _ = place("x", [P, KT, S], F32)
        hhi, _ = place("hhi", [P, KT, S], F32R)
        hlo, _ = place("hlo", [P, KT, S], F32R)
        proj, _ = place("proj", [P, 14, S], F32)
        vtok, _ = place("vtok", [P, NT, 640], F32)
        kmem, kmem_at = place("kmem", [P, 4, S], F32)
        vmem, _ = place("vmem", [P, NT, 512], F32)
        mem, _ = place("mem", [P, KT, S], F32, at=kmem_at)
        yhi, y_at = place("yhi", [P, 12, S], F32R)
        ylo, ylo_at = place("ylo", [P, 12, S], F32R)
        probs, _ = place("probs", [P, 2, 514], F32)
        pt, pt_at = place("pt", [P, 2, 512], F32)
        dist_i, _ = place("dist_i", [P, 384], I32, at=pt_at)
        lam_in, _ = place("lam_in", [P, 4, HD], F32, at=pt_at + 2048)
        dist_swa, _ = place("dist_swa", [P, 384], F32)
        dist_diff, _ = place("dist_diff", [P, 384], F32)
        causal, _ = place("causal", [P, 384], F32)
        vec, _ = place("vec", [P, NV], F32)
        ident, _ = place("ident", [P, P], F32)
        mean_d, _ = place("mean_d", [P, P], F32)
        mean_128, _ = place("mean_128", [P, P], F32)
        mean_64, _ = place("mean_64", [P, P], F32)
        small, _ = place("small", [P, 256], F32)
        std, _ = place("std", [P, N_STAT], F32)
        rstd, _ = place("rstd", [P, N_STAT], F32)
        _, scratch_at = place("scratch", [P, 24, S], F32)
        ada = [place(f"ada{i}", [P, D], F32, at=a + 8 * S * 4)[0] for i, a in enumerate((y_at, ylo_at))]
        gate, _ = place("gate", [P, 24, S], F32, at=scratch_at)
        tmp, _ = place("tmp", [P, KT, S], F32, at=scratch_at + 16 * S * 4)
        conv_c, _ = place("conv_c", [P, 4, S], F32, at=scratch_at + 12 * S * 4)
        conv_t, _ = place("conv_t", [P, 4, S], F32, at=scratch_at + 8 * S * 4)
        conv_u, _ = place("conv_u", [P, 4, S + 2], F32, at=scratch_at + 19 * S * 4)
        squares, _ = place("squares", [P, KT, S], F32, at=scratch_at)
        fa, _ = place("fa", [P, 2, 2, S + 2], F32, at=scratch_at)
        fc, _ = place("fc", [P, 2, 2 * S], F32, at=scratch_at + 5 * 1024)
        fg, _ = place("fg", [P, 2, 2 * S], F32, at=scratch_at + 9 * 1024)
        fp, _ = place("fp", [P, 2, 2 * S], F32, at=scratch_at + 13 * 1024)
        cw, _ = place("cw", [P, 2, 4, 2], F32)
        fhi, _ = place("fhi", [P, 2, 2 * S], F32R, at=y_at)
        flo, _ = place("flo", [P, 2, 2 * S], F32R, at=y_at + 4096)
        ps = ctx.enter_context(nc.psum_tensor("ps", [P, 8, 512], F32))

        def f32(ap):
            return ap.bitcast(F32)

        mg = proj
        QA, KA, QD, KD = 0, (4, 13), 5, 9
        Q2, K2, QM = 0, 4, 8
        mod = small[:, 0:48]
        gs1, gs2 = small[:, 48:56], small[:, 56:64]
        half_bg = small[:, 64:88]
        cs = small[:, 88:96]
        csig = small[:, 96:104]
        sinks = small[:, 104:112]
        nmax, rsum, rinv = small[:, 112:116], small[:, 116:120], small[:, 120:124]
        neglam = small[:, 124:125]
        lam_d, lam_e, lam_s = small[:, 126:128], small[:, 128:130], small[:, 130:131]
        gdiff, gmoba, gmem = small[:, 131:132], small[:, 132:133], small[:, 133:134]
        eps = small[:, 134:135]
        one, eps_root = small[:, 135:136], small[:, 140:141]
        rlam = small[:, 136:138]

        def col(name, i=0, n=1):
            c = COLUMN[name] + i
            return vec[:, c:c + n]

        sems = {}

        def sem(name):
            if name not in sems:
                sems[name] = ctx.enter_context(nc.semaphore(name))
            return sems[name]

        landed = [sem(f"raw_landed{i}") for i in range(RAW)]
        raw_done = sem("raw_done")
        hi_ready = sem("hi_ready")
        gemm_done = sem("gemm_done")
        emptied = {"act": sem("emptied_by_act"), "dve": sem("emptied_by_dve"),
                   "x1": sem("x1_ready"), "x5": sem("x5_ready")}

        def unit_source(w):
            for name, first in (("w_o_2", WO2), ("branches_2", BR2), ("w_in_2", WIN2), ("w_mem_kv_2", MEMKV),
                                ("w_out", WO1), ("branches", BR1), ("w_in", WIN1)):
                if w >= first:
                    return t[name][w - first]

        def ffn_source(f, kind, j):
            array = t[("w_down", "w_down_2")[f] if kind == "d" else ("w_up", "w_up_2")[f]]
            return array.rearrange("u p n -> p u n")[:, bass.ds(j + (FJ if kind == "g" else 0), 1), :]

        block = ctx.enter_context(nc.Block())

        FF = [FFN1, FFN2]

        @block.sync
        def _(sp):
            def load(r, src, it=0):
                if r >= RAW:
                    sp.wait_ge(raw_done, it * BODY + (r - RAW + 1))
                dst = raw[:, r % RAW:r % RAW + 1, :] if len(src.shape) == 3 else raw[:, r % RAW, :]
                sp.dma_start(dst, src).then_inc(landed[r % RAW], 16)

            for r, (kind, n) in enumerate(PLAN):
                if (kind, n) == ("w", 8):
                    sp.dma_start(mem[:, :, :].rearrange("p a b -> p (a b)"), t["mem_2"]).then_inc(sem("mem_landed"), 16)
                f = 1 if n >= FFN2 else 0
                c = n - FF[f]
                if kind == "ada":
                    load(r, t["w_ada"][n])
                elif not 0 <= c < 3 * FJ:
                    load(r, unit_source(n))
                elif c < len(FFN_HEAD):
                    load(r, ffn_source(f, *FFN_HEAD[c]))
                elif c == len(FFN_HEAD):
                    with sp.Fori(0, FFN_LOOPS) as it:
                        for b, (kind_, j) in enumerate(FFN_BODY):
                            load(r + b, ffn_source(f, kind_, it * STEPS + j), it)
                elif c >= 3 * FJ - len(FFN_TAIL):
                    load(r, ffn_source(f, *FFN_TAIL[c - 3 * FJ]))
            for u in range(4):
                sp.wait_ge(sem("x6_ready"), u + 1)
                sp.dma_start(out[u], x[:, 2 * u:2 * u + 2, :].rearrange("p a b -> p (a b)")).then_inc(sem("stored"), 16)
            sp.wait_ge(sem("stored"), 16 * 4)

        @block.gpsimd
        def _(pool):
            n = 0

            def step(ins):
                nonlocal n
                n += 1
                ins.then_inc(sem("const_made"), 1)
                pool.wait_ge(sem("const_made"), n)

            step(nc.gpsimd.memset(ident[:, :], 0.0))
            step(nc.gpsimd.affine_select(out=ident[:, :], in_=ident[:, :], compare_op=ALU.not_equal, fill=1.0,
                                         base=0, pattern=[[-1, P]], channel_multiplier=1))
            step(nc.gpsimd.memset(eps, EPS))
            step(nc.gpsimd.memset(one, 1.0))
            step(nc.gpsimd.memset(mean_d[:, :], 1.0 / D))
            step(nc.gpsimd.memset(mean_128[:, :], 1.0 / 128))
            step(nc.gpsimd.memset(mean_64[:, :], 0.0))
            step(nc.gpsimd.memset(mean_64[0:64, 0:64], 1.0 / 64))
            step(nc.gpsimd.memset(mean_64[64:128, 64:128], 1.0 / 64))
            step(nc.gpsimd.iota(dist_i[:, 0:128], pattern=[[-1, 128]], base=0, channel_multiplier=1))
            step(nc.gpsimd.iota(dist_i[:, 128:384], pattern=[[-1, 256]], base=128, channel_multiplier=1))
            step(nc.gpsimd.memset(causal[:, :], 0.0))
            pool.wait_ge(sem("dist_float"), 1)
            for tile, fill in ((dist_diff, BIG), (causal, -BIG)):
                for c0, cn, b in ((0, 128, 0), (128, 256, 128)):
                    step(nc.gpsimd.affine_select(out=tile[:, c0:c0 + cn], in_=tile[:, c0:c0 + cn], compare_op=ALU.is_ge,
                                                 fill=fill, base=b, pattern=[[-1, cn]], channel_multiplier=1))
            step(nc.gpsimd.tensor_copy(dist_swa[:, 0:128], dist_diff[:, 0:128]))
            step(nc.gpsimd.affine_select(out=dist_swa[:, 128:384], in_=dist_diff[:, 128:384], compare_op=ALU.is_ge,
                                         fill=BIG, base=127 - 128, pattern=[[1, 256]], channel_multiplier=-1))
            assert n == MADE_ALL

        @block.scalar
        def _(act):
            act.dma_start(vec[:, :], t["vectors"]).then_inc(sem("vec_landed"), 16)
            act.dma_start(x[:, :, :].rearrange("p a b -> p (a b)"), t["x"]).then_inc(sem("x_landed"), 16)
            act.dma_start(lam_in[:, :, :].rearrange("p a b -> p (a b)"),
                          t["diff_lambda"].rearrange("o a b -> o (a b)").to_broadcast([P, 4 * HD]))\
                .then_inc(sem("lam_landed"), 16)
            act.dma_start(sinks, t["swa_sinks"].to_broadcast([P, 8])).then_inc(sem("sinks_landed"), 16)

            def copy(dst, src, func=ACT.Copy, **kw):
                return nc.scalar.activation(dst, src, func, **kw)

            def round_unit(w, it=0):
                if w >= NW:
                    return
                r = RAW_OF[("w", w)]
                act.wait_ge(landed[r % RAW], it * (16 * BODY // RAW) + 16 * (r // RAW + 1))
                if w >= SPLIT:
                    act.wait_ge(gemm_done, it * BODY + (w - SPLIT + 1))
                copy(whi[:, w % SPLIT, :], raw[:, r % RAW, :]).then_inc(hi_ready, 1)

            def square(src, dst, i, ready=None):
                if ready is not None:
                    act.wait_ge(ready, i + 1)
                copy(dst[:, 2 * i:2 * i + 2, :], src[:, 2 * i:2 * i + 2, :], ACT.Square).then_inc(sem("sq_ready"), 1)

            def square_all(src, dst, ready=None):
                for i in range(4):
                    square(src, dst, i, ready)

            def root(name, preload=False):
                if preload:
                    copy(eps_root, eps, ACT.Sqrt)
                (c, n), bank = STAT[name], NORMS[name][2]
                act.wait_ge(sem(f"{name}_mean"), 1)
                copy(std[:, c:c + n], ps[:, bank, 0:n], ACT.Sqrt, bias=eps).then_inc(sem(f"{name}_std"), 1)

            def round_h(k, shift=None, src=tmp):
                for c in range(KT):
                    act.wait_ge(sem("scaled_ready"), KT * k + c + 1)
                    if shift is None:
                        ins = copy(hhi[:, c, :], src[:, c, :])
                    else:
                        ins = copy(hhi[:, c, :], src[:, c, :], ACT.Identity, bias=shift[:, c:c + 1])
                    ins.then_inc(sem("hhi_ready"), 1)

            def empty(w, dst, src, func=ACT.Copy, **kw):
                act.wait_ge(gemm_done, w + 1)
                copy(dst, src, func, **kw).then_inc(emptied["act"], 1)

            def pair(bank):
                return bank.rearrange("p (a b) -> p a b", a=2)

            act.wait_ge(sem("vec_landed"), 16)
            copy(csig, col("c", n=8), ACT.Sigmoid).then_inc(sem("csig_ready"), 1)
            act.wait_ge(sem("x_landed"), 16)
            square_all(x, squares)
            act.wait_ge(sem("const_made"), MADE_EPS)
            root("one", preload=True)
            act.wait_ge(sem("lam_dots"), 2)
            copy(lam_e, lam_d, ACT.Exp).then_inc(sem("lam_exp"), 1)
            round_unit(0)
            round_unit(1)
            round_h(0)
            round_unit(2)

            def exps(item):
                kind, i = item
                n = ITEM_NO[item]
                act.wait_ge(sem("max_ready"), n + 1)
                for m in range(2):
                    for q, (a, b) in enumerate(item_spans(kind)):
                        src = ps[:, SCORE_BANK + m, a - 1:b - 1] if kind == "mem" else probs[:, m, a:b]
                        c = 2 * m + q
                        k = STAT["qm"][0] + 4 * i + c
                        ins = copy(probs[:, m, a:b], src, ACT.Exp, bias=nmax[:, c:c + 1], accum_out=rsum[:, c:c + 1],
                                   scale=rstd[:, k:k + 1] if kind == "mem" else 1.0)
                ins.then_inc(sem("exp_done"), 1)

            def empty_pt(item):
                act.wait_ge(sem("pt_done"), ITEM_NO[item] + 1)
                w = 512 if item[0] == "mem" else 384
                copy(pt[:, 0, 0:w], ps[:, PT_BANKS[0], 0:w]).then_inc(sem("pt0_ready"), 1)
                if item[0] in ("moba", "mem"):
                    copy(pt[:, 1, 0:w], ps[:, PT_BANKS[1], 0:w]).then_inc(sem("pt1_ready"), 1)

            def empty_pv(item):
                kind, i = item
                act.wait_ge(sem("pv_done"), ITEM_NO[item] + 1)
                if kind == "diff":
                    copy(proj[:, KD + i, :], ps[:, PV_BANK, 0:S], ACT.Square)
                    ins = copy(proj[:, QD + i, :], ps[:, PV_BANK, 0:S])
                elif kind == "mem":
                    ins = copy(yhi[:, 8 + 2 * i:10 + 2 * i, :], pair(ps[:, PV_BANK, :]))
                else:
                    ins = copy(yhi[:, Y_TILE[kind] + i, :], ps[:, PV_BANK, 0:S])
                ins.then_inc(sem("yhi_ready"), 1)

            def attention(items, s, w):
                if s - 2 in items:
                    empty_pv(items[s - 2])
                if s - 1 in items:
                    empty_pt(items[s - 1])
                if s in items:
                    round_unit(w)
                    exps(items[s])

            for s in range(18):
                if s >= 1:
                    w, k = WIN1 + s - 1, s - 1
                    kind, bank = IN1[k], ps[:, unit_banks(w)[0], :]
                    if kind == "qa":
                        empty(w, proj[:, QA + 2 * k:QA + 2 * k + 2, :], pair(bank), scale=HD ** -0.5)
                    elif kind == "kava":
                        act.wait_ge(gemm_done, w + 1)
                        copy(proj[:, KA[0], :], bank[:, 0:S])
                        copy(proj[0:64, KA[1], :], bank[64:128, 0:S])
                        copy(proj[64:128, KA[1], :], bank[0:64, 0:S])
                        empty(w, vtok[:, :, 512:640], pair(bank[:, S:2 * S]))
                    elif kind == "qd":
                        c = QD + 2 * (k - 3)
                        empty(w, proj[:, c:c + 2, :], pair(bank), scale=HD ** -0.5)
                    elif kind == "kd":
                        c = KD + 2 * (k - 5)
                        empty(w, proj[:, c:c + 2, :], pair(bank))
                    elif kind == "vd":
                        c = 256 * (k - 7)
                        empty(w, vtok[:, :, c:c + 256], pair(bank))
                    else:
                        empty(w, gate[:, 2 * (k - 9):2 * (k - 9) + 2, :], pair(bank), ACT.Tanh, scale=0.5)
                if s not in ITEMS1:
                    round_unit(WIN1 + s + AHEAD)
                attention(ITEMS1, s, WIN1 + s + AHEAD)
                if s == 12:
                    act.wait_ge(sem("mem_landed"), 16)
                    act.wait_ge(sem("hlo_ready"), KT)
                    square_all(mem, tmp)
                if s == 14:
                    root("mem")
                    root("diff")
                if s == 15:
                    for i in range(2):
                        act.wait_ge(sem("diff_out"), i + 1)
                        copy(yhi[:, 4 + 2 * i:6 + 2 * i, :], proj[:, QD + 2 * i:QD + 2 * i + 2, :])\
                            .then_inc(sem("ydhi_ready"), 1)

            def merge_and_project(b0, nbr, o0, k, name):
                for u in range(1, 2 * nbr):
                    if u == nbr:
                        round_merged(k, 0)
                    if u < 2 * nbr - 1:
                        round_unit(b0 + u + AHEAD)
                round_merged(k, 1)
                round_unit(o0 + AHEAD - 1)
                for u in range(4):
                    if u < 3:
                        round_unit(o0 + u + AHEAD)
                    square(x, mg, u, sem(name))

            def round_merged(k, half):
                for i in range(2):
                    act.wait_ge(sem("merged"), 4 * k + 2 * half + i + 1)
                    c = 4 * half + 2 * i
                    copy(hhi[:, c:c + 2, :], mg[:, c:c + 2, :], scale=0.5).then_inc(sem("mghi_ready"), 1)

            merge_and_project(BR1, 2, WO1, 0, "x1_ready")
            root("two", preload=True)
            round_unit(WO1 + 3 + AHEAD)
            act.wait_ge(sem("mods_ready"), 4)
            round_h(1, shift=mod[:, 24:32])

            def ffn(f):
                w0 = FF[f]
                func = (ACT.Gelu, ACT.Silu)[f]

                def pad_a(c, j, b, it=0):
                    act.wait_ge(gemm_done, it * BODY + (w0 + c + 1))
                    if j >= 2:
                        act.wait_ge(sem(f"conv_done{f}"), it * STEPS + (j - 1))
                    else:
                        act.wait_ge(sem(f"pads_ready"), f + 1)
                    copy(fa[:, b, :, 2:S + 2], pair(ps[:, (0, 2)[b], :])).then_inc(sem(f"a_ready{f}"), 1)

                def activate(j, b, it=0):
                    act.wait_ge(sem(f"conv_done{f}"), it * STEPS + (j + 1))
                    if j >= 2:
                        act.wait_ge(sem(f"glu_done{f}"), it * STEPS + (j - 1))
                    copy(fg[:, b, :], fc[:, b, :], func).then_inc(sem(f"act_done{f}"), 1)

                def round_product(j, b, it=0):
                    act.wait_ge(sem(f"glu_done{f}"), it * STEPS + (j + 1))
                    if j >= 2:
                        act.wait_ge(gemm_done, it * BODY + (w0 + 3 * j - 1))
                    copy(fhi[:, b, :], fp[:, b, :]).then_inc(sem(f"fhi_ready{f}"), 1)

                def slot(c, kind, j, it=0):
                    if f == 0 and c == 3 * FJ - 1:
                        act.wait_ge(gemm_done, w0 + 3 * FJ - 2)
                        round_h(2, src=mg)
                    round_unit(w0 + c + AHEAD, it)
                    if kind == "g":
                        pad_a(c - 1, j, j % 2, it)
                    if kind == "d" and j + 1 < FJ or kind == "a" and c == 2:
                        k = j + 1 if kind == "d" else 0
                        activate(k, k % 2, it)
                        round_product(k, k % 2, it)

                for c, (kind, j) in enumerate(FFN_HEAD):
                    slot(c, kind, j)
                with act.Fori(0, FFN_LOOPS) as it:
                    for c, (kind, j) in enumerate(FFN_BODY):
                        slot(len(FFN_HEAD) + c, kind, j, it)
                for c, (kind, j) in enumerate(FFN_TAIL):
                    slot(3 * FJ - len(FFN_TAIL) + c, kind, j)

            def memory_keys(i):
                w = MEMKV + i
                bank = ps[:, unit_banks(w)[0], :]
                act.wait_ge(gemm_done, w + 1)
                copy(squares[:, 2 * i:2 * i + 2, :], pair(bank), ACT.Square).then_inc(sem("memk_sq"), 1)
                empty(w, kmem[:, 2 * i:2 * i + 2, :], pair(bank))

            def memory_values(i):
                w = MEMKV + 2 + i
                empty(w, vmem[:, :, 256 * i:256 * i + 256], pair(ps[:, unit_banks(w)[0], :]))

            ffn(0)
            square_all(x, mg, sem("x2_ready"))
            round_unit(MEMKV + 3)
            memory_keys(0)
            round_unit(MEMKV + 4)
            root("final", preload=True)
            memory_keys(1)
            round_unit(MEMKV + 5)
            square_all(x, mg, sem("x3_ready"))
            memory_values(0)
            root("mix")
            memory_values(1)
            round_h(3)
            round_unit(MEMKV + 6)

            for s in range(27):
                if s == 2:
                    root("memk")
                if s >= 1:
                    w, k = WIN2 + s - 1, s - 1
                    kind, bank = IN2[k][0], ps[:, unit_banks(w)[0], :]
                    if kind in ("q", "k"):
                        act.wait_ge(gemm_done, w + 1)
                        copy(tmp[:, 2 * k:2 * k + 2, :], pair(bank), ACT.Square).then_inc(sem("qk_sq"), 1)
                        empty(w, proj[:, 2 * k:2 * k + 2, :], pair(bank))
                    elif kind == "v":
                        empty(w, vtok[:, :, 256 * (k - 4):256 * (k - 4) + 256], pair(bank))
                    elif kind == "qm":
                        c = 2 * (k - 6)
                        act.wait_ge(gemm_done, w + 1)
                        copy(conv_t[:, c:c + 2, :], pair(bank), ACT.Square).then_inc(sem("qm_sq"), 1)
                        empty(w, proj[:, QM + c:QM + c + 2, :], pair(bank))
                    elif kind == "cc":
                        c = 2 * (k - 8)
                        empty(w, conv_c[:, c:c + 2, :], pair(bank))
                    elif kind == "g":
                        act.wait_ge(gemm_done, w + 1)
                        g = 2 * (k - 14)
                        copy(gate[:, g, :], bank[:, 0:S], ACT.Tanh, scale=0.5, bias=half_bg[:, g:g + 1])
                        empty(w, gate[:, g + 1, :], bank[:, S:2 * S], ACT.Tanh, scale=0.5, bias=half_bg[:, g + 1:g + 2])
                if s not in ITEMS2:
                    round_unit(WIN2 + s + AHEAD)
                attention(ITEMS2, s, WIN2 + s + AHEAD)
                if s == 5:
                    root("qk")
                if s == 9:
                    root("qm")
                if s in (14, 15):
                    i = s - 14
                    act.wait_ge(emptied["dve"], EVACUATED[WIN2 + 12 + i][1])
                    copy(yhi[:, 2 * i:2 * i + 2, :], conv_t[:, 2 * i:2 * i + 2, :]).then_inc(sem("ychi_ready"), 1)
            merge_and_project(BR2, 3, WO2, 1, "x5_ready")
            root("ffn2", preload=True)
            round_unit(WO2 + 3 + AHEAD)
            round_h(4)
            ffn(1)

        @block.vector
        def _(dve):
            V = nc.vector
            link_n = 0

            def link(ins):
                nonlocal link_n
                link_n += 1
                ins.then_inc(sem("dve_step"), 1)
                dve.wait_ge(sem("dve_step"), link_n)

            def pair(bank):
                return bank.rearrange("p (a b) -> p a b", a=2)

            def fold_ada(a):
                r, m, k = RAW_OF[("ada", a)], a // 4, a % 4
                acc = ada[m % 2]
                if k == 0 and m >= 2:
                    dve.wait_ge(sem("mod_done"), m - 1)
                dve.wait_ge(landed[r % RAW], 16 * (r // RAW + 1))
                src = raw[:, r % RAW, :].rearrange("p (a b) -> p a b", a=2)
                if k:
                    dve.wait_ge(raw_done, RAW_OF[("ada", a - 1)] + 1)
                    link(V.scalar_tensor_tensor(out=acc[:, :], in0=src[:, 0, :], scalar=cs[:, 2 * k:2 * k + 1],
                                                in1=acc[:, :], op0=ALU.mult, op1=ALU.add))
                else:
                    link(V.tensor_scalar(acc[:, :], src[:, 0, :], cs[:, 0:1], None, ALU.mult))
                V.scalar_tensor_tensor(out=acc[:, :], in0=src[:, 1, :], scalar=cs[:, 2 * k + 1:2 * k + 2],
                                       in1=acc[:, :], op0=ALU.mult, op1=ALU.add).then_inc(raw_done, 1)

            def split_low(w, it=0, fold=True):
                if w >= NW:
                    return
                r = RAW_OF[("w", w)]
                dve.wait_ge(hi_ready, it * BODY + (w + 1))
                if w >= SPLIT:
                    dve.wait_ge(gemm_done, it * BODY + (w - SPLIT + 1))
                V.tensor_tensor(wlo[:, w % SPLIT, :], raw[:, r % RAW, :], f32(whi[:, w % SPLIT, :]),
                                ALU.subtract).then_inc(raw_done, 1)
                if fold:
                    fold_after(w)

            def fold_after(w):
                r = RAW_OF[("w", w)] + 1
                while r < len(PLAN) and PLAN[r][0] == "ada":
                    fold_ada(PLAN[r][1])
                    r += 1

            def mods(m):
                dve.wait_ge(sem("mod_done"), m + 1)
                bank, c = MOD_AT[m]
                V.tensor_tensor(mod[:, 8 * m:8 * m + 8], ps[:, bank, c:c + 8],
                                col("b_ada", 8 * m, 8), ALU.add).then_inc(sem("mods_ready"), 1)
                dve.wait_ge(sem("mods_ready"), m + 1)

            def gains(dst, m, name):
                link(V.scalar_tensor_tensor(out=dst, in0=mod[:, 8 * m:8 * m + 8], scalar=1.0, in1=col(name, n=8),
                                            op0=ALU.add, op1=ALU.mult))

            def sum_squares(name, n, src, i):
                dve.wait_ge(sem("sq_ready"), 4 * n + i + 1)
                for c in (2 * i, 2 * i + 1):
                    if c:
                        ins = V.tensor_tensor(src[:, 0, :], src[:, 0, :], src[:, c, :], ALU.add)
                        if c < KT - 1:
                            link(ins)
                        else:
                            ins.then_inc(sem(f"{name}_summed"), 1)

            def invert(name):
                c, n = STAT[name]
                dve.wait_ge(sem(f"{name}_std"), 1)
                V.reciprocal(rstd[:, c:c + n], std[:, c:c + n]).then_inc(sem(f"{name}_rstd"), 1)

            def spread(name, i=0):
                dve.wait_ge(sem(f"{name}_spread"), 1)
                _, heads, _, bank = NORMS[name]
                return pair(ps[:, bank + i, :]) if heads else ps[:, bank, BCAST:BCAST + S]

            def norm_h(k, scaled, shift=None, tmp=tmp):
                for c in range(KT + 2):
                    if c < KT:
                        scaled(c).then_inc(sem("scaled_ready"), 1)
                    if c >= 2:
                        e = c - 2
                        dve.wait_ge(sem("hhi_ready"), KT * k + e + 1)
                        if shift is None:
                            ins = V.tensor_tensor(hlo[:, e, :], tmp[:, e, :], f32(hhi[:, e, :]), ALU.subtract)
                        else:
                            ins = V.scalar_tensor_tensor(out=hlo[:, e, :], in0=tmp[:, e, :], scalar=shift[:, e:e + 1],
                                                         in1=f32(hhi[:, e, :]), op0=ALU.add, op1=ALU.subtract)
                        ins.then_inc(sem("hlo_ready"), 1)

            def norm_wide(k, name, src, gcol, shift=None):
                invert(name)
                r = spread(name)
                norm_h(k, lambda c: V.scalar_tensor_tensor(out=tmp[:, c, :], in0=src[:, c, :], scalar=gcol(c), in1=r,
                                                           op0=ALU.mult, op1=ALU.mult), shift)

            dve.wait_ge(sem("vec_landed"), 16)
            dve.wait_ge(sem("csig_ready"), 1)
            link(V.tensor_tensor(cs, col("c", n=8), csig, ALU.mult))
            fold_ada(0)
            fold_ada(1)
            V.tensor_scalar(gdiff, col("diff_subln_g"), 1.0 - LAM_INIT, None, ALU.mult)
            V.tensor_scalar(gmoba, col("moba_q_gain_2"), col("moba_k_gain_2"), HD ** -0.5, ALU.mult, ALU.mult)
            V.tensor_scalar(gmem, col("memq_gain_2"), col("memk_gain_2"), P ** -0.5, ALU.mult, ALU.mult)
            V.tensor_scalar(half_bg, col("b_gate_2", n=24), 0.5, None, ALU.mult)
            fold_ada(2)
            fold_ada(3)
            invert("one")
            dve.wait_ge(sem("lam_landed"), 16)
            for i in range(2):
                V.tensor_tensor_reduce(out=lam_in[:, 2 * i, :], in0=lam_in[:, 2 * i, :], in1=lam_in[:, 2 * i + 1, :],
                                       scale=1.0, scalar=0.0, op0=ALU.mult, op1=ALU.add,
                                       accum_out=lam_d[:, i:i + 1]).then_inc(sem("lam_dots"), 1)
            dve.wait_ge(sem("const_made"), MADE_DIST)
            V.tensor_copy(dist_diff[:, :], dist_i[:, :]).then_inc(sem("dist_float"), 1)
            fold_ada(4)
            r = spread("one")
            for c in range(KT):
                ins = V.tensor_tensor(tmp[:, c, :], x[:, c, :], r, ALU.mult)
            link(ins)
            dve.wait_ge(sem("lam_exp"), 1)
            link(V.tensor_tensor(lam_s, lam_e[:, 0:1], lam_e[:, 1:2], ALU.subtract))
            link(V.tensor_scalar(neglam, lam_s, LAM_INIT, -1.0, ALU.add, ALU.mult))
            for a in (5, 6, 7):
                fold_ada(a)

            mods(0)
            split_low(0)
            mods(1)
            gains(gs1, 1, "norm1_g")
            norm_h(0, lambda c: V.tensor_scalar(tmp[:, c, :], tmp[:, c, :], gs1[:, c:c + 1], mod[:, c:c + 1],
                                                ALU.mult, ALU.add))
            split_low(1)
            split_low(2)

            def scores(item):
                kind, i = item
                n = ITEM_NO[item]
                if kind == "mem":
                    dve.wait_ge(sem("scores_done"), n + 1)
                else:
                    if n:
                        dve.wait_ge(sem("pt_done"), n)
                    if n == 0:
                        dve.wait_ge(sem("sinks_landed"), 16)
                    if kind == "swa":
                        for m in range(2):
                            V.tensor_copy(probs[:, m, 0:386:385],
                                          sinks[:, 2 * i + m:2 * i + m + 1].to_broadcast([P, 2]))
                    dve.wait_ge(sem("scores_done"), n + 1)
                    if n == 0:
                        dve.wait_ge(sem("const_made"), MADE_ALL)
                    for m in range(2):
                        if kind == "moba":
                            for q, (a, b) in enumerate(item_spans(kind)):
                                c = STAT["qk"][0] + (i * NT + q) * 2 + m
                                ins = V.scalar_tensor_tensor(out=probs[:, m, a:b], in0=ps[:, SCORE_BANK + m, a - 1:b - 1],
                                                             scalar=rstd[:, c:c + 1], in1=causal[:, a - 1:b - 1],
                                                             op0=ALU.mult, op1=ALU.add)
                            continue
                        slope = {"swa": 2.0 ** -(2 * i + m + 1), "diff": 2.0 ** (-2 * (i + 1))}[kind]
                        dist = {"swa": dist_swa, "diff": dist_diff}[kind]
                        ins = V.scalar_tensor_tensor(out=probs[:, m, 1:385], in0=dist[:, :], scalar=-slope,
                                                     in1=ps[:, SCORE_BANK + m, 0:384], op0=ALU.mult, op1=ALU.add)
                    link(ins)
                for q, (a, b) in enumerate(item_spans(kind)):
                    src = ps[:, SCORE_BANK:SCORE_BANK + 2, a - 1:b - 1] if kind == "mem" else probs[:, :, a:b]
                    ins = V.tensor_reduce(nmax[:, q:4:2], src, AX_X, ALU.max, negate=True)
                if kind == "mem":
                    link(ins)
                    c = STAT["qm"][0] + 4 * i
                    ins = V.tensor_tensor(nmax, nmax, rstd[:, c:c + 4], ALU.mult)
                ins.then_inc(sem("max_ready"), 1)

            def normalise(item):
                kind, i = item
                dve.wait_ge(sem("exp_done"), ITEM_NO[item] + 1)
                link(V.reciprocal(rinv, rsum))
                spans = [(1, 257), (257, 513)] if kind == "mem" else [(1, 129), (129, 385)]
                if kind == "diff":
                    link(V.tensor_scalar(rlam, rinv[:, 2:4], neglam, None, ALU.mult))
                    for q, (a, b) in enumerate(spans):
                        ins = V.tensor_scalar(probs[:, 1, a:b], probs[:, 1, a:b], rlam[:, q:q + 1], None, ALU.mult)
                    link(ins)
                    for q, (a, b) in enumerate(spans):
                        ins = V.scalar_tensor_tensor(out=probs[:, 0, a:b], in0=probs[:, 0, a:b], scalar=rinv[:, q:q + 1],
                                                     in1=probs[:, 1, a:b], op0=ALU.mult, op1=ALU.add)
                else:
                    for m in range(2):
                        for q, (a, b) in enumerate(spans):
                            c = 2 * m + q
                            ins = V.tensor_scalar(probs[:, m, a:b], probs[:, m, a:b], rinv[:, c:c + 1], None, ALU.mult)
                ins.then_inc(sem("probs_ready"), 1)

            def empty_pt(item):
                if item[0] != "swa":
                    return
                dve.wait_ge(sem("pt_done"), ITEM_NO[item] + 1)
                V.tensor_copy(pt[:, 1, 0:384], ps[:, PT_BANKS[1], 0:384]).then_inc(sem("pt1_ready"), 1)

            def low_pv(item):
                kind, i = item
                if kind == "diff":
                    return
                dve.wait_ge(sem("yhi_ready"), ITEM_NO[item] + 1)
                if kind == "mem":
                    c = slice(8 + 2 * i, 10 + 2 * i)
                    ins = V.tensor_tensor(ylo[:, c, :], pair(ps[:, PV_BANK, :]), f32(yhi[:, c, :]), ALU.subtract)
                else:
                    c = Y_TILE[kind] + i
                    ins = V.tensor_tensor(ylo[:, c, :], ps[:, PV_BANK, 0:S], f32(yhi[:, c, :]), ALU.subtract)
                ins.then_inc(sem("ylo_ready"), 1)

            def attention(items, s, w):
                if s - 1 in items:
                    empty_pt(items[s - 1])
                if s in items:
                    scores(items[s])
                    split_low(w, fold=False)
                    normalise(items[s])
                    fold_after(w)

            for s in range(18):
                if s not in ITEMS1:
                    split_low(WIN1 + s + AHEAD)
                if s - 2 in ITEMS1:
                    low_pv(ITEMS1[s - 2])
                if s in MOD_SLOTS:
                    mods(MOD_SLOTS[s])
                attention(ITEMS1, s, WIN1 + s + AHEAD)
                if s == 12:
                    for i in range(4):
                        sum_squares("mem", 1, tmp, i)
                if s == 14:
                    invert("mem")
                    invert("diff")
                if s == 15:
                    for i in range(2):
                        r = spread("diff", i)
                        c = slice(QD + 2 * i, QD + 2 * i + 2)
                        V.scalar_tensor_tensor(out=proj[:, c, :], in0=proj[:, c, :], scalar=gdiff, in1=r,
                                               op0=ALU.mult, op1=ALU.mult).then_inc(sem("diff_out"), 1)
                if s == 16:
                    for i in range(2):
                        dve.wait_ge(sem("ydhi_ready"), i + 1)
                        c = slice(4 + 2 * i, 6 + 2 * i)
                        V.tensor_tensor(ylo[:, c, :], proj[:, QD + 2 * i:QD + 2 * i + 2, :], f32(yhi[:, c, :]),
                                        ALU.subtract).then_inc(sem("ydlo_ready"), 1)

            def merge(w, b, nbr, k, by_bank=False):
                r, half = b % nbr, b // nbr
                dve.wait_ge(sem("first_bank_done") if by_bank else gemm_done, k + 1 if by_bank else w + 1)
                for i, bank in enumerate(unit_banks(w)):
                    if by_bank and i == 1:
                        dve.wait_ge(gemm_done, w + 1)
                    c = 4 * half + 2 * i
                    g = gate[:, KT * r + c:KT * r + c + 2, :]
                    if r == 0:
                        ins = V.scalar_tensor_tensor(out=mg[:, c:c + 2, :], in0=g, scalar=1.0, in1=pair(ps[:, bank, :]),
                                                     op0=ALU.add, op1=ALU.mult)
                        if i == 1:
                            ins.then_inc(emptied["dve"], 1)
                    else:
                        term = pair(probs[:, i, 0:512])
                        ins = V.scalar_tensor_tensor(out=term, in0=g, scalar=1.0, in1=pair(ps[:, bank, :]),
                                                     op0=ALU.add, op1=ALU.mult)
                        if i == 1:
                            ins.then_inc(emptied["dve"], 1)
                            dve.wait_ge(emptied["dve"], EVACUATED[w][1])
                        else:
                            link(ins)
                        ins = V.tensor_tensor(mg[:, c:c + 2, :], mg[:, c:c + 2, :], term, ALU.add)
                        if r == nbr - 1:
                            ins.then_inc(sem("merged"), 1)
                            dve.wait_ge(sem("merged"), 4 * k + 2 * half + i + 1)
                        else:
                            link(ins)

            def low_merged(k, half):
                for i in range(2):
                    dve.wait_ge(sem("mghi_ready"), 4 * k + 2 * half + i + 1)
                    c = slice(4 * half + 2 * i, 4 * half + 2 * i + 2)
                    V.scalar_tensor_tensor(out=hlo[:, c, :], in0=mg[:, c, :], scalar=0.5, in1=f32(hhi[:, c, :]),
                                           op0=ALU.mult, op1=ALU.subtract).then_inc(sem("mglo_ready"), 1)

            def merge_all(b0, nbr, o0, k):
                for u in range(1, 2 * nbr):
                    merge(b0 + u - 1, u - 1, nbr, k)
                    if u % nbr == 0:
                        low_merged(k, 0)
                    if u < 2 * nbr - 1:
                        split_low(b0 + u + AHEAD)
                merge(b0 + 2 * nbr - 1, 2 * nbr - 1, nbr, k, by_bank=True)
                low_merged(k, 1)
                split_low(o0 + AHEAD - 1)
                split_low(o0 + AHEAD)

            merge_all(BR1, 2, WO1, 0)
            for u in range(4):
                w = WO1 + u
                dve.wait_ge(gemm_done, w + 1)
                bank = ps[:, unit_banks(w)[0], :]
                for i in range(2):
                    c = 2 * u + i
                    ins = V.scalar_tensor_tensor(out=x[:, c, :], in0=bank[:, S * i:S * i + S],
                                                 scalar=mod[:, 16 + c:17 + c], in1=x[:, c, :], op0=ALU.mult, op1=ALU.add)
                ins.then_inc(sem("x1_ready"), 1)
                if u == 0:
                    mods(4)
                    gains(gs2, 4, "norm2_g")
                if u >= 1:
                    sum_squares("two", 2, mg, u - 1)
                if u in (1, 2):
                    split_low(w + AHEAD)
            sum_squares("two", 2, mg, 3)
            norm_wide(1, "two", x, lambda c: gs2[:, c:c + 1], shift=mod[:, 24:32])
            split_low(WO1 + 3 + AHEAD)

            def ffn(f):
                w0 = FF[f]
                table = col(("conv_w", "ffn_conv_w_2")[f], n=88).rearrange("p (a b) -> p a b", b=22)
                conv_step = sem(f"conv_step{f}")
                V.memset(fa[:, :, :, 0:2].rearrange("p a b c -> p (a b) c"), 0.0).then_inc(sem("pads_ready"), 1)
                dve.wait_ge(sem("pads_ready"), f + 1)

                def convolve(j, b, it=0):
                    n = 5 * (it * STEPS + j)
                    if j >= 2:
                        dve.wait_ge(sem(f"act_done{f}"), it * STEPS + (j - 1))
                    V.tensor_copy(cw[:, b, :, :], table[:, :, bass.ds(it * 2 * STEPS + 2 * j, 2)]).then_inc(conv_step, 1)
                    dve.wait_ge(sem(f"a_ready{f}"), it * STEPS + (j + 1))
                    dve.wait_ge(conv_step, n + 1)
                    for tap in range(3):
                        for c in range(2):
                            dst = fc[:, b, S * c:S * c + S]
                            src = fa[:, b, c, tap:tap + S]
                            if tap == 0:
                                V.tensor_scalar(dst, src, cw[:, b, 0, c:c + 1], cw[:, b, 3, c:c + 1],
                                                ALU.mult, ALU.add).then_inc(conv_step, 1)
                                continue
                            dve.wait_ge(conv_step, n + 2 * tap + c)
                            ins = V.scalar_tensor_tensor(out=dst, in0=src, scalar=cw[:, b, tap, c:c + 1], in1=dst,
                                                         op0=ALU.mult, op1=ALU.add)
                            if tap == 1:
                                ins.then_inc(conv_step, 1)
                    ins.then_inc(sem(f"conv_done{f}"), 1)

                def gate_it(c, j, b, it=0):
                    dve.wait_ge(sem(f"act_done{f}"), it * STEPS + (j + 1))
                    dve.wait_ge(gemm_done, it * BODY + (w0 + c + 1))
                    V.tensor_tensor(fp[:, b, :], fg[:, b, :], ps[:, (1, 3)[b], :], ALU.mult)\
                        .then_inc(sem(f"glu_done{f}"), 1)
                    dve.wait_ge(sem(f"fhi_ready{f}"), it * STEPS + (j + 1))
                    V.tensor_tensor(flo[:, b, :], fp[:, b, :], f32(fhi[:, b, :]), ALU.subtract)\
                        .then_inc(sem(f"flo_ready{f}"), 1)

                def slot(c, kind, j, it=0):
                    if f == 0 and c == 3 * FJ - 3:
                        mods(5)
                    if f == 0 and c == 3 * FJ - 1:
                        r = spread("mem")
                        norm_h(2, lambda c: V.scalar_tensor_tensor(out=mg[:, c, :], in0=mem[:, c, :],
                                                                   scalar=col("g_mem_2", c), in1=r,
                                                                   op0=ALU.mult, op1=ALU.mult), tmp=mg)
                    split_low(w0 + c + AHEAD, it)
                    if kind == "g":
                        convolve(j, j % 2, it)
                    if kind == "d" and j + 1 < FJ or kind == "a" and c == 2:
                        k = j + 1 if kind == "d" else 0
                        gate_it(3 * k if k else 1, k, k % 2, it)

                for c, (kind, j) in enumerate(FFN_HEAD):
                    slot(c, kind, j)
                with dve.Fori(0, FFN_LOOPS) as it:
                    for c, (kind, j) in enumerate(FFN_BODY):
                        slot(len(FFN_HEAD) + c, kind, j, it)
                for c, (kind, j) in enumerate(FFN_TAIL):
                    slot(3 * FJ - len(FFN_TAIL) + c, kind, j)

            def w_down_summed(f, u):
                if u < 3:
                    dve.wait_ge(sem(f"bank_summed{f}"), u + 1)
                else:
                    dve.wait_ge(gemm_done, FF[f] + 3 * FJ)

            ffn(0)
            for u in range(4):
                w_down_summed(0, u)
                for i in range(2):
                    c = 2 * u + i
                    ins = V.scalar_tensor_tensor(out=x[:, c, :], in0=ps[:, 4 + u, S * i:S * i + S],
                                                 scalar=mod[:, 40 + c:41 + c], in1=x[:, c, :], op0=ALU.mult, op1=ALU.add)
                ins.then_inc(sem("x2_ready"), 1)
            for i in range(4):
                sum_squares("final", 3, mg, i)
            split_low(MEMKV + 3)
            invert("final")
            r = spread("final")
            for c in range(KT):
                ins = V.scalar_tensor_tensor(out=x[:, c, :], in0=x[:, c, :], scalar=col("final_g", c), in1=r,
                                             op0=ALU.mult, op1=ALU.mult)
                if c % 2:
                    ins.then_inc(sem("x3_ready"), 1)
            for i in range(4):
                sum_squares("mix", 4, mg, i)
            split_low(MEMKV + 4)
            norm_wide(3, "mix", x, lambda c: col("g_mix_2", c))
            split_low(MEMKV + 5)
            split_low(MEMKV + 6)

            for s in range(27):
                if s not in ITEMS2:
                    split_low(WIN2 + s + AHEAD)
                if s == 2:
                    invert("memk")
                if s == 3:
                    for i in range(2):
                        r = spread("memk", i)
                        V.scalar_tensor_tensor(out=kmem[:, 2 * i:2 * i + 2, :], in0=kmem[:, 2 * i:2 * i + 2, :],
                                               scalar=gmem, in1=r,
                                               op0=ALU.mult, op1=ALU.mult).then_inc(sem("kmem_ready"), 1)
                if s == 5:
                    invert("qk")
                if s == 6:
                    for i in range(2):
                        r = spread("qk", i)
                        c = slice(K2 + 2 * i, K2 + 2 * i + 2)
                        V.scalar_tensor_tensor(out=proj[:, c, :], in0=proj[:, c, :], scalar=gmoba, in1=r,
                                               op0=ALU.mult, op1=ALU.mult).then_inc(sem("qk_ready"), 1)
                    link(V.memset(conv_u[:, :, 0:2], 0.0))
                if s == 9:
                    invert("qm")
                w, k = WIN2 + s - 1, s - 1
                kind = IN2[k][0] if s else ""
                if kind in ("cx", "cb"):
                    dve.wait_ge(gemm_done, w + 1)
                    bank = pair(ps[:, unit_banks(w)[0], :])
                if kind == "cx":
                    c = slice(2 * (k - 10), 2 * (k - 10) + 2)
                    dve.wait_ge(emptied["act"], EVACUATED[WIN2 + 8 + (k - 10)][1])
                    V.tensor_tensor(conv_u[:, c, 2:S + 2], conv_c[:, c, :], bank, ALU.mult).then_inc(emptied["dve"], 1)
                if kind == "cb":
                    h = k - 12
                    dve.wait_ge(emptied["dve"], EVACUATED[w - 2][1])
                    for tap in range(3):
                        for i in range(2):
                            c = 2 * h + i
                            src, wt = conv_u[:, c, tap:tap + S], col("conv_w_2", 4 * tap + c)
                            if tap == 0:
                                ins = V.tensor_scalar(conv_t[:, c, :], src, wt, col("conv_b_2", c), ALU.mult, ALU.add)
                            else:
                                ins = V.scalar_tensor_tensor(out=conv_t[:, c, :], in0=src, scalar=wt, in1=conv_t[:, c, :],
                                                             op0=ALU.mult, op1=ALU.add)
                        link(ins)
                    c = slice(2 * h, 2 * h + 2)
                    V.tensor_tensor(conv_t[:, c, :], conv_t[:, c, :], bank, ALU.mult).then_inc(emptied["dve"], 1)
                if s - 2 in ITEMS2:
                    low_pv(ITEMS2[s - 2])
                attention(ITEMS2, s, WIN2 + s + AHEAD)
                if s in (14, 15):
                    i = s - 14
                    dve.wait_ge(sem("ychi_ready"), i + 1)
                    c = slice(2 * i, 2 * i + 2)
                    V.tensor_tensor(ylo[:, c, :], conv_t[:, c, :], f32(yhi[:, c, :]), ALU.subtract)\
                        .then_inc(sem("yclo_ready"), 1)
            merge_all(BR2, 3, WO2, 1)
            for u in range(4):
                w = WO2 + u
                dve.wait_ge(gemm_done, w + 1)
                V.tensor_tensor(x[:, 2 * u:2 * u + 2, :], x[:, 2 * u:2 * u + 2, :], pair(ps[:, unit_banks(w)[0], :]),
                                ALU.add).then_inc(sem("x5_ready"), 1)
                if u >= 1:
                    sum_squares("ffn2", 5, mg, u - 1)
                if u in (1, 2):
                    split_low(w + AHEAD)
            sum_squares("ffn2", 5, mg, 3)
            norm_wide(4, "ffn2", x, lambda c: col("g_ffn_2", c))
            split_low(WO2 + 3 + AHEAD)
            ffn(1)
            for u in range(4):
                w_down_summed(1, u)
                V.tensor_tensor(x[:, 2 * u:2 * u + 2, :], x[:, 2 * u:2 * u + 2, :], pair(ps[:, 4 + u, :]),
                                ALU.add).then_inc(sem("x6_ready"), 1)

        @block.tensor
        def _(pe):
            mm = nc.tensor.matmul

            def three(out_, whi_, wlo_, ahi, alo, start, stop, weights_move=False, **kw):
                terms = [(whi_, ahi), (whi_, alo), (wlo_, ahi)]
                for i, (w_, a_) in enumerate(terms):
                    l, r = (a_, w_) if weights_move else (w_, a_)
                    ins = mm(out_, l, r, start=start and i == 0, stop=stop and i == 2, **kw)
                return ins

            def begin(w):
                pe.wait_ge(raw_done, RAW_OF[("w", w)] + 1)
                for v in sorted(BANK_BEFORE.get(w, ())):
                    e, n = EVACUATED[v]
                    pe.wait_ge(emptied[e], n)

            def wt(ring, w, kt, c, n, width):
                return ring[:, w % SPLIT, kt * width + c:kt * width + c + n]

            def channels(w, i, width, ah, al, kts, last=False, bank=None, signal=None):
                b = unit_banks(w)[i // 2] if bank is None else bank
                for kt in range(kts):
                    ins = three(ps[:, b, S * (i % 2):S * (i % 2) + S], wt(whi, w, kt, P * i, P, width),
                                wt(wlo, w, kt, P * i, P, width), ah[:, kt, :], al[:, kt, :], kt == 0, kt == kts - 1)
                if last:
                    ins.then_inc(gemm_done, 1)
                if signal is not None:
                    ins.then_inc(signal, 1)

            def positions(w, tt, c, n, out_, last=False):
                for kt in range(KT):
                    ins = three(out_, wt(whi, w, kt, c, n, 256), wt(wlo, w, kt, c, n, 256),
                                hhi[:, kt, P * tt:P * tt + P], hlo[:, kt, P * tt:P * tt + P], kt == 0, kt == KT - 1,
                                weights_move=True)
                if last:
                    ins.then_inc(gemm_done, 1)

            def both_channels(w, ready, bank=None):
                b = unit_banks(w)[0] if bank is None else bank
                for kt in range(KT):
                    pe.wait_ge(ready[0], ready[1] + (kt // ready[2]) + 1)
                    for i in range(2):
                        for n, (w_, a_) in enumerate(((whi, hhi), (whi, hlo), (wlo, hhi))):
                            ins = mm(ps[:, b, S * i:S * i + S], wt(w_, w, kt, P * i, P, 256), a_[:, kt, :],
                                     start=kt == 0 and i == 0 and n == 0, stop=kt == KT - 1 and n == 2,
                                     skip_group_check=True)
                ins.then_inc(gemm_done, 1)

            def statistics(name, src, ready=None):
                tiles, heads, bank, _ = NORMS[name]
                mean = mean_64[:, 0:P:64] if heads == 2 else (mean_128 if heads else mean_d)[:, 0:1]
                if name in SUMMED:
                    pe.wait_ge(sem(f"{name}_summed"), 1)
                    for tt in range(NT):
                        ins = mm(ps[:, bank, tt:tt + 1], src[:, 0, P * tt:P * tt + P], mean, start=True, stop=True)
                    ins.then_inc(sem(f"{name}_mean"), 1)
                    return
                for c in range(tiles):
                    if c % 2 == 0:
                        pe.wait_ge(ready[0], ready[1] + c // 2 + 1)
                    for tt in range(NT):
                        if heads:
                            at = (c * NT + tt) * heads
                            ins = mm(ps[:, bank, at:at + heads], src[:, c, P * tt:P * tt + P], mean,
                                     start=True, stop=True)
                        else:
                            ins = mm(ps[:, bank, tt:tt + 1], src[:, c, P * tt:P * tt + P], mean,
                                     start=c == 0 and tt == 0, stop=c == KT - 1, skip_group_check=True)
                ins.then_inc(sem(f"{name}_mean"), 1)

            def broadcast(name, first=0):
                tiles, heads, _, bank = NORMS[name]
                at = STAT[name][0]
                pe.wait_ge(sem(f"{name}_rstd"), 1)
                for c in range(first, tiles if heads else 1):
                    for tt in range(NT):
                        b, to = (bank + (c - first) // 2, S * (c % 2)) if heads else (bank, BCAST)
                        rows = P // (heads or 1)
                        for h in range(heads or 1):
                            k = at + (c * NT + tt) * (heads or 1) + h
                            ins = mm(ps[rows * h:rows * h + rows, b, to + P * tt:to + P * tt + P],
                                     rstd[:, k:k + 1].to_broadcast([P, rows]), ident[:, :], start=True, stop=True)
                ins.then_inc(sem(f"{name}_spread"), 1)

            def mod_sums(m):
                pe.wait_ge(raw_done, RAW_OF[("ada", 4 * m + 3)] + 1)
                if m:
                    pe.wait_ge(sem("mods_ready"), m)
                if MOD_PV.get(m):
                    pe.wait_ge(sem("yhi_ready"), MOD_PV[m])
                    pe.wait_ge(sem("ylo_ready"), min(4, MOD_PV[m]))
                bank, at = MOD_AT[m]
                for c in range(KT):
                    ins = mm(ps[:, bank, at + c:at + c + 1], ada[m % 2][:, P * c:P * c + P],
                             one, start=True, stop=True)
                ins.then_inc(sem("mod_done"), 1)

            pe.wait_ge(sem("const_made"), MADE_MATRICES)
            statistics("one", squares, (sem("sq_ready"), 0))
            broadcast("one")
            mod_sums(0)
            mod_sums(1)

            def score_maps(item):
                kind, i = item
                n = ITEM_NO[item]
                if n:
                    pe.wait_ge(sem("exp_done"), n)
                if kind == "diff" and i == 0:
                    pe.wait_ge(emptied["act"], EVACUATED[WIN1 + 6][1])
                if kind == "swa" and i == 0:
                    pe.wait_ge(emptied["act"], EVACUATED[WIN1 + 2][1])
                if kind == "moba" and i == 0:
                    pe.wait_ge(sem("qk_ready"), 2)
                if kind == "mem" and i == 0:
                    pe.wait_ge(emptied["act"], EVACUATED[WIN2 + 7][1])
                    pe.wait_ge(sem("kmem_ready"), 2)
                for m in range(2):
                    part = slice(64 * m, 64 * m + 64)
                    if kind == "swa":
                        q, k = proj[part, QA + i, :], proj[part, KA[0 if i // 2 == m else 1], :]
                    elif kind == "diff":
                        q, k = proj[part, QD + i, :], proj[part, KD + i, :]
                    elif kind == "moba":
                        q, k = proj[part, Q2 + i, :], proj[part, K2 + i, :]
                    else:
                        q, k = proj[:, QM + 2 * i + m, :], kmem[:, 2 * i + m, :]
                    first = 256 if kind == "mem" else 128
                    b = SCORE_BANK + m
                    mm(ps[:, b, 0:first], q[:, 0:P], k[:, 0:first], start=True, stop=True)
                    ins = mm(ps[:, b, first:first + 256], q[:, P:2 * P], k[:, 0:256], start=True, stop=True)
                ins.then_inc(sem("scores_done"), 1)

            def turn_probs(item):
                kind, i = item
                n = ITEM_NO[item]
                pe.wait_ge(sem("probs_ready"), n + 1)
                if n == 0:
                    pe.wait_ge(sem("mods_ready"), 3)
                if n:
                    pe.wait_ge(sem("pt0_ready"), n)
                    pe.wait_ge(sem("pt1_ready"), two_map_items(n - 1) if n - 1 < 4 or n - 1 >= 8 else 4)
                for m in range(1 if kind == "diff" else 2):
                    b = PT_BANKS[m]
                    if kind == "mem":
                        blocks = [(1, 0), (257, 128), (129, 256), (385, 384)]
                    else:
                        blocks = [(1, 0), (129, 128), (257, 256)]
                    for src, dst in blocks:
                        ins = nc.tensor.transpose(ps[:, b, dst:dst + P], probs[:, m, src:src + P], ident[:, :])
                ins.then_inc(sem("pt_done"), 1)

            def values(item):
                kind, i = item
                n = ITEM_NO[item]
                pe.wait_ge(sem("pt0_ready"), n + 1)
                if kind != "diff":
                    pe.wait_ge(sem("pt1_ready"), two_map_items(n))
                if n:
                    pe.wait_ge(sem("yhi_ready"), n)
                    pe.wait_ge(sem("ylo_ready"), two_map_items(n - 1) if n - 1 < 4 or n - 1 >= 8 else 4)
                if kind == "diff" and i == 0:
                    pe.wait_ge(emptied["act"], EVACUATED[WIN1 + 8][1])
                if kind == "moba" and i == 0:
                    pe.wait_ge(emptied["act"], EVACUATED[WIN2 + 5][1])
                if kind in ("swa", "diff"):
                    pe.wait_ge(sem("mods_ready"), mods_before[0])
                for m in range(1 if kind == "diff" else 2):
                    if kind == "swa":
                        o, v = ps[64 * m:64 * m + 64, PV_BANK, 0:S], vtok[:, :, 512 + 64 * (i // 2):576 + 64 * (i // 2)]
                    elif kind == "diff":
                        o, v = ps[:, PV_BANK, 0:S], vtok[:, :, P * i:P * i + P]
                    elif kind == "moba":
                        h = 2 * i + m
                        o, v = ps[64 * m:64 * m + 64, PV_BANK, 0:S], vtok[:, :, 64 * h:64 * h + 64]
                    else:
                        h = 2 * i + m
                        o, v = ps[:, PV_BANK, S * m:S * m + S], vmem[:, :, P * h:P * h + P]
                    mm(o, v[:, 0, :], pt[:, m, 0:256], start=True, stop=False)
                    if kind == "mem":
                        ins = mm(o, v[:, 1, :], pt[:, m, 256:512], start=False, stop=True)
                    else:
                        ins = mm(o[:, P:2 * P], v[:, 1, :], pt[:, m, 256:384], start=False, stop=True)
                ins.then_inc(sem("pv_done"), 1)

            def slot(w, items, s, halves):
                begin(w)
                halves(0)
                if s - 1 in items:
                    turn_probs(items[s - 1])
                if s in items:
                    score_maps(items[s])
                halves(1)
                if s - 1 in items:
                    values(items[s - 1])

            mods_before = [2]
            for s in range(17):
                w = WIN1 + s
                kind = IN1[s]
                if s in MOD_SLOTS:
                    mod_sums(MOD_SLOTS[s])
                    mods_before[0] = MOD_SLOTS[s] + 1
                b = unit_banks(w)[0]

                def halves(i):
                    if kind == "vd":
                        positions(w, i, 0, 256, ps[:, b, 256 * i:256 * i + 256], last=i == 1)
                    elif kind == "kava" and i == 0:
                        channels(w, 0, 256, hhi, hlo, KT)
                    elif kind == "kava":
                        for tt in range(2):
                            positions(w, tt, P, P, ps[:, b, S + P * tt:S + P * tt + P], last=tt == 1)
                    else:
                        channels(w, i, 256, hhi, hlo, KT, last=i == 1)

                if s == 0:
                    begin(w)
                    both_channels(w, (sem("hlo_ready"), 0, 1))
                    continue
                slot(w, ITEMS1, s, halves)
                if s == 13:
                    statistics("mem", tmp)
                if s == 13:
                    statistics("diff", proj[:, KD:KD + 4, :], (sem("yhi_ready"), 6))
                if s == 14:
                    broadcast("diff")

            def branch(w, tile0, waits, last=False):
                begin(w)
                for s_, n in waits:
                    pe.wait_ge(s_, n)
                for i in range(4):
                    channels(w, i, 512, yhi[:, tile0:tile0 + 4, :], ylo[:, tile0:tile0 + 4, :], 4, last=i == 3,
                             signal=sem("first_bank_done") if last and i == 1 else None)

            def project_merged(o0, k, name):
                for u in range(4):
                    if k == 0 and u == 3:
                        pe.wait_ge(sem("mods_ready"), 5)
                    begin(o0 + u)
                    if u == 0:
                        both_channels(o0, (sem("mglo_ready"), 4 * k, 2))
                        if k == 0:
                            mod_sums(4)
                        continue
                    for i in range(2):
                        channels(o0 + u, i, 256, hhi, hlo, KT, last=i == 1)
                statistics(name, mg)
                broadcast(name)

            for u in range(4):
                if u == 2:
                    pe.wait_ge(sem("mods_ready"), 4)
                branch(BR1 + u, 4 * (u % 2), [(sem("ylo_ready"), 4)] if u == 0 else [(sem("ydlo_ready"), 2)], last=u == 3)
            project_merged(WO1, 0, "two")

            def ffn(f):
                w0 = FF[f]

                def up(c, kind, j, it=0):
                    w = w0 + c
                    pe.wait_ge(raw_done, it * BODY + (RAW_OF[("w", w)] + 1))
                    if j >= 2:
                        pe.wait_ge(sem(f"a_ready{f}" if kind == "a" else f"glu_done{f}"), it * STEPS + (j - 1))
                    bank = 2 * (j % 2) + (kind == "g")
                    if c == 0:
                        both_channels(w, (sem("hlo_ready"), KT * (1, 4)[f], 1), bank)
                        return
                    if c == 3 * FJ - 3 and f == 0:
                        pe.wait_ge(sem("glu_done0"), FJ - 1)
                        mod_sums(5)
                    for i in range(2):
                        channels(w, i, 256, hhi, hlo, KT, last=i == 1, bank=bank)

                def down(c, j, it=0):
                    w = w0 + c
                    first = j == 0 and isinstance(it, int)
                    pe.wait_ge(raw_done, it * BODY + (RAW_OF[("w", w)] + 1))
                    pe.wait_ge(sem(f"flo_ready{f}"), it * STEPS + (j + 1))
                    for i in range(KT):
                        for kt in range(2):
                            ins = three(ps[:, 4 + i // 2, S * (i % 2):S * (i % 2) + S], wt(whi, w, kt, P * i, P, D),
                                        wt(wlo, w, kt, P * i, P, D), fhi[:, j % 2, S * kt:S * kt + S],
                                        flo[:, j % 2, S * kt:S * kt + S], first and i % 2 == 0 and kt == 0,
                                        j == FJ - 1 and kt == 1, skip_group_check=True)
                        if c == 3 * FJ - 1 and i in (1, 3, 5):
                            ins.then_inc(sem(f"bank_summed{f}"), 1)
                    ins.then_inc(gemm_done, 1)

                def slot_(c, kind, j, it=0):
                    if kind == "d":
                        if f == 0 and c == 3 * FJ - 2:
                            pe.wait_ge(sem("mods_ready"), 6)
                            broadcast("mem")
                        down(c, j, it)
                    else:
                        up(c, kind, j, it)

                for c, (kind, j) in enumerate(FFN_HEAD):
                    slot_(c, kind, j)
                with pe.Fori(0, FFN_LOOPS) as it:
                    for c, (kind, j) in enumerate(FFN_BODY):
                        slot_(len(FFN_HEAD) + c, kind, j, it)
                for c, (kind, j) in enumerate(FFN_TAIL):
                    slot_(3 * FJ - len(FFN_TAIL) + c, kind, j)

            ffn(0)
            def memory_values(u, tt):
                positions(MEMKV + 2 + u, tt, 0, 256, ps[:, unit_banks(MEMKV + 2 + u)[0], 256 * tt:256 * tt + 256],
                          last=tt == 1)

            begin(MEMKV)
            both_channels(MEMKV, (sem("hlo_ready"), KT * 2, 1))
            begin(MEMKV + 1)
            for i in range(2):
                channels(MEMKV + 1, i, 256, hhi, hlo, KT, last=i == 1)
            statistics("final", mg)
            begin(MEMKV + 2)
            memory_values(0, 0)
            broadcast("final")
            memory_values(0, 1)
            begin(MEMKV + 3)
            for tt in range(NT):
                memory_values(1, tt)
            statistics("mix", mg)
            broadcast("mix")

            for s in range(26):
                w = WIN2 + s
                kind = IN2[s][0]
                b = unit_banks(w)[0]

                def halves(i):
                    if kind == "v":
                        positions(w, i, 0, 256, ps[:, b, 256 * i:256 * i + 256], last=i == 1)
                    else:
                        channels(w, i, 256, hhi, hlo, KT, last=i == 1)

                if s == 0:
                    begin(w)
                    both_channels(w, (sem("hlo_ready"), KT * 3, 1))
                    continue
                slot(w, ITEMS2, s, halves)
                if s == 1:
                    statistics("memk", squares, (sem("memk_sq"), 0))
                if s == 2:
                    broadcast("memk")
                if s == 4:
                    pe.wait_ge(sem("kmem_ready"), 2)
                    statistics("qk", tmp, (sem("qk_sq"), 0))
                if s == 5:
                    broadcast("qk", first=4)
                if s == 8:
                    statistics("qm", conv_t, (sem("qm_sq"), 0))
            for u in range(6):
                r = u % 3
                waits = [[(sem("yclo_ready"), 2)], [(sem("ylo_ready"), 8)], [(sem("ylo_ready"), 10)]][r]
                branch(BR2 + u, 4 * r, waits, last=u == 5)
            project_merged(WO2, 1, "ffn2")
            ffn(1)


def kernel(**inputs):
    import concourse.bacc as bacc
    from concourse.bass_utils import run_bass_kernel_spmd

    a = {name: np.asarray(v) for name, v in inputs.items()}

    def column_units(w, order=None):
        n = w.shape[1] // 256
        u = w.reshape(KT, P, n, 256).transpose(2, 1, 0, 3).reshape(n, P, UNIT)
        return u if order is None else u[order]

    def branch_units(ws):
        return np.stack([w.reshape(4, P, 2, 512).transpose(2, 1, 0, 3).reshape(2, P, UNIT) for w in ws], axis=1)\
            .reshape(2 * len(ws), P, UNIT)

    def row_units(w):
        return w.reshape(FJ, 2, P, D).transpose(0, 2, 1, 3).reshape(FJ, P, UNIT)

    def channel_major(v):
        return v[0].T.reshape(KT, P, S).transpose(1, 0, 2).reshape(P, KT * S)

    doubled = {n: np.concatenate([a[n], a[n]]) for n in ("moba_q_gain_2", "moba_k_gain_2")}
    arrays = {
        "w_mem_kv_2": column_units(a["w_mem_kv_2"]),
        "w_ada": a["w_ada"][0].reshape(4, 2, P, 6, D).transpose(3, 0, 2, 1, 4).reshape(24, P, UNIT),
        "w_in": column_units(a["w_in"][0]),
        "branches": branch_units([a["w_branch_swa"][0], a["w_branch_diff"][0]]),
        "w_out": column_units(a["w_out"][0]),
        "w_up": column_units(a["w_up"][0]),
        "w_down": row_units(a["w_down"][0]),
        "w_in_2": column_units(a["w_in_2"], [c // 256 for _, c in IN2]),
        "branches_2": branch_units([a["w_br_conv_2"], a["w_br_moba_2"], a["w_br_mem_2"]]),
        "w_o_2": column_units(a["w_o_2"]),
        "w_up_2": column_units(a["w_up_2"]),
        "w_down_2": row_units(a["w_down_2"]),
        "vectors": np.concatenate([doubled.get(n, a[n]).reshape(-1, P) for n, _ in VECTORS]).T,
        "x": channel_major(a["x"]),
        "mem_2": channel_major(a["mem_2"]),
        "swa_sinks": a["swa_sinks"],
        "diff_lambda": a["diff_lambda"],
    }
    nc = bacc.Bacc("TRN2", target_bir_lowering=False, num_devices=1, dynamic_dma_scratch_size=2048)
    feeds, tensors = {}, {}
    for name, v in arrays.items():
        feeds[f"in_{name}"] = np.ascontiguousarray(v)
        tensors[name] = nc.dram_tensor(f"in_{name}", v.shape, mybir.dt.from_np(v.dtype), kind="ExternalInput").ap()
    out = nc.dram_tensor("out", (4, P, 2 * S), F32, kind="ExternalOutput").ap()
    two_blocks(nc, tensors, out)
    r = run_bass_kernel_spmd(nc, [feeds], core_ids=[0])
    return r.results[0]["out"].reshape(4, P, 2, S).transpose(3, 0, 2, 1).reshape(1, S, D)
```
